# Optimizing a Trainium2 kernel written in Bass

```python
import jax
import jax.numpy as jnp
from jax import lax
import numpy as np
import math
import jax, jax.numpy as jnp

D_MODEL = 1024
BATCH = 1
SEQ = 512
DEPTH = 2

GRID_W = 64
CTX_LEN = 256
N_MIXERS = 2
N_LAYERS_A = (DEPTH + N_MIXERS - 1) // N_MIXERS
N_LAYERS_B = DEPTH // N_MIXERS
N_MOD = 6
NORM_EPS = 1e-6
CHUNK = 128
GMLP_WIDTH = 2 * D_MODEL
GMLP_GROUP_CH = 128
GMLP_GROUPS = GMLP_WIDTH // GMLP_GROUP_CH
LN_EPS = 1e-5
RWKV_HEAD = 64
RWKV_HEADS = D_MODEL // RWKV_HEAD
DECAY_LORA = 64
AAA_LORA = 64
GATE_LORA = 160
GN_EPS = 64e-5
N_DIR = 2
N_GROUPS = 4
EXPERTS_PER_GROUP = 8
N_EXPERTS = N_GROUPS * EXPERTS_PER_GROUP
EXPERT_HIDDEN = 512
TOP_K = 2
MOE_BLOCK = 128


def rmsnorm(x, g):
    xf = x.astype(jnp.float32)
    y = xf * lax.rsqrt(jnp.mean(xf * xf, axis=-1, keepdims=True) + NORM_EPS)
    return y.astype(x.dtype) * g

def layernorm(x, g, b, eps):
    xf = x.astype(jnp.float32)
    mu = jnp.mean(xf, axis=-1, keepdims=True)
    var = jnp.mean(jnp.square(xf - mu), axis=-1, keepdims=True)
    return ((xf - mu) * lax.rsqrt(var + eps)).astype(x.dtype) * g + b

def gmlp_mixer(h, w_in, b_in, ln_g, ln_b, w_s, b_s, w_out, b_out):
    bsz, n, _ = h.shape
    z = jax.nn.gelu(h @ w_in + b_in, approximate=False)
    u, v = jnp.split(z, 2, axis=-1)
    v = layernorm(v, ln_g, ln_b, LN_EPS)
    v = v.reshape(bsz, n // CHUNK, CHUNK, GMLP_GROUPS, GMLP_GROUP_CH)
    v = jnp.einsum('gpq,bcqgd->bcpgd', w_s, v) + b_s.T[:, :, None]
    return (u * v.reshape(bsz, n, GMLP_WIDTH)) @ w_out + b_out

def qshift_grid(h, rows):
    bsz, n, d = h.shape
    q = d // 4
    g = h.reshape(bsz, rows, GRID_W, d)
    left = jnp.pad(g[:, :, :-1, :q], ((0, 0), (0, 0), (1, 0), (0, 0)))
    right = jnp.pad(g[:, :, 1:, q:2 * q], ((0, 0), (0, 0), (0, 1), (0, 0)))
    up = jnp.pad(g[:, :-1, :, 2 * q:3 * q], ((0, 0), (1, 0), (0, 0), (0, 0)))
    down = jnp.pad(g[:, 1:, :, 3 * q:], ((0, 0), (0, 1), (0, 0), (0, 0)))
    return jnp.concatenate([left, right, up, down], axis=-1).reshape(bsz, n, d)

def bishift_1d(h):
    half = h.shape[-1] // 2
    prev = jnp.pad(h[:, :-1, :half], ((0, 0), (1, 0), (0, 0)))
    nxt = jnp.pad(h[:, 1:, half:], ((0, 0), (0, 1), (0, 0)))
    return jnp.concatenate([prev, nxt], axis=-1)

def _heads(z):
    return z.reshape(*z.shape[:-1], RWKV_HEADS, RWKV_HEAD)

def _both_dirs(z):
    return jnp.stack([z, z[:, ::-1]])

def _rev_dir1(z):
    return jnp.stack([z[0], z[1][:, ::-1]])

def _scan_layout(z):
    return jnp.moveaxis(_heads(z), 2, 0).astype(jnp.float32)

def rwkv_prepare(h, h_shift, mu, wr, wk, wv, w0, w1, w2, a0, a1, a2, k_k, k_a):
    xx = h_shift - h
    xr, xw, xk, xv, xa = [h + xx * mu[j] for j in range(5)]
    r = xr @ wr
    k = xk @ wk
    v = xv @ wv
    lw = jnp.einsum('zbtr,zrd->zbtd', jnp.tanh(jnp.einsum('btd,zdr->zbtr', xw, w1)), w2)
    w_log = -jax.nn.softplus(-(w0[:, None, None, :] + lw).astype(jnp.float32)) - 0.5
    decay = jnp.exp(-jnp.exp(w_log))
    la = jnp.einsum('zbtr,zrd->zbtd', jnp.einsum('btd,zdr->zbtr', xa, a1), a2)
    a = jax.nn.sigmoid((a0[:, None, None, :] + la).astype(jnp.float32))
    kk = _heads(k * k_k).astype(jnp.float32)
    kk = (kk * lax.rsqrt(jnp.sum(kk * kk, axis=-1, keepdims=True) + 1e-12)).reshape(k.shape)
    k_mod = k[None] * (1 + (a - 1) * k_a)
    scan_in = (_scan_layout(_both_dirs(r)), _scan_layout(_rev_dir1(decay)), _scan_layout(_rev_dir1(k_mod)),
               _scan_layout(_both_dirs(v)), _scan_layout(_both_dirs(-kk)), _scan_layout(_rev_dir1(kk[None] * a)))
    return scan_in, r, k_mod, v, xx

def _wkv_step(S, inp):
    r_t, w_t, k_t, v_t, a_t, b_t = inp
    sa = jnp.einsum('zbhvk,zbhk->zbhv', S, a_t)
    S = S * w_t[..., None, :] + sa[..., :, None] * b_t[..., None, :] + v_t[..., :, None] * k_t[..., None, :]
    return S, jnp.einsum('zbhvk,zbhk->zbhv', S, r_t)

def wkv_bidir(state0, scan_in):
    state, ys = lax.scan(_wkv_step, state0, scan_in)
    ys = jnp.moveaxis(ys, 0, 2)
    return state, ys[0] + ys[1][:, ::-1]

def rwkv_out(y, h, xx, r, k_mod, v, mu, ln_g, ln_b, r_k, g1, g2, wo):
    bsz, n, d = r.shape
    y = layernorm(y, ln_g.reshape(RWKV_HEADS, RWKV_HEAD), ln_b.reshape(RWKV_HEADS, RWKV_HEAD), GN_EPS)
    bonus = jnp.einsum('bthk,zbthk->bth', _heads(r) * r_k, _heads(k_mod))
    y = y.astype(r.dtype) + bonus[..., None] * _heads(v)
    xg = h + xx * mu[5]
    gate = jax.nn.sigmoid(xg @ g1) @ g2
    return (y.reshape(bsz, n, d) * gate) @ wo

def rwkv_mixer(hc, hl, rows, need_ctx_out, mu, wr, wk, wv, wo, w0, w1, w2, a0, a1, a2, g1, g2,
               k_k, k_a, r_k, ln_g, ln_b):
    proj = (mu, wr, wk, wv, w0, w1, w2, a0, a1, a2, k_k, k_a)
    scan_c, r_c, km_c, v_c, xx_c = rwkv_prepare(hc, bishift_1d(hc), *proj)
    scan_l, r_l, km_l, v_l, xx_l = rwkv_prepare(hl, qshift_grid(hl, rows), *proj)
    state0 = jnp.zeros((N_DIR, hc.shape[0], RWKV_HEADS, RWKV_HEAD, RWKV_HEAD), jnp.float32)
    state_c, y_c = wkv_bidir(state0, scan_c)
    _, y_l = wkv_bidir(state_c, scan_l)
    outp = (mu, ln_g, ln_b, r_k, g1, g2, wo)
    out_l = rwkv_out(y_l, hl, xx_l, r_l, km_l, v_l, *outp)
    out_c = rwkv_out(y_c, hc, xx_c, r_c, km_c, v_c, *outp) if need_ctx_out else None
    return out_c, out_l

def hier_moe(h, w_grp, b_grp, w_exp, b_exp, w_gate, w_up, w_down):
    n_tok, d = h.shape
    hf = h.astype(jnp.float32)
    grp_logits = hf @ w_grp.astype(jnp.float32) + b_grp.astype(jnp.float32)
    grp_prob = jax.nn.softmax(grp_logits, axis=-1)
    grp = jnp.argmax(grp_logits, axis=-1)
    p_grp = jnp.take_along_axis(grp_prob, grp[:, None], axis=-1)
    exp_logits = (hf @ w_exp.astype(jnp.float32) + b_exp.astype(jnp.float32)).reshape(n_tok, N_GROUPS, EXPERTS_PER_GROUP)
    exp_logits = jnp.take_along_axis(exp_logits, grp[:, None, None], axis=1)[:, 0]
    top_logit, top_idx = lax.top_k(exp_logits, TOP_K)
    weights = (p_grp * jax.nn.softmax(top_logit, axis=-1)).astype(h.dtype)
    expert_id = (grp[:, None] * EXPERTS_PER_GROUP + top_idx).reshape(-1)
    n_assign = n_tok * TOP_K
    order = jnp.argsort(expert_id)
    sorted_e = expert_id[order]
    token_of = order // TOP_K
    counts = jnp.bincount(expert_id, length=N_EXPERTS)
    padded = ((counts + MOE_BLOCK - 1) // MOE_BLOCK) * MOE_BLOCK
    pad_end = jnp.cumsum(padded)
    pad_start = pad_end - padded
    raw_start = jnp.cumsum(counts) - counts
    dest = pad_start[sorted_e] + (jnp.arange(n_assign) - raw_start[sorted_e])
    n_blocks = (n_assign + MOE_BLOCK - 1) // MOE_BLOCK + N_EXPERTS
    cap = n_blocks * MOE_BLOCK
    buf = jnp.zeros((cap, d), h.dtype).at[dest].set(h[token_of])
    block_expert = jnp.minimum(jnp.searchsorted(pad_end, jnp.arange(n_blocks) * MOE_BLOCK, side='right'),
                               N_EXPERTS - 1)

    def expert_block(args):
        xb, e = args
        return (jax.nn.silu(xb @ w_gate[e]) * (xb @ w_up[e])) @ w_down[e]

    out = lax.map(expert_block, (buf.reshape(n_blocks, MOE_BLOCK, d), block_expert)).reshape(cap, d)
    y = jnp.zeros((n_assign, d), h.dtype).at[order].set(out[dest]).reshape(n_tok, TOP_K, d)
    return jnp.einsum('tk,tkd->td', weights, y)

def first_inputs(seed: int = 0) -> dict:
    key = jax.random.key(seed)
    keys = iter(jax.random.split(key, 48))
    f32 = jnp.float32

    def nrm(shape, scale):
        return scale * jax.random.normal(next(keys), shape, f32)

    def gain(shape):
        return 1.0 + nrm(shape, 0.1)

    def unif(shape, lo, hi):
        return jax.random.uniform(next(keys), shape, f32, lo, hi)

    D, W, F = D_MODEL, GMLP_WIDTH, EXPERT_HIDDEN
    NA, NB = N_LAYERS_A, N_LAYERS_B
    return {
        'x': nrm((BATCH, SEQ, D), 1.0),
        'c': nrm((BATCH, D), 1.0),
        'ctx': nrm((BATCH, CTX_LEN, D), 1.0),
        'c_ctx': nrm((D,), 1.0),
        'ada_w': nrm((DEPTH, D, N_MOD * D), 0.5 * D ** -0.5),
        'ada_b': nrm((DEPTH, N_MOD * D), 0.05),
        'norm1_g': gain((DEPTH, D)),
        'norm2_g': gain((DEPTH, D)),
        'final_g': gain((D,)),
        'ga_w_in': nrm((NA, D, 2 * W), D ** -0.5),
        'ga_b_in': nrm((NA, 2 * W), 0.02),
        'ga_ln_g': gain((NA, W)),
        'ga_ln_b': nrm((NA, W), 0.02),
        'ga_w_s': nrm((NA, GMLP_GROUPS, CHUNK, CHUNK), 0.5 * CHUNK ** -0.5),
        'ga_b_s': gain((NA, GMLP_GROUPS, CHUNK)),
        'ga_w_out': nrm((NA, W, D), W ** -0.5),
        'ga_b_out': nrm((NA, D), 0.02),
        'rw_mu': unif((NB, N_MOD, D), 0.0, 1.0),
        'rw_wr': nrm((NB, D, D), D ** -0.5),
        'rw_wk': nrm((NB, D, D), D ** -0.5),
        'rw_wv': nrm((NB, D, D), D ** -0.5),
        'rw_wo': nrm((NB, D, D), D ** -0.5),
        'rw_w0': unif((NB, N_DIR, D), -6.0, 0.0),
        'rw_w1': nrm((NB, N_DIR, D, DECAY_LORA), 0.5 * D ** -0.5),
        'rw_w2': nrm((NB, N_DIR, DECAY_LORA, D), 0.5 * DECAY_LORA ** -0.5),
        'rw_a0': nrm((NB, N_DIR, D), 0.5),
        'rw_a1': nrm((NB, N_DIR, D, AAA_LORA), 0.5 * D ** -0.5),
        'rw_a2': nrm((NB, N_DIR, AAA_LORA, D), 0.5 * AAA_LORA ** -0.5),
        'rw_g1': nrm((NB, D, GATE_LORA), D ** -0.5),
        'rw_g2': nrm((NB, GATE_LORA, D), GATE_LORA ** -0.5),
        'rw_k_k': 0.85 + nrm((NB, D), 0.05),
        'rw_k_a': gain((NB, D)),
        'rw_r_k': nrm((NB, RWKV_HEADS, RWKV_HEAD), 0.1),
        'rw_ln_g': gain((NB, D)),
        'rw_ln_b': nrm((NB, D), 0.02),
        'moe_w_grp': nrm((DEPTH, D, N_GROUPS), D ** -0.5),
        'moe_b_grp': nrm((DEPTH, N_GROUPS), 0.01),
        'moe_w_exp': nrm((DEPTH, D, N_EXPERTS), D ** -0.5),
        'moe_b_exp': nrm((DEPTH, N_EXPERTS), 0.01),
        'moe_w_gate': nrm((DEPTH, N_EXPERTS, D, F), D ** -0.5),
        'moe_w_up': nrm((DEPTH, N_EXPERTS, D, F), D ** -0.5),
        'moe_w_down': nrm((DEPTH, N_EXPERTS, F, D), F ** -0.5),
    }

def first_block(x, c, ctx, c_ctx, ada_w, ada_b, norm1_g, norm2_g, final_g,
              ga_w_in, ga_b_in, ga_ln_g, ga_ln_b, ga_w_s, ga_b_s, ga_w_out, ga_b_out,
              rw_mu, rw_wr, rw_wk, rw_wv, rw_wo, rw_w0, rw_w1, rw_w2, rw_a0, rw_a1, rw_a2,
              rw_g1, rw_g2, rw_k_k, rw_k_a, rw_r_k, rw_ln_g, rw_ln_b,
              moe_w_grp, moe_b_grp, moe_w_exp, moe_b_exp, moe_w_gate, moe_w_up, moe_w_down):
    bsz, n, d = x.shape
    rows = n // GRID_W
    xc = ctx
    silu_c = jax.nn.silu(c)
    silu_cc = jax.nn.silu(c_ctx)
    for i in range(DEPTH):
        last = i == DEPTH - 1
        j = i // N_MIXERS
        mod_l = silu_c @ ada_w[i] + ada_b[i]
        mod_c = silu_cc @ ada_w[i] + ada_b[i]
        sh1, sc1, gt1, sh2, sc2, gt2 = jnp.split(mod_l[:, None, :], N_MOD, axis=-1)
        csh1, csc1, cgt1, csh2, csc2, cgt2 = jnp.split(mod_c, N_MOD, axis=-1)
        hl = rmsnorm(x, norm1_g[i]) * (1 + sc1) + sh1
        hc = rmsnorm(xc, norm1_g[i]) * (1 + csc1) + csh1
        if i % N_MIXERS == 0:
            gp = (ga_w_in[j], ga_b_in[j], ga_ln_g[j], ga_ln_b[j], ga_w_s[j], ga_b_s[j], ga_w_out[j], ga_b_out[j])
            yl = gmlp_mixer(hl, *gp)
            yc = None if last else gmlp_mixer(hc, *gp)
        else:
            yc, yl = rwkv_mixer(hc, hl, rows, not last, rw_mu[j], rw_wr[j], rw_wk[j], rw_wv[j], rw_wo[j],
                                rw_w0[j], rw_w1[j], rw_w2[j], rw_a0[j], rw_a1[j], rw_a2[j], rw_g1[j], rw_g2[j],
                                rw_k_k[j], rw_k_a[j], rw_r_k[j], rw_ln_g[j], rw_ln_b[j])
        x = x + gt1 * yl
        hl2 = rmsnorm(x, norm2_g[i]) * (1 + sc2) + sh2
        mp = (moe_w_grp[i], moe_b_grp[i], moe_w_exp[i], moe_b_exp[i], moe_w_gate[i], moe_w_up[i], moe_w_down[i])
        if last:
            x = x + gt2 * hier_moe(hl2.reshape(-1, d), *mp).reshape(x.shape)
        else:
            xc = xc + cgt1 * yc
            hc2 = rmsnorm(xc, norm2_g[i]) * (1 + csc2) + csh2
            out = hier_moe(jnp.concatenate([hl2.reshape(-1, d), hc2.reshape(-1, d)], axis=0), *mp)
            x = x + gt2 * out[:bsz * n].reshape(x.shape)
            xc = xc + cgt2 * out[bsz * n:].reshape(xc.shape)
    return rmsnorm(x, final_g)


HEAD_DIM = 64
BLOCK = 128
A_HEADS = 8
A_KV_HEADS = 2
A_WINDOW = 128
B_HEADS = 8
B_CONFIGS = ((128, 1), (512, 4), (2048, 16))
NUM_BUCKETS = 32
MAX_DISTANCE = 2048
C_HEADS = 16
C_Q_RANK = 256
C_KV_RANK = 128
C_NOPE = 64
C_ROPE = 32
C_V = 64
ROPE_THETA = 10000.0
EPS = 1e-6

A_WIDTH = A_HEADS * HEAD_DIM
A_KV_WIDTH = A_KV_HEADS * HEAD_DIM
B_WIDTH = B_HEADS * HEAD_DIM
AB_WIDTH = A_WIDTH + B_WIDTH
AB_IN = A_WIDTH + 2 * A_KV_WIDTH + 3 * B_WIDTH + AB_WIDTH
C_WIDTH = C_HEADS * C_V
C_IN = C_Q_RANK + C_KV_RANK + C_ROPE + C_WIDTH
N_AB = (DEPTH + 1) // 2
N_C = DEPTH // 2


def rmsnorm_2(x, w):
    xf = x.astype(jnp.float32)
    y = xf * lax.rsqrt(jnp.mean(xf * xf, axis=-1, keepdims=True) + EPS)
    return (y * w.astype(jnp.float32)).astype(x.dtype)

def t5_bucket(dist):
    max_exact = NUM_BUCKETS // 2
    d = jnp.maximum(dist, 1).astype(jnp.float32)
    large = max_exact + (jnp.log(d / max_exact) / math.log(MAX_DISTANCE / max_exact)
                         * (NUM_BUCKETS - max_exact)).astype(jnp.int32)
    large = jnp.minimum(large, NUM_BUCKETS - 1)
    return jnp.where(dist < max_exact, dist, large)

def band_bias(rel_bias_h, dilation, window):
    i = jnp.arange(BLOCK)[:, None]
    j = jnp.arange(2 * BLOCK)[None, :]
    dist = i + BLOCK - j
    in_band = (dist >= 0) & (dist <= window)
    bucket = t5_bucket(jnp.maximum(dist, 0) * dilation)
    bias = jnp.transpose(rel_bias_h[bucket].astype(jnp.float32), (2, 0, 1))
    return bias, in_band

def banded_attention(q, k, v, bias, in_band, sink=None):
    n, length, hq, dh = q.shape
    hkv = k.shape[2]
    g = hq // hkv
    nb = -(-length // BLOCK)
    padw = ((0, 0), (0, nb * BLOCK - length), (0, 0), (0, 0))
    qb = jnp.pad(q, padw).reshape(n, nb, BLOCK, hkv, g, dh)
    kb = jnp.pad(k, padw).reshape(n, nb, BLOCK, hkv, dh)
    vb = jnp.pad(v, padw).reshape(n, nb, BLOCK, hkv, dh)

    def with_prev(t):
        prev = jnp.pad(t, ((0, 0), (1, 0), (0, 0), (0, 0), (0, 0)))[:, :-1]
        return jnp.concatenate([prev, t], axis=2)

    kk, vv = with_prev(kb), with_prev(vb)
    s = jnp.einsum('nbqhgd,nbkhd->nbhgqk', qb, kk).astype(jnp.float32) * (dh ** -0.5)
    s = s + bias.reshape(hkv, g, BLOCK, 2 * BLOCK)
    kpos = (jnp.arange(nb)[:, None] - 1) * BLOCK + jnp.arange(2 * BLOCK)[None, :]
    mask = in_band[None] & (kpos >= 0)[:, None, :]
    s = jnp.where(mask[None, :, None, None], s, -jnp.inf)
    m = jnp.max(s, axis=-1, keepdims=True)
    if sink is not None:
        sk = sink.astype(jnp.float32).reshape(1, 1, hkv, g, 1, 1)
        m = jnp.maximum(m, sk)
    p = jnp.exp(s - m)
    denom = jnp.sum(p, axis=-1, keepdims=True)
    if sink is not None:
        denom = denom + jnp.exp(sk - m)
    o = jnp.einsum('nbhgqk,nbkhd->nbqhgd', (p / denom).astype(v.dtype), vv)
    o = o.reshape(n, nb * BLOCK, hq, dh)[:, :length]
    lse = (m + jnp.log(denom))[..., 0]
    lse = jnp.transpose(lse, (0, 1, 4, 2, 3)).reshape(n, nb * BLOCK, hq)[:, :length]
    return o, lse

def to_strided(t, d):
    b, s = t.shape[:2]
    sp = -(-s // d) * d
    t = jnp.pad(t, ((0, 0), (0, sp - s)) + ((0, 0),) * (t.ndim - 2))
    t = jnp.moveaxis(t.reshape((b, sp // d, d) + t.shape[2:]), 2, 1)
    return t.reshape((b * d, sp // d) + t.shape[3:])

def from_strided(t, b, s, d):
    length = t.shape[1]
    t = jnp.moveaxis(t.reshape((b, d, length) + t.shape[2:]), 1, 2)
    return t.reshape((b, length * d) + t.shape[3:])[:, :s]

def swa_dilated_layer(h, w_in, sinks, w_out, rel_bias):
    b, s, _ = h.shape
    splits = list(np.cumsum([A_WIDTH, A_KV_WIDTH, A_KV_WIDTH, B_WIDTH, B_WIDTH, B_WIDTH]))
    qa, ka, va, qb, kb, vb, z = jnp.split(h @ w_in, splits, axis=-1)
    qa = qa.reshape(b, s, A_HEADS, HEAD_DIM)
    ka = ka.reshape(b, s, A_KV_HEADS, HEAD_DIM)
    va = va.reshape(b, s, A_KV_HEADS, HEAD_DIM)
    qb, kb, vb = (t.reshape(b, s, B_HEADS, HEAD_DIM) for t in (qb, kb, vb))

    bias_a, band_a = band_bias(rel_bias[:, :A_HEADS], 1, A_WINDOW)
    oa, _ = banded_attention(qa, ka, va, bias_a, band_a, sinks)

    outs, lses = [], []
    for window, dil in B_CONFIGS:
        bias_b, band_b = band_bias(rel_bias[:, A_HEADS:], dil, window // dil)
        o, lse = banded_attention(to_strided(qb, dil), to_strided(kb, dil),
                                  to_strided(vb, dil), bias_b, band_b)
        outs.append(from_strided(o, b, s, dil))
        lses.append(from_strided(lse, b, s, dil))
    wts = jax.nn.softmax(jnp.stack(lses), axis=0)
    ob = jnp.sum(wts[..., None] * jnp.stack(outs).astype(jnp.float32), axis=0).astype(h.dtype)

    o = jnp.concatenate([oa.reshape(b, s, A_WIDTH), ob.reshape(b, s, B_WIDTH)], axis=-1)
    return (o * jax.nn.silu(z)) @ w_out

def rope(t, cos, sin):
    half = t.shape[-1] // 2
    t1, t2 = t[..., :half], t[..., half:]
    return jnp.concatenate([t1 * cos - t2 * sin, t1 * sin + t2 * cos], axis=-1).astype(t.dtype)

def mla_layer(h, positions, w_in, q_norm, w_qb, kv_norm, w_kvb, w_out):
    b, s, _ = h.shape
    splits = list(np.cumsum([C_Q_RANK, C_KV_RANK, C_ROPE]))
    c_q, c_kv, k_pe, z = jnp.split(h @ w_in, splits, axis=-1)
    q = (rmsnorm_2(c_q, q_norm) @ w_qb).reshape(b, s, C_HEADS, C_NOPE + C_ROPE)
    q_nope, q_pe = q[..., :C_NOPE], q[..., C_NOPE:]
    kv = (rmsnorm_2(c_kv, kv_norm) @ w_kvb).reshape(b, s, C_HEADS, C_NOPE + C_V)
    k_nope, v = kv[..., :C_NOPE], kv[..., C_NOPE:]

    inv_freq = ROPE_THETA ** (-jnp.arange(0, C_ROPE, 2, dtype=jnp.float32) / C_ROPE)
    ang = positions.astype(jnp.float32)[..., None] * inv_freq
    cos, sin = jnp.cos(ang)[:, :, None], jnp.sin(ang)[:, :, None]
    q_pe = rope(q_pe, cos, sin)
    k_pe = rope(k_pe[:, :, None], cos, sin)[:, :, 0]

    scale = (C_NOPE + C_ROPE) ** -0.5
    nb = s // BLOCK
    kpos = jnp.arange(s)

    def to_blocks(t):
        return jnp.moveaxis(t.reshape((b, nb, BLOCK) + t.shape[2:]), 1, 0)

    def attend_block(args):
        qn, qp, blk = args
        sc = (jnp.einsum('bqhd,bkhd->bhqk', qn, k_nope)
              + jnp.einsum('bqhr,bkr->bhqk', qp, k_pe)).astype(jnp.float32) * scale
        qpos = blk * BLOCK + jnp.arange(BLOCK)
        sc = jnp.where(kpos[None, :] <= qpos[:, None], sc, -jnp.inf)
        p = jax.nn.softmax(sc, axis=-1).astype(v.dtype)
        return jnp.einsum('bhqk,bkhd->bqhd', p, v)

    o = lax.map(attend_block, (to_blocks(q_nope), to_blocks(q_pe), jnp.arange(nb)))
    o = jnp.moveaxis(o, 0, 1).reshape(b, s, C_WIDTH)
    return (o * jax.nn.silu(z)) @ w_out

def second_inputs(seed: int = 0) -> dict:
    key = jax.random.key(seed)
    ks = jax.random.split(key, 16)
    f32 = jnp.float32

    def dense(k, shape):
        return jax.random.normal(k, shape, f32) * shape[-2] ** -0.5

    def gain(k, shape):
        return 1.0 + 0.02 * jax.random.normal(k, shape, f32)

    return {
        "x": jax.random.normal(ks[0], (BATCH, SEQ, D_MODEL), f32),
        "positions": jnp.tile(jnp.arange(SEQ, dtype=jnp.int32)[None, :], (BATCH, 1)),
        "norm_w": gain(ks[1], (DEPTH, D_MODEL)),
        "rel_bias": 0.5 * jax.random.normal(ks[2], (NUM_BUCKETS, A_HEADS + B_HEADS), f32),
        "ab_w_in": dense(ks[3], (N_AB, D_MODEL, AB_IN)),
        "ab_sinks": jax.random.normal(ks[4], (N_AB, A_HEADS), f32),
        "ab_w_out": dense(ks[5], (N_AB, AB_WIDTH, D_MODEL)),
        "c_w_in": dense(ks[6], (N_C, D_MODEL, C_IN)),
        "c_q_norm": gain(ks[7], (N_C, C_Q_RANK)),
        "c_w_qb": dense(ks[8], (N_C, C_Q_RANK, C_HEADS * (C_NOPE + C_ROPE))),
        "c_kv_norm": gain(ks[9], (N_C, C_KV_RANK)),
        "c_w_kvb": dense(ks[10], (N_C, C_KV_RANK, C_HEADS * (C_NOPE + C_V))),
        "c_w_out": dense(ks[11], (N_C, C_WIDTH, D_MODEL)),
        "final_norm": gain(ks[12], (D_MODEL,)),
    }

def second_block(x, positions, norm_w, rel_bias, ab_w_in, ab_sinks, ab_w_out,
              c_w_in, c_q_norm, c_w_qb, c_kv_norm, c_w_kvb, c_w_out, final_norm):
    for layer in range(DEPTH):
        h = rmsnorm_2(x, norm_w[layer])
        i = layer // 2
        if layer % 2 == 0:
            y = swa_dilated_layer(h, ab_w_in[i], ab_sinks[i], ab_w_out[i], rel_bias)
        else:
            y = mla_layer(h, positions, c_w_in[i], c_q_norm[i], c_w_qb[i],
                          c_kv_norm[i], c_w_kvb[i], c_w_out[i])
        x = x + y
    return rmsnorm_2(x, final_norm)


def setup_inputs(seed=0):
    out = dict(first_inputs(seed))
    for name, value in second_inputs(seed + 1).items():
        if name != "x":
            out[name + "_2"] = value
    return out


def reference(
    x, c, ctx, c_ctx, ada_w, ada_b, norm1_g, norm2_g, final_g, ga_w_in, ga_b_in, ga_ln_g,
    ga_ln_b, ga_w_s, ga_b_s, ga_w_out, ga_b_out, rw_mu, rw_wr, rw_wk, rw_wv, rw_wo, rw_w0,
    rw_w1, rw_w2, rw_a0, rw_a1, rw_a2, rw_g1, rw_g2, rw_k_k, rw_k_a, rw_r_k, rw_ln_g, rw_ln_b,
    moe_w_grp, moe_b_grp, moe_w_exp, moe_b_exp, moe_w_gate, moe_w_up, moe_w_down, positions_2,
    norm_w_2, rel_bias_2, ab_w_in_2, ab_sinks_2, ab_w_out_2, c_w_in_2, c_q_norm_2, c_w_qb_2,
    c_kv_norm_2, c_w_kvb_2, c_w_out_2, final_norm_2,
):
    x = first_block(
        x, c, ctx, c_ctx, ada_w, ada_b, norm1_g, norm2_g, final_g, ga_w_in, ga_b_in, ga_ln_g,
        ga_ln_b, ga_w_s, ga_b_s, ga_w_out, ga_b_out, rw_mu, rw_wr, rw_wk, rw_wv, rw_wo, rw_w0,
        rw_w1, rw_w2, rw_a0, rw_a1, rw_a2, rw_g1, rw_g2, rw_k_k, rw_k_a, rw_r_k, rw_ln_g,
        rw_ln_b, moe_w_grp, moe_b_grp, moe_w_exp, moe_b_exp, moe_w_gate, moe_w_up, moe_w_down,
    )
    return second_block(
        x, positions_2, norm_w_2, rel_bias_2, ab_w_in_2, ab_sinks_2, ab_w_out_2, c_w_in_2,
        c_q_norm_2, c_w_qb_2, c_kv_norm_2, c_w_kvb_2, c_w_out_2, final_norm_2,
    )


_drawn_inputs = setup_inputs


def setup_inputs(seed=0):
    import zlib

    import numpy as np

    out = dict(_drawn_inputs(seed))
    spreads = {}
    factors = {'ga_b_in': 4.689,
     'ga_ln_g': 3.171,
     'ga_ln_b': 8.0,
     'ga_b_out': 4.057,
     'rw_w1': 6.46,
     'rw_w2': 7.443,
     'rw_a1': 2.755,
     'rw_k_k': 2.849,
     'rw_ln_g': 2.81,
     'rw_ln_b': 8.0,
     'moe_b_grp': 4.407,
     'moe_b_exp': 7.235,
     'norm_w_2': 8.0,
     'ab_sinks_2': 8.0,
     'c_q_norm_2': 8.0,
     'c_kv_norm_2': 8.0,
     'final_norm_2': 2.817}
    for name, (base, spread) in spreads.items():
        noise = np.random.default_rng([zlib.crc32(name.encode()), seed]).standard_normal(out[name].shape)
        drawn = base * np.exp(spread * noise) if base else spread * noise
        out[name] = jnp.asarray(drawn.astype(out[name].dtype))
    for name, factor in factors.items():
        out[name] = (out[name] * factor).astype(out[name].dtype)
    return out
```

```python
from contextlib import ExitStack, contextmanager

import numpy as np

import concourse.bass as bass
from concourse import mybir

P = 128
F32 = mybir.dt.float32
I32 = mybir.dt.int32
U32 = mybir.dt.uint32
ALU = mybir.AluOpType
ACT = mybir.ActivationFunctionType
AX = mybir.AxisListType.X

D = 1024
KD = D // P
T = 512
TC = 256
NT = T // P
NTA = (T + TC) // P
TA = T + TC
W = 2 * D
KW = W // P
NMOD = 6
NEG = -1.0e30
HALF = 512


@contextmanager
def signals(nc, names, soft=None):
    soft = soft or {}
    with ExitStack() as held:
        sems = [soft[n] if n in soft else held.enter_context(nc.semaphore(n)) for n in names.split()]
        hard = [s for n, s in zip(names.split(), sems) if n not in soft]
        yield sems
        with nc.Block() as block:
            @block.sync
            def _(sp):
                for s in hard:
                    sp.sem_clear(s)

            if len(hard) < len(sems):
                @block.gpsimd
                def _(pool):
                    pool.dma_reset()
                    for n in names.split():
                        if n in soft:
                            pool.sem_clear(soft[n])


class Chain:

    def __init__(self, eng, sem):
        self.eng, self.sem, self.n = eng, sem, 0

    def __call__(self, ins):
        self.n += 1
        ins.then_inc(self.sem, 1)
        self.eng.wait_ge(self.sem, self.n)

    def restart(self):
        self.eng.sem_clear(self.sem)
        self.n = 0


def rows(ap, offset, n, parts=P):
    return bass.AP(tensor=ap.tensor, offset=ap.offset + offset, ap=[[0, parts], [1, n]])


def side_by_side(parts):
    where, cols, at = {}, [], 0
    for k, v in parts.items():
        where[k] = (at, v.shape[1])
        at += v.shape[1]
        cols.append(np.asarray(v, np.float32))
    return where, np.ascontiguousarray(np.concatenate(cols, 1))


def constants():
    i, j = np.meshgrid(np.arange(P), np.arange(P), indexing="ij")
    return side_by_side({"ident": i == j, "before": i < j, "ones": np.ones((P, P)), "iota": np.tile(np.arange(32), (P, 1))})


def scan_constants():
    i, j = np.meshgrid(np.arange(P), np.arange(P), indexing="ij")
    same = (i // CHUNK) == (j // CHUNK)
    parts = {
        "head_ones": i // 64 == j // 64, "head_pick": i[:, :2] // 64 == j[:, :2],
        "lt0": same & (i < j), "le0": same & (i <= j), "lt1": same & (i > j), "le1": same & (i >= j),
        "scan_keep": np.tile((np.arange(TA) % CHUNK != 0), (P, 1)),
    }
    size, n = 2, 0
    while size <= CHUNK:
        quarter = (i // size == j // size) & (i % size >= size // 2) & (j % size < size // 2)
        parts[f"q1_{n}"], parts[f"q0_{n}"] = quarter.T, quarter
        size, n = 2 * size, n + 1
    return side_by_side(parts)


CHUNK = 64
NB0 = 32 + (2 * TA) // P
NB1 = 32 + (2 * T) // P
WHERE, CONST = constants()
SCAN_WHERE, SCAN_CONST = scan_constants()


class Core:

    def __init__(self, nc, held, ins):
        self.nc, self.ins = nc, ins
        sb = lambda name, shape, dt=F32: held.enter_context(nc.sbuf_tensor(name, shape, dt))
        self.x = sb("x_tokens", [P, NTA, D])
        self.const = sb("const_cols", [P, CONST.shape[1]])
        self.ps = held.enter_context(nc.psum_tensor("banks", [P, 8, HALF], F32))
        self.calls = 0
        self.soft = {n: held.enter_context(nc.semaphore(n)) for n in
                     "cols_in params_in pos_in x_in x_in0 x_in1 y_out y_out0 y_out1 scattered".split()}
        self.mods = nc.dram_tensor("mods", [2, 2, NMOD, D], F32, kind="Internal").ap()

    def c(self, name, parts=P):
        at, n = WHERE[name]
        return self.const[0:parts, at:at + n]


def load_start(core):
    nc, ins = core.nc, core.ins
    with signals(nc, "loaded") as (loaded,):
        with nc.Block() as block:
            @block.sync
            def _(sp):
                sp.dma_start(core.x[:, 0:NT, :], ins["x"].rearrange("a (t p) d -> p (a t) d", p=P)).then_inc(loaded, 16)
                sp.dma_start(core.x[:, NT:NTA, :], ins["ctx"].rearrange("a (t p) d -> p (a t) d", p=P)).then_inc(loaded, 16)
                sp.dma_start(core.const[:, :], ins["const"]).then_inc(loaded, 16)
                sp.wait_ge(loaded, 48)


def modulation(core):
    nc, ins = core.nc, core.ins
    N = NMOD * D // HALF
    RING = 3
    with ExitStack() as held:
        sb = lambda name, shape, dt=F32: held.enter_context(nc.sbuf_tensor(name, shape, dt))
        c_rows = sb("c_rows", [2, D])
        c_cols = sb("c_cols", [P, KD, 2])
        wring = sb("ada_ring", [P, RING, KD, HALF])
        out = sb("mod_rows", [2, 2 * NMOD * D])
        gain = sb("gain_rows", [2, 4, D])
        sems = held.enter_context(signals(nc, "c_in silu_done c_turned c_ready bias_in w_in0 w_in1 w_in2 w_used product taken dve_chain stored"))
        c_in, silu_done, c_turned, c_ready, bias_in, w0, w1, w2, w_used, product, taken, chain_s, stored = sems
        w_in = [w0, w1, w2]
        with nc.Block() as block:
            @block.sync
            def _(sp):
                sp.dma_start(c_rows[0:1, :], ins["c"]).then_inc(c_in, 16)
                sp.dma_start(c_rows[1:2, :], ins["c_ctx"].rearrange("(a d) -> a d", a=1)).then_inc(c_in, 16)
                for layer in range(2):
                    sp.dma_start(out[:, layer * NMOD * D:(layer + 1) * NMOD * D],
                                 rows(ins["ada_b"], layer * NMOD * D, NMOD * D, 2)).then_inc(bias_in, 16)
                    sp.dma_start(gain[:, layer, :], rows(ins["norm1_g"], layer * D, D, 2)).then_inc(bias_in, 16)
                    sp.dma_start(gain[:, 2 + layer, :], rows(ins["norm2_g"], layer * D, D, 2)).then_inc(bias_in, 16)
                for layer in range(2):
                    src = ins["ada_w"][layer].rearrange("(k p) n -> p k n", p=P)
                    with sp.Fori(0, N // RING) as i:
                        for r in range(RING):
                            sp.wait_ge(w_used, i * RING + (layer * N + r + 1))
                            sp.dma_start(wring[:, r, :, :], src[:, :, bass.ds(i * (RING * HALF) + r * HALF, HALF)]).then_inc(w_in[r], 16)
                sp.wait_ge(stored, 1)
                for layer in range(2):
                    sp.dma_start(core.mods[layer].rearrange("s m d -> s (m d)"),
                                 out[:, layer * NMOD * D:(layer + 1) * NMOD * D]).then_inc(c_in, 16)
                sp.wait_ge(c_in, 64)

            @block.scalar
            def _(act):
                act.wait_ge(c_in, 32)
                act.activation(c_rows[:, :], c_rows[:, :], ACT.Silu).then_inc(silu_done, 1)

            @block.tensor
            def _(pe):
                pe.wait_ge(silu_done, 1)
                for k in range(KD):
                    last = pe.transpose(core.ps[:, 0, 2 * k:2 * k + 2], c_rows[:, k * P:(k + 1) * P], core.c("ident", 2)[:, 0:2])
                last.then_inc(c_turned, 1)
                pe.sem_inc(w_used, RING)
                pe.wait_ge(c_ready, 1)
                for layer in range(2):
                    with pe.Fori(0, N // RING) as i:
                        for r in range(RING):
                            pe.wait_ge(w_in[r], i * 16 + (layer * (N // RING) + 1) * 16)
                            pe.wait_ge(taken, i * RING + (layer * N + r + 1))
                            for k in range(KD):
                                last = pe.matmul(core.ps[0:2, 1 + r, :], c_cols[:, k, :], wring[:, r, k, :], start=k == 0, stop=k == KD - 1)
                            last.then_inc(product, 1)
                            pe.wait_ge(product, i * RING + (layer * N + r + 1))
                            pe.sem_inc(w_used, 1)

            @block.vector
            def _(dve):
                chain = Chain(dve, chain_s)
                dve.wait_ge(c_turned, 1)
                dve.tensor_copy(c_cols[:, :, :].rearrange("p k s -> p (k s)"), core.ps[:, 0, 0:2 * KD]).then_inc(c_ready, 1)
                dve.wait_ge(bias_in, 96)
                dve.sem_inc(taken, RING)
                for layer in range(2):
                    with dve.Fori(0, N // RING) as i:
                        for r in range(RING):
                            dve.wait_ge(product, i * RING + (layer * N + r + 1))
                            cols = out[:, bass.ds(i * (RING * HALF) + (layer * N + r) * HALF, HALF)]
                            dve.tensor_tensor(cols, core.ps[0:2, 1 + r, :], cols, ALU.add).then_inc(taken, 1)
                dve.wait_ge(taken, RING + 2 * N)
                for layer in range(2):
                    for half in range(2):
                        at = (layer * NMOD + 1 + 3 * half) * D
                        last = dve.scalar_tensor_tensor(out[:, at:at + D], out[:, at:at + D], 1.0, gain[:, 2 * half + layer, :],
                                                        ALU.add, ALU.mult)
                        chain(last)
                dve.sem_inc(stored, 1)


def norm_turn(core, tiles, gains, shifts, eps, hT, keep=None):
    nc = core.nc
    n = len(tiles)
    name = lambda row: (row[0].tensor.name, row[0].offset + row[1])
    core.calls += 1
    tag = core.calls
    srcs = list({name(row): row for row in gains + shifts if row is not None}.values())
    place = {name(row): k for k, row in enumerate(srcs)}
    with ExitStack() as held:
        sb = lambda name, shape, dt=F32: held.enter_context(nc.sbuf_tensor(f"{name}_{tag}", shape, dt))
        spread = sb("spread_rows", [P, len(srcs), D])
        h = sb("h_tokens", [P, 2, D])
        junk = sb("squares", [P, D])
        ss = sb("sum_squares", [P, n])
        rs = sb("rstd", [P, n])
        sems = held.enter_context(signals(nc, "spread_in squared rooted rstd_ready scaled h_ready turned moved_low moved_high kept0 kept1 dve_chain act_chain"))
        spread_in, squared, rooted, rstd_ready, scaled, h_ready, turned, moved_low, moved_high, kept0, kept1, chain_s, act_s = sems
        kept = [kept0, kept1]
        with nc.Block() as block:
            @block.sync
            def _(sp):
                for k, (ap, at) in enumerate(srcs):
                    sp.dma_start(spread[:, k, :], rows(ap, at, D)).then_inc(spread_in, 16)
                if keep is not None:
                    for j, t in enumerate(tiles):
                        sp.wait_ge(h_ready, j + 1)
                        sp.dma_start(keep[t * P:(t + 1) * P, :], h[:, j % 2, :]).then_inc(kept[j % 2], 16)
                    sp.wait_ge(kept[0], 16 * ((n + 1) // 2))
                    sp.wait_ge(kept[1], 16 * (n // 2))

            @block.scalar
            def _(act):
                chain = Chain(act, act_s)
                for j, t in enumerate(tiles):
                    chain(act.activation(junk[:, :], core.x[:, t, :], ACT.Square, accum_out=ss[:, j:j + 1]))
                act.sem_inc(squared, 1)
                act.wait_ge(rooted, 1)
                act.activation(rs[:, :], ss[:, :], ACT.Sqrt).then_inc(rstd_ready, 1)
                for j, t in enumerate(tiles):
                    act.wait_ge(turned, 2 * j + 2)
                    act.activation(hT[:, 4:8, t * P:(t + 1) * P], core.ps[:, 2 * (j % 2) + 1, :].rearrange("p (k c) -> p k c", k=4),
                                   ACT.Copy).then_inc(moved_high, 1)

            @block.vector
            def _(dve):
                chain = Chain(dve, chain_s)
                dve.wait_ge(squared, 1)
                dve.tensor_scalar(ss[:, :], ss[:, :], 1.0 / D, eps, ALU.mult, ALU.add).then_inc(rooted, 1)
                dve.wait_ge(rstd_ready, 1)
                chain(dve.reciprocal(rs[:, :], rs[:, :]))
                dve.wait_ge(spread_in, 16 * len(srcs))

                def evacuate(j):
                    dve.wait_ge(turned, 2 * j + 1)
                    dve.tensor_copy(hT[:, 0:4, tiles[j] * P:(tiles[j] + 1) * P],
                                    core.ps[:, 2 * (j % 2), :].rearrange("p (k c) -> p k c", k=4)).then_inc(moved_low, 1)

                for j, t in enumerate(tiles):
                    if j >= 2:
                        dve.wait_ge(turned, 2 * (j - 1))
                        if keep is not None:
                            dve.wait_ge(kept[j % 2], 16 * (j // 2))
                    g, s = place[name(gains[j])], shifts[j]
                    op = dve.scalar_tensor_tensor(h[:, j % 2, :], core.x[:, t, :], rs[:, j:j + 1], spread[:, g, :], ALU.mult, ALU.mult)
                    if s is not None:
                        chain(op)
                        op = dve.tensor_tensor(h[:, j % 2, :], h[:, j % 2, :], spread[:, place[name(s)], :], ALU.add)
                    op.then_inc(h_ready, 1)
                    if j >= 1:
                        evacuate(j - 1)
                evacuate(n - 1)

            @block.tensor
            def _(pe):
                for j in range(n):
                    pe.wait_ge(h_ready, j + 1)
                    if j >= 2:
                        pe.wait_ge(moved_low, j - 1)
                        pe.wait_ge(moved_high, j - 1)
                    for half in range(2):
                        for k in range(4):
                            c0 = (half * 4 + k) * P
                            last = pe.transpose(core.ps[:, 2 * (j % 2) + half, k * P:(k + 1) * P], h[:, j % 2, c0:c0 + P], core.c("ident"))
                        last.then_inc(turned, 1)


def mod_row(core, layer, stream, m):
    return (core.mods, ((layer * 2 + stream) * NMOD + m) * D)


def tables(nt):
    nb = 32 + 2 * nt
    lane = np.arange(P, dtype=np.int32)
    cells = np.zeros((P, nb, 2), np.int32)
    cells[:, :, 1] = 2 * nt * P + lane[:, None]
    entries = np.zeros((P, 2, nt, 2), np.int32)
    for c in range(2):
        for t in range(nt):
            entries[:, c, t, 0] = t * P + lane
            entries[:, c, t, 1] = (c * nt + t) * P + lane
    return cells.reshape(P, -1), entries.reshape(P, -1)



def gmlp(core, hT):
    nc, ins = core.nc, core.ins
    w_in = ins["ga_w_in"][0].rearrange("(k p) n -> p k n", p=P)
    w_out = ins["ga_w_out"][0].rearrange("(k p) n -> p k n", p=P)
    N = 2 * W // HALF
    NU = N // 2
    TOK = TA // 2
    with ExitStack() as held:
        sb = lambda name, shape, dt=F32: held.enter_context(nc.sbuf_tensor(name, shape, dt))
        uT = sb("u_channels", [P, KW, TA])
        v = sb("v_tokens", [P, NTA, W])
        wring = sb("gmlp_weights", [P, 2, KD, HALF])
        b_u = sb("b_u_cols", [P, KW])
        b_v = sb("b_v_spread", [P, W])
        ws = sb("spatial", [P, KW, P])
        wsT = ws
        bs = sb("spatial_bias", [1, KW, P])
        stats = sb("v_stats", [P, NTA, W // HALF, 6])
        mv = sb("v_mean_var", [P, NTA, 2])
        eps = sb("ln_eps", [P, NTA])
        ln_g = hT[:, 0:2, :].rearrange("p k t -> p (k t)")[:, 0:1536]
        flat = hT[:, :, :].rearrange("p k t -> p (k t)")
        ln_g, ln_b = flat[:, 0:W], flat[:, W:2 * W]
        b_o, gt_l, gt_c = (flat[:, n * D:(n + 1) * D] for n in range(3))
        sems = held.enter_context(signals(nc, "consts_in cols_in w0_in w1_in u_sum u_done v_sum v_biased v_done dve_chain act_chain ws_turned ws_ready", core.soft))
        consts_in, cols_in, w0_in, w1_in, u_sum, u_done, v_sum, v_biased, v_done, chain_s, act_s, ws_turned, ws_ready = sems
        w_arrived = [w0_in, w1_in]

        with nc.Block() as block:
            @block.sync
            def _(sp):
                sp.dma_start(ws[:, :, :], ins["ga_w_s"][0].rearrange("g p q -> p g q")).then_inc(consts_in, 16)
                sp.dma_start(bs[:, :, :], ins["ga_b_s"]).then_inc(consts_in, 16)
                sp.dma_start(b_v[:, :], rows(ins["ga_b_in"], W, W)).then_inc(consts_in, 16)
                for n in range(N):
                    if n >= 2:
                        if n - 2 < NU:
                            sp.wait_ge(u_sum, 8 * (n - 1))
                        else:
                            sp.wait_ge(v_sum, NTA * (n - 2 - NU + 1))
                    sp.dma_start(wring[:, n % 2, :, :], w_in[:, :, n * HALF:(n + 1) * HALF]).then_inc(w_arrived[n % 2], 16)

            @block.gpsimd
            def _(pool):
                with nc.allow_non_contiguous_dma(reason="2048 bias values, one by one"):
                    pool.dma_start(b_u[:, :], ins["ga_b_in"][0, 0:W].rearrange("(k p) -> p k", p=P)).then_inc(cols_in, 16)

            @block.tensor
            def _(pe):
                pe.wait_ge(consts_in, 48)
                for g in range(KW):
                    pe.transpose(core.ps[:, g // 4, (g % 4) * P:(g % 4 + 1) * P], ws[:, g, :], core.c("ident")).then_inc(ws_turned, 1)
                pe.wait_ge(ws_ready, 1)
                step = 0
                for n in range(NU):
                    pe.wait_ge(w_arrived[n % 2], 16 * (n // 2 + 1))
                    for m in range(4):
                        for half in range(2):
                            if step >= 8:
                                pe.wait_ge(u_done, step - 7)
                            for k in range(KD):
                                last = pe.matmul(core.ps[:, step % 8, 0:TOK], wring[:, n % 2, k, m * P:(m + 1) * P],
                                                 hT[:, k, half * TOK:(half + 1) * TOK], start=k == 0, stop=k == KD - 1)
                            last.then_inc(u_sum, 1)
                            step += 1
                pe.wait_ge(u_done, step)
                step = 0
                for n in range(NU, N):
                    pe.wait_ge(w_arrived[n % 2], 16 * (n // 2 + 1))
                    for t in range(NTA):
                        if step >= 8:
                            pe.wait_ge(v_biased, step - 7)
                        for k in range(KD):
                            last = pe.matmul(core.ps[:, step % 8, :], hT[:, k, t * P:(t + 1) * P], wring[:, n % 2, k, :],
                                             start=k == 0, stop=k == KD - 1)
                        last.then_inc(v_sum, 1)
                        step += 1

            @block.scalar
            def _(act):
                act.wait_ge(cols_in, 16)
                step = 0
                for n in range(NU):
                    for m in range(4):
                        for half in range(2):
                            step += 1
                            act.wait_ge(u_sum, step)
                            g = n * 4 + m
                            act.activation(uT[:, g, half * TOK:(half + 1) * TOK], core.ps[:, (step - 1) % 8, 0:TOK], ACT.Gelu,
                                           bias=b_u[:, g:g + 1]).then_inc(u_done, 1)
                step = 0
                for n in range(NU):
                    for t in range(NTA):
                        step += 1
                        act.wait_ge(v_biased, step)
                        part = v[:, t, n * HALF:(n + 1) * HALF]
                        act.activation(part, part, ACT.Gelu).then_inc(v_done, 1)

            @block.vector
            def _(dve):
                for g in range(4):
                    dve.wait_ge(ws_turned, 4 * g + 4)
                    chain_op = dve.tensor_copy(ws[:, 4 * g:4 * g + 4, :].rearrange("p g q -> p (g q)"), core.ps[:, g, :])
                chain_op.then_inc(ws_ready, 1)
                dve.wait_ge(consts_in, 48)

                def stat(step):
                    n, t = divmod(step, NTA)
                    dve.wait_ge(v_done, step + 1)
                    dve.bn_stats(stats[:, t, n, :], v[:, t, n * HALF:(n + 1) * HALF])

                for step in range(NU * NTA):
                    n, t = divmod(step, NTA)
                    dve.wait_ge(v_sum, step + 1)
                    dve.tensor_tensor(v[:, t, n * HALF:(n + 1) * HALF], core.ps[:, step % 8, :], b_v[:, n * HALF:(n + 1) * HALF],
                                      ALU.add).then_inc(v_biased, 1)
                    if step >= 2:
                        stat(step - 2)
                stat(NU * NTA - 2)
                stat(NU * NTA - 1)

        sems = held.enter_context(signals(nc, "ln_in varied rooted v_ready mixed multiplied wo_in0 wo_in1 out_sum added rows_in"))
        ln_in, varied, rooted, v_ready, mixed, multiplied, wo_in0, wo_in1, out_sum, added, rows_in = sems
        wo_in = [wo_in0, wo_in1]
        GB = KW // 4
        with nc.Block() as block:
            @block.sync
            def _(sp):
                sp.dma_start(ln_g, rows(ins["ga_ln_g"], 0, W)).then_inc(ln_in, 16)
                sp.dma_start(ln_b, rows(ins["ga_ln_b"], 0, W)).then_inc(ln_in, 16)
                for n in range(4):
                    if n >= 2:
                        sp.wait_ge(out_sum, n - 1)
                    half, rest = divmod(n, 2)
                    sp.dma_start(wring[:, n % 2, :, :], w_out[:, rest * KD:(rest + 1) * KD, half * HALF:(half + 1) * HALF]).then_inc(wo_in[n % 2], 16)
                    if n == 1:
                        sp.wait_ge(v_ready, NTA)
                        sp.dma_start(b_o, rows(ins["ga_b_out"], 0, D)).then_inc(rows_in, 16)
                        for dst, s in ((gt_l, 0), (gt_c, 1)):
                            ap, at = mod_row(core, 0, s, 2)
                            sp.dma_start(dst, rows(ap, at, D)).then_inc(rows_in, 16)

            @block.scalar
            def _(act):
                act.wait_ge(varied, 1)
                act.activation(eps[:, :], eps[:, :], ACT.Sqrt).then_inc(rooted, 1)

            @block.vector
            def _(dve):
                chain = Chain(dve, chain_s)
                for t in range(NTA):
                    last = dve.bn_aggr(mv[:, t, :], stats[:, t, :, :].rearrange("p n s -> p (n s)"))
                chain(last)
                dve.tensor_scalar(eps[:, :], mv[:, :, 1], 1e-5, None, ALU.add).then_inc(varied, 1)
                dve.wait_ge(rooted, 1)
                chain(dve.reciprocal(eps[:, :], eps[:, :]))
                dve.wait_ge(ln_in, 32)

                def multiply(t):
                    for b in range(GB):
                        dve.wait_ge(mixed, t * GB + b + 1)
                        part = uT[:, 4 * b:4 * b + 4, t * P:(t + 1) * P]
                        dve.tensor_tensor(part, part, core.ps[:, (t * GB + b) % 8, :].rearrange("p (g q) -> p g q", g=4),
                                          ALU.mult).then_inc(multiplied, 1)

                for t in range(NTA):
                    chain(dve.tensor_scalar(v[:, t, :], v[:, t, :], mv[:, t, 0:1], eps[:, t:t + 1], ALU.subtract, ALU.mult))
                    chain(dve.tensor_tensor(v[:, t, :], v[:, t, :], ln_g, ALU.mult))
                    dve.tensor_tensor(v[:, t, :], v[:, t, :], ln_b, ALU.add).then_inc(v_ready, 1)
                    if t >= 1:
                        multiply(t - 1)
                multiply(NTA - 1)
                dve.wait_ge(rows_in, 48)
                for half in range(2):
                    dve.wait_ge(out_sum, 2 * half + 2)
                    cols = slice(half * HALF, (half + 1) * HALF)
                    for t in range(NTA):
                        y = v[:, t, cols]
                        chain(dve.tensor_tensor(y, core.ps[:, (half * NTA + t) % 8, :], b_o[:, cols], ALU.add))
                        chain(dve.tensor_tensor(y, y, (gt_l if t < NT else gt_c)[:, cols], ALU.mult))
                        dve.tensor_tensor(core.x[:, t, cols], core.x[:, t, cols], y, ALU.add).then_inc(added, 1)

            @block.tensor
            def _(pe):
                for t in range(NTA):
                    pe.wait_ge(v_ready, t + 1)
                    for b in range(GB):
                        step = t * GB + b
                        if step >= 8:
                            pe.wait_ge(multiplied, step - 7)
                        bank = core.ps[:, step % 8, :]
                        pe.matmul(bank, core.c("ones", 1), bs[:, 4 * b:4 * b + 4, :].rearrange("a g q -> a (g q)"), start=True, stop=False)
                        for g in range(4):
                            last = pe.matmul(bank[:, g * P:(g + 1) * P], v[:, t, (4 * b + g) * P:(4 * b + g + 1) * P], wsT[:, 4 * b + g, :],
                                             start=False, stop=g == 3)
                        last.then_inc(mixed, 1)
                pe.wait_ge(multiplied, NTA * GB)
                for half in range(2):
                    for rest in range(2):
                        pe.wait_ge(wo_in[rest], 16 * (half + 1))
                        for t in range(NTA):
                            bank = (half * NTA + t) % 8
                            if half and t >= 2 and rest == 0:
                                pe.wait_ge(added, t - 1)
                            for k in range(KD):
                                last = pe.matmul(core.ps[:, bank, :], uT[:, rest * KD + k, t * P:(t + 1) * P], wring[:, rest, k, :],
                                                 start=rest == 0 and k == 0, stop=rest == 1 and k == KD - 1)
                        last.then_inc(out_sum, 1)


E = 32
EG = 8
NG = 4
F = 512
KF = F // P
ROUTER = NG + E


def moe(core, layer, nt):
    nc, ins = core.nc, core.ins
    tl = nt * P
    nb = E + 2 * nt
    with ExitStack() as held:
        sb = lambda name, shape, dt=F32: held.enter_context(nc.sbuf_tensor(f"{name}_{layer}", shape, dt))
        h_rows = nc.dram_tensor(f"h_rows_{layer}", [tl, D], F32, kind="Internal").ap()
        cells = nc.dram_tensor(f"cells_{layer}", [P * nb, 2], I32, kind="Internal").ap()
        y_rows = nc.dram_tensor(f"y_rows_{layer}", [2 * tl + P, D], F32, kind="Internal").ap()
        wg = sb("w_gate_ring", [P, 2, KD, F])
        wu = sb("w_up_ring", [P, 2, KD, F])
        wd = sb("w_down_ring", [P, 2, KF, D])
        weights = sb("choice_weights", [P, 2, nt])
        index = sb("cell_index", [P, nb, 2], I32)
        beyond = sb("blocks_beyond", [P, 2 * nt + 1], I32)
        gate_src = ins["moe_w_gate"][layer].rearrange("e (k p) f -> e p k f", p=P)
        up_src = ins["moe_w_up"][layer].rearrange("e (k p) f -> e p k f", p=P)
        down_src = ins["moe_w_down"][layer].rearrange("e (k p) d -> e p k d", p=P)
        gate_in, gate_in1, up_in, up_in1, down_in, down_in1 = held.enter_context(
            signals(nc, "gate_in0 gate_in1 up_in0 up_in1 down_in0 down_in1"))
        gate_in, up_in, down_in = [gate_in, gate_in1], [up_in, up_in1], [down_in, down_in1]

        with nc.Block() as block:
            @block.sync
            def _(sp):
                for r in range(2):
                    sp.dma_start(wg[:, r, :, :], gate_src[r]).then_inc(gate_in[r], 16)
                    sp.dma_start(wu[:, r, :, :], up_src[r]).then_inc(up_in[r], 16)
                    sp.dma_start(wd[:, r, :, :], down_src[r]).then_inc(down_in[r], 16)

        with nc.sbuf_tensor(f"h_turned_{layer}", [P, KD, tl], F32) as hT:
            norm_turn(core, list(range(nt)), [mod_row(core, layer, t >= NT, 4) for t in range(nt)],
                      [mod_row(core, layer, t >= NT, 3) for t in range(nt)], 1e-6, hT, keep=h_rows)
            route(core, layer, nt, nb, hT, cells, weights, index, beyond)
        experts(core, layer, nb, h_rows, y_rows, index, wg, wu, wd, gate_src, up_src, down_src, gate_in, up_in, down_in)
        experts_beyond(core, layer, nt, h_rows, y_rows, index, beyond, wg, wu, wd, gate_src, up_src, down_src)
        combine(core, layer, nt, y_rows, weights)


def route(core, layer, nt, nb, hT, cells, weights, index, beyond):
    nc, ins = core.nc, core.ins
    with ExitStack() as held:
        sb = lambda name, shape, dt=F32: held.enter_context(nc.sbuf_tensor(f"{name}_{layer}", shape, dt))
        wr = sb("router_w", [P, KD, ROUTER])
        br = sb("router_b", [P, ROUTER])
        logits = sb("router_logits", [P, nt, ROUTER])
        grp = sb("grp", [P, 4, nt, NG])
        m = sb("maxima", [P, 12, nt])
        masked = sb("masked", [P, nt, E])
        hit = sb("hit", [P, nt, E])
        work = sb("work", [P, nt, E])
        one_hot = sb("one_hot", [P, 2, nt, E])
        both = sb("both", [P, nt, E])
        pos = sb("pos", [P, nt, E])
        count = sb("count", [P, 6, E])
        slot = sb("slot", [P, 6, nt])
        choice = sb("choice", [P, 2, nt])
        cell = sb("cell", [P, 2, nt], U32)
        entry = sb("entry", [P, 2, nt, 2], I32)
        s = held.enter_context(signals(nc, "router_in cells_set logit_sum dve_chain shifted exp_done second exp2_done chosen placed cells_ready entry_in scattered index_in", core.soft))
        router_in, cells_set, logit_sum, chain_s, shifted, exp_done, second, exp2_done, chosen, placed, cells_ready, entry_in, scattered, index_in = s
        iota = core.c("iota")
        per = lambda ap, n: ap.unsqueeze(2).to_broadcast([P, nt, n])
        over = lambda ap, n: ap.unsqueeze(1).to_broadcast([P, nt, n])
        with nc.Block() as block:
            @block.sync
            def _(sp):
                sp.dma_start(cells.rearrange("(p b) c -> p (b c)", p=P), ins[f"cells{layer}"]).then_inc(cells_set, 16)
                with nc.allow_non_contiguous_dma(reason="router weights: rows of 4 and 32 columns"):
                    sp.dma_start(wr[:, :, 0:NG], ins["moe_w_grp"][layer].rearrange("(k p) n -> p k n", p=P)).then_inc(router_in, 16)
                    sp.dma_start(wr[:, :, NG:], ins["moe_w_exp"][layer].rearrange("(k p) n -> p k n", p=P)).then_inc(router_in, 16)
                    sp.dma_start(br[:, 0:NG], rows(ins["moe_b_grp"], layer * NG, NG)).then_inc(router_in, 16)
                    sp.dma_start(br[:, NG:], rows(ins["moe_b_exp"], layer * E, E)).then_inc(router_in, 16)
                    sp.dma_start(entry[:, :, :, :].rearrange("p k t c -> p (k t c)"), ins[f"entries{layer}"]).then_inc(entry_in, 16)
                    sp.wait_ge(scattered, 16 * 2 * nt)
                    sp.dma_start(index[:, :, :].rearrange("p b c -> p (b c)"), cells.rearrange("(p b) c -> p (b c)", p=P)).then_inc(index_in, 16)
                    sp.wait_ge(index_in, 16)

            @block.tensor
            def _(pe):
                pe.wait_ge(router_in, 64)
                for t in range(nt):
                    for k in range(KD):
                        last = pe.matmul(core.ps[:, 0, t * ROUTER:(t + 1) * ROUTER], hT[:, k, t * P:(t + 1) * P], wr[:, k, :],
                                         start=k == 0, stop=k == KD - 1)
                last.then_inc(logit_sum, 1)
                pe.wait_ge(chosen, 1)
                for t in range(nt):
                    for u in range(t + 1):
                        pe.matmul(core.ps[:, 1, t * E:(t + 1) * E], core.c("before" if u == t else "ones"), both[:, u, :],
                                  start=u == 0, stop=u == t)
                for t in range(nt):
                    last = pe.matmul(core.ps[:, 2, 0:E], core.c("ones"), both[:, t, :], start=t == 0, stop=t == nt - 1)
                last.then_inc(placed, 1)

            @block.scalar
            def _(act):
                act.wait_ge(shifted, 1)
                act.activation(grp[:, 3, :, :], grp[:, 0, :, :], ACT.Exp).then_inc(exp_done, 1)
                act.wait_ge(second, 1)
                act.activation(m[:, 7, :], m[:, 6, :], ACT.Exp).then_inc(exp2_done, 1)

            @block.vector
            def _(dve):
                do = Chain(dve, chain_s)
                dve.wait_ge(logit_sum, 1)
                do(dve.tensor_tensor(logits[:, :, :], core.ps[:, 0, 0:nt * ROUTER].rearrange("p (t n) -> p t n", t=nt), over(br[:, :], ROUTER), ALU.add))
                gl, el = logits[:, :, 0:NG], logits[:, :, NG:]
                do(dve.tensor_reduce(m[:, 0, :], gl, AX, ALU.max))
                dve.tensor_tensor(grp[:, 0, :, :], gl, per(m[:, 0, :], NG), ALU.subtract).then_inc(shifted, 1)
                do(dve.tensor_tensor(grp[:, 1, :, :], gl, per(m[:, 0, :], NG), ALU.is_lt))
                do(dve.scalar_tensor_tensor(grp[:, 1, :, :], grp[:, 1, :, :], 100.0, over(iota[:, 0:NG], NG), ALU.mult, ALU.add))
                do(dve.tensor_reduce(m[:, 1, :], grp[:, 1, :, :], AX, ALU.min))
                do(dve.tensor_tensor(grp[:, 2, :, :], over(iota[:, 0:NG], NG), per(m[:, 1, :], NG), ALU.is_equal))
                dve.wait_ge(exp_done, 1)
                do(dve.tensor_reduce(m[:, 2, :], grp[:, 3, :, :], AX, ALU.add))
                do(dve.reciprocal(m[:, 3, :], m[:, 2, :]))
                do(dve.tensor_scalar(grp[:, 2, :, :], grp[:, 2, :, :], -1.0, -NEG, ALU.add, ALU.mult))
                for g in range(NG):
                    op = dve.tensor_tensor(masked[:, :, g * EG:(g + 1) * EG], el[:, :, g * EG:(g + 1) * EG], per(grp[:, 2, :, g], EG), ALU.add)
                do(op)
                for c in range(2):
                    top, at = m[:, 4 + c, :], choice[:, c, :]
                    do(dve.tensor_reduce(top, masked[:, :, :], AX, ALU.max))
                    do(dve.tensor_tensor(hit[:, :, :], masked[:, :, :], per(top, E), ALU.is_lt))
                    do(dve.scalar_tensor_tensor(hit[:, :, :], hit[:, :, :], 100.0, over(iota, E), ALU.mult, ALU.add))
                    do(dve.tensor_reduce(at, hit[:, :, :], AX, ALU.min))
                    do(dve.tensor_tensor(one_hot[:, c, :, :], over(iota, E), per(at, E), ALU.is_equal))
                    if c == 0:
                        do(dve.scalar_tensor_tensor(masked[:, :, :], one_hot[:, 0, :, :], 2 * NEG, masked[:, :, :], ALU.mult, ALU.add))
                dve.tensor_tensor(both[:, :, :], one_hot[:, 0, :, :], one_hot[:, 1, :, :], ALU.add).then_inc(chosen, 1)
                dve.tensor_tensor(m[:, 6, :], m[:, 5, :], m[:, 4, :], ALU.subtract).then_inc(second, 1)
                dve.wait_ge(exp2_done, 1)
                do(dve.tensor_scalar(m[:, 8, :], m[:, 7, :], 1.0, None, ALU.add))
                do(dve.reciprocal(m[:, 8, :], m[:, 8, :]))
                do(dve.tensor_tensor(weights[:, 0, :], m[:, 3, :], m[:, 8, :], ALU.mult))
                do(dve.tensor_tensor(weights[:, 1, :], weights[:, 0, :], m[:, 7, :], ALU.mult))
                dve.wait_ge(placed, 1)
                do(dve.tensor_copy(pos[:, :, :], core.ps[:, 1, 0:nt * E].rearrange("p (t e) -> p t e", t=nt)))
                do(dve.tensor_copy(count[:, 0, :], core.ps[:, 2, 0:E]))
                do(dve.tensor_scalar(count[:, 1, :], count[:, 0, :], float(P), None, ALU.is_gt))
                for b in range(2, nt):
                    do(dve.scalar_tensor_tensor(count[:, 1, :], count[:, 0, :], float(b * P), count[:, 1, :], ALU.is_gt, ALU.add))
                do(dve.tensor_tensor_scan(count[:, 2, :], core.c("ones")[:, 0:E], count[:, 1, :], 0.0, ALU.mult, ALU.add))
                do(dve.tensor_tensor(count[:, 3, :], count[:, 2, :], count[:, 1, :], ALU.subtract))
                do(dve.scalar_tensor_tensor(count[:, 3, :], count[:, 3, :], float(E - 1), iota, ALU.add, ALU.subtract))
                for b in range(2 * nt):
                    do(dve.tensor_scalar(count[:, 4, :], count[:, 2, :], float(b), None, ALU.is_le))
                    do(dve.tensor_reduce(slot[:, 0, 0:1], count[:, 4, :], AX, ALU.add))
                    do(dve.tensor_scalar(beyond[:, b + 1:b + 2], slot[:, 0, 0:1], float(E - 1), None, ALU.min))
                do(dve.tensor_copy(beyond[:, 0:1], count[:, 2, E - 1:E]))
                for c in range(2):
                    where, shift, blk, first, got = (slot[:, n, :] for n in range(5))
                    do(dve.tensor_tensor(work[:, :, :], pos[:, :, :], one_hot[:, c, :, :], ALU.mult))
                    do(dve.tensor_reduce(where, work[:, :, :], AX, ALU.add))
                    do(dve.tensor_tensor(work[:, :, :], one_hot[:, c, :, :], over(count[:, 3, :], E), ALU.mult))
                    do(dve.tensor_reduce(shift, work[:, :, :], AX, ALU.add))
                    do(dve.tensor_scalar(first, where, float(P), None, ALU.is_ge))
                    do(dve.tensor_copy(blk, first))
                    for b in range(2, nt):
                        do(dve.scalar_tensor_tensor(blk, where, float(b * P), blk, ALU.is_ge, ALU.add))
                    do(dve.scalar_tensor_tensor(where, blk, float(-P), where, ALU.mult, ALU.add))
                    do(dve.tensor_tensor(blk, blk, shift, ALU.add))
                    do(dve.tensor_tensor(blk, blk, first, ALU.mult))
                    do(dve.tensor_tensor(blk, blk, choice[:, c, :], ALU.add))
                    do(dve.scalar_tensor_tensor(got, where, float(nb), blk, ALU.mult, ALU.add))
                    do(dve.tensor_copy(cell[:, c, :], got))
                dve.sem_inc(cells_ready, 1)

            @block.gpsimd
            def _(pool):
                pool.wait_ge(cells_set, 16)
                pool.wait_ge(entry_in, 16)
                pool.wait_ge(cells_ready, 1)
                for c in range(2):
                    for t in range(nt):
                        pool.indirect_dma_start(cells, bass.IndirectOffsetOnAxis(ap=cell[:, c, t:t + 1], axis=0),
                                                entry[:, c, t, :], None).then_inc(scattered, 16)
                pool.wait_ge(scattered, 16 * 2 * nt)


def experts(core, layer, nb, h_rows, y_rows, index, wg, wu, wd, gate_src, up_src, down_src, gate_in, up_in, down_in):
    nc = core.nc
    ps = core.ps
    X_LOW, X_HIGH, G, U, H, Y = 0, 1, 2, 3, 4, 5
    with ExitStack() as held:
        sb = lambda name, shape, dt=F32: held.enter_context(nc.sbuf_tensor(f"{name}_{layer}", shape, dt))
        take = sb("take_rows", [P, 2], I32)
        put = sb("put_rows", [P, 2], I32)
        xs = sb("x_rows", [P, 2, D])
        xT = sb("x_turned", [P, 2, KD, P])
        sg = sb("silu_gate", [P, F])
        h = sb("hidden", [P, F])
        hT = sb("hidden_turned", [P, KF, P])
        ys = sb("y_out_rows", [P, 2, D])
        s = held.enter_context(signals(nc, "x_in0 x_in1 x_used x_turned x_low x_high g_sum u_sum silu_done h_ready h_turned hT_ready y_sum y_low y_high y_free y_out0 y_out1 rows_out pool_chain", core.soft))
        x_in0, x_in1, x_used, x_turned, x_low, x_high, g_sum, u_sum, silu_done, h_ready, h_turned, hT_ready, y_sum, y_low, y_high, y_free, y_out0, y_out1, rows_out, pool_s = s
        x_in, y_out = [x_in0, x_in1], [y_out0, y_out1]
        with nc.Block() as block:
            @block.sync
            def _(sp):
                with sp.Fori(0, E // 2 - 1) as i:
                    for r in range(2):
                        sp.wait_ge(u_sum, 2 * i + (r + 1))
                        sp.dma_start(wg[:, r, :, :], gate_src[bass.ds(2 * i + (r + 2), 1)].rearrange("a p k f -> p (a k) f")).then_inc(gate_in[r], 16)
                        sp.dma_start(wu[:, r, :, :], up_src[bass.ds(2 * i + (r + 2), 1)].rearrange("a p k f -> p (a k) f")).then_inc(up_in[r], 16)
                        sp.wait_ge(y_sum, 2 * i + (r + 1))
                        sp.dma_start(wd[:, r, :, :], down_src[bass.ds(2 * i + (r + 2), 1)].rearrange("a p k f -> p (a k) f")).then_inc(down_in[r], 16)

            @block.gpsimd
            def _(pool):
                do = Chain(pool, pool_s)

                def gather(r):
                    pool.indirect_dma_start(xs[:, r, :], None, h_rows, bass.IndirectOffsetOnAxis(ap=take[:, r:r + 1].bitcast(U32), axis=0)).then_inc(x_in[r], 16)

                do(pool.tensor_copy(take[:, 0:1], index[:, 0, 0:1]))
                gather(0)
                pool.sem_inc(y_free, 2)
                with pool.Fori(0, E // 2) as i:
                    do.restart()
                    for r in range(2):
                        pool.wait_ge(x_used, 2 * i + (r + 1))
                        do(pool.tensor_copy(take[:, 1 - r:2 - r], index[:, bass.ds(2 * i + (r + 1), 1), 0:1].rearrange("p a c -> p (a c)")))
                        gather(1 - r)
                        do(pool.tensor_copy(put[:, r:r + 1], index[:, bass.ds(2 * i + r, 1), 1:2].rearrange("p a c -> p (a c)")))
                        pool.wait_ge(y_low, 2 * i + (r + 2))
                        pool.wait_ge(y_high, 2 * i + (r + 2))
                        pool.sem_inc(rows_out, 1)
                        pool.indirect_dma_start(y_rows, bass.IndirectOffsetOnAxis(ap=put[:, r:r + 1].bitcast(U32), axis=0), ys[:, r, :], None).then_inc(y_out[r], 16)
                        pool.wait_ge(y_out[r], i * 16 + 16)
                        pool.sem_inc(y_free, 1)
                pool.wait_ge(x_in[0], 16 * (E // 2 + 1))

            @block.tensor
            def _(pe):
                def turn_x(r):
                    for k in range(KD):
                        last = pe.transpose(ps[:, X_LOW + k // 4, (k % 4) * P:(k % 4 + 1) * P], xs[:, r, k * P:(k + 1) * P], core.c("ident"))
                        if k == KD - 1:
                            last.then_inc(x_turned, 1)

                pe.sem_inc(x_used, 1)
                pe.wait_ge(x_in[0], 16)
                turn_x(0)
                with pe.Fori(0, E // 2) as i:
                    for r in range(2):
                        pe.wait_ge(x_low, 2 * i + (r + 1))
                        pe.wait_ge(x_high, 2 * i + (r + 1))
                        pe.wait_ge(gate_in[r], i * 16 + 16)
                        pe.wait_ge(silu_done, 2 * i + (r + 1))
                        for k in range(KD):
                            last = pe.matmul(ps[:, G, :], xT[:, r, k, :], wg[:, r, k, :], start=k == 0, stop=k == KD - 1)
                        last.then_inc(g_sum, 1)
                        pe.wait_ge(up_in[r], i * 16 + 16)
                        pe.wait_ge(h_ready, 2 * i + (r + 1))
                        for k in range(KD):
                            last = pe.matmul(ps[:, U, :], xT[:, r, k, :], wu[:, r, k, :], start=k == 0, stop=k == KD - 1)
                        last.then_inc(u_sum, 1)
                        pe.wait_ge(x_in[1 - r], i * 16 + 16 * (r + 1))
                        turn_x(1 - r)
                        pe.wait_ge(x_turned, 2 * i + (r + 2))
                        pe.sem_inc(x_used, 1)
                        pe.wait_ge(h_ready, 2 * i + (r + 2))
                        for k in range(KF):
                            last = pe.transpose(ps[:, H, k * P:(k + 1) * P], h[:, k * P:(k + 1) * P], core.c("ident"))
                        last.then_inc(h_turned, 1)
                        pe.wait_ge(hT_ready, 2 * i + (r + 1))
                        pe.wait_ge(down_in[r], i * 16 + 16)
                        pe.wait_ge(y_low, 2 * i + (r + 1))
                        pe.wait_ge(y_high, 2 * i + (r + 1))
                        for half in range(2):
                            for k in range(KF):
                                last = pe.matmul(ps[:, Y + half, :], hT[:, k, :], wd[:, r, k, half * HALF:(half + 1) * HALF], start=k == 0, stop=k == KF - 1)
                        last.then_inc(y_sum, 1)

            @block.scalar
            def _(act):
                def move_x(r):
                    return act.activation(xT[:, r, 4:8, :].rearrange("p k c -> p (k c)"), ps[:, X_HIGH, :], ACT.Copy)

                act.sem_inc(silu_done, 1)
                act.sem_inc(y_high, 1)
                act.wait_ge(x_turned, 1)
                move_x(0).then_inc(x_high, 1)
                with act.Fori(0, E // 2) as i:
                    for r in range(2):
                        act.wait_ge(g_sum, 2 * i + (r + 1))
                        act.wait_ge(h_ready, 2 * i + (r + 1))
                        act.activation(sg[:, :], ps[:, G, :], ACT.Silu).then_inc(silu_done, 1)
                        act.wait_ge(x_turned, 2 * i + (r + 2))
                        move_x(1 - r).then_inc(x_high, 1)
                        act.wait_ge(h_turned, 2 * i + (r + 1))
                        act.activation(hT[:, :, :].rearrange("p k c -> p (k c)"), ps[:, H, :], ACT.Copy).then_inc(hT_ready, 1)
                        act.wait_ge(y_sum, 2 * i + (r + 1))
                        act.wait_ge(y_free, 2 * i + (r + 1))
                        act.activation(ys[:, r, HALF:D], ps[:, Y + 1, :], ACT.Copy).then_inc(y_high, 1)

            @block.vector
            def _(dve):
                def move_x(r):
                    return dve.tensor_copy(xT[:, r, 0:4, :].rearrange("p k c -> p (k c)"), ps[:, X_LOW, :])

                dve.sem_inc(h_ready, 1)
                dve.sem_inc(y_low, 1)
                dve.wait_ge(x_turned, 1)
                move_x(0).then_inc(x_low, 1)
                with dve.Fori(0, E // 2) as i:
                    for r in range(2):
                        dve.wait_ge(u_sum, 2 * i + (r + 1))
                        dve.wait_ge(silu_done, 2 * i + (r + 2))
                        dve.tensor_tensor(h[:, :], sg[:, :], ps[:, U, :], ALU.mult).then_inc(h_ready, 1)
                        dve.wait_ge(x_turned, 2 * i + (r + 2))
                        move_x(1 - r).then_inc(x_low, 1)
                        dve.wait_ge(y_sum, 2 * i + (r + 1))
                        dve.wait_ge(y_free, 2 * i + (r + 1))
                        dve.tensor_copy(ys[:, r, 0:HALF], ps[:, Y, :]).then_inc(y_low, 1)


def experts_beyond(core, layer, nt, h_rows, y_rows, index, beyond, wg, wu, wd, gate_src, up_src, down_src):
    nc, ps = core.nc, core.ps
    with ExitStack() as held:
        sb = lambda name, shape, dt=F32: held.enter_context(nc.sbuf_tensor(f"{name}_b{layer}", shape, dt))
        lanes = sb("lanes", [P, 2], I32)
        number = sb("number", [P, 2], I32)
        xs = sb("x_rows", [P, D])
        xT = sb("x_turned", [P, KD, P])
        sg = sb("silu_gate", [P, F])
        h = sb("hidden", [P, F])
        hT = sb("hidden_turned", [P, KF, P])
        ys = sb("y_out_rows", [P, D])
        left = nc.values_load(beyond[0:1, 0:1], min_val=0, max_val=2 * nt)
        with nc.Fori(0, 2 * nt) as b:
            with nc.If(left > b):
                with signals(nc, "lanes_set x_in w_in x_turned x_moved gu_sum silu_done h_ready h_turned hT_ready y_sum y_ready y_out", core.soft) as (
                        lanes_set, x_in, w_in, x_turned, x_moved, gu_sum, silu_done, h_ready, h_turned, hT_ready, y_sum, y_ready, y_out):
                    with nc.Block() as block:
                        @block.sync
                        def _(sp):
                            e = sp.value_load(beyond[0:1, bass.ds(b + 1, 1)], min_val=0, max_val=E - 1)
                            sp.dma_start(wg[:, 0, :, :], gate_src[bass.ds(e, 1)].rearrange("a p k f -> p (a k) f")).then_inc(w_in, 16)
                            sp.dma_start(wu[:, 0, :, :], up_src[bass.ds(e, 1)].rearrange("a p k f -> p (a k) f")).then_inc(w_in, 16)
                            sp.dma_start(wd[:, 0, :, :], down_src[bass.ds(e, 1)].rearrange("a p k f -> p (a k) f")).then_inc(w_in, 16)

                        @block.gpsimd
                        def _(pool):
                            pool.tensor_copy(lanes[:, :], index[:, bass.ds(b + E, 1), :].rearrange("p a c -> p (a c)")).then_inc(lanes_set, 1)
                            pool.wait_ge(lanes_set, 1)
                            pool.indirect_dma_start(xs[:, :], None, h_rows, bass.IndirectOffsetOnAxis(ap=lanes[:, 0:1].bitcast(U32), axis=0)).then_inc(x_in, 16)
                            pool.wait_ge(y_ready, 2)
                            pool.indirect_dma_start(y_rows, bass.IndirectOffsetOnAxis(ap=lanes[:, 1:2].bitcast(U32), axis=0), ys[:, :], None).then_inc(y_out, 16)
                            pool.wait_ge(y_out, 16)

                        @block.tensor
                        def _(pe):
                            pe.wait_ge(x_in, 16)
                            for k in range(KD):
                                last = pe.transpose(ps[:, k // 4, (k % 4) * P:(k % 4 + 1) * P], xs[:, k * P:(k + 1) * P], core.c("ident"))
                            last.then_inc(x_turned, 1)
                            pe.wait_ge(x_moved, 2)
                            pe.wait_ge(w_in, 48)
                            for w, bank in ((wg, 2), (wu, 3)):
                                for k in range(KD):
                                    last = pe.matmul(ps[:, bank, :], xT[:, k, :], w[:, 0, k, :], start=k == 0, stop=k == KD - 1)
                            last.then_inc(gu_sum, 1)
                            pe.wait_ge(h_ready, 1)
                            for k in range(KF):
                                last = pe.transpose(ps[:, 4, k * P:(k + 1) * P], h[:, k * P:(k + 1) * P], core.c("ident"))
                            last.then_inc(h_turned, 1)
                            pe.wait_ge(hT_ready, 1)
                            for half in range(2):
                                for k in range(KF):
                                    last = pe.matmul(ps[:, 5 + half, :], hT[:, k, :], wd[:, 0, k, half * HALF:(half + 1) * HALF], start=k == 0, stop=k == KF - 1)
                            last.then_inc(y_sum, 1)

                        @block.scalar
                        def _(act):
                            act.wait_ge(gu_sum, 1)
                            act.activation(sg[:, :], ps[:, 2, :], ACT.Silu).then_inc(silu_done, 1)

                        @block.vector
                        def _(dve):
                            dve.wait_ge(x_turned, 1)
                            for half in range(2):
                                dve.tensor_copy(xT[:, 4 * half:4 * half + 4, :].rearrange("p k c -> p (k c)"), ps[:, half, :]).then_inc(x_moved, 1)
                            dve.wait_ge(silu_done, 1)
                            dve.tensor_tensor(h[:, :], sg[:, :], ps[:, 3, :], ALU.mult).then_inc(h_ready, 1)
                            dve.wait_ge(h_turned, 1)
                            dve.tensor_copy(hT[:, :, :].rearrange("p k c -> p (k c)"), ps[:, 4, :]).then_inc(hT_ready, 1)
                            dve.wait_ge(y_sum, 1)
                            for half in range(2):
                                dve.tensor_copy(ys[:, half * HALF:(half + 1) * HALF], ps[:, 5 + half, :]).then_inc(y_ready, 1)


def combine(core, layer, nt, y_rows, weights):
    nc = core.nc
    tl = nt * P
    with ExitStack() as held:
        sb = lambda name, shape, dt=F32: held.enter_context(nc.sbuf_tensor(f"{name}_{layer}", shape, dt))
        y = sb("y_back", [P, 2, 2, D])
        gt = sb("gate_spread", [P, 2, D])
        s = held.enter_context(signals(nc, "gate_rows_in y_in0 y_in1 y_added dve_chain"))
        gate_rows_in, y_in0, y_in1, y_added, chain_s = s
        y_in = [y_in0, y_in1]
        with nc.Block() as block:
            @block.sync
            def _(sp):
                for st in range(2):
                    ap, at = mod_row(core, layer, st, 5)
                    sp.dma_start(gt[:, st, :], rows(ap, at, D)).then_inc(gate_rows_in, 16)
                for t in range(nt):
                    if t >= 2:
                        sp.wait_ge(y_added, t - 1)
                    sp.dma_start(y[:, t % 2, :, :], y_rows[0:2 * tl, :].rearrange("(c t p) d -> t p c d", c=2, p=P)[t]).then_inc(y_in[t % 2], 16)

            @block.vector
            def _(dve):
                do = Chain(dve, chain_s)
                dve.wait_ge(gate_rows_in, 32)
                for t in range(nt):
                    dve.wait_ge(y_in[t % 2], 16 * (t // 2 + 1))
                    y1, y2 = y[:, t % 2, 0, :], y[:, t % 2, 1, :]
                    do(dve.tensor_scalar(y1, y1, weights[:, 0, t:t + 1], None, ALU.mult))
                    do(dve.scalar_tensor_tensor(y1, y2, weights[:, 1, t:t + 1], y1, ALU.mult, ALU.add))
                    do(dve.tensor_tensor(y1, y1, gt[:, int(t >= NT), :], ALU.mult))
                    dve.tensor_tensor(core.x[:, t, :], core.x[:, t, :], y1, ALU.add).then_inc(y_added, 1)


DIRS = 2
LORA = 64
GLORA = 160
GRID_W = 64
GRID_H = T // GRID_W
CHUNKS = TA // CHUNK
LEVELS = 6
PARAMS = ("mu0", "mu1", "mu2", "mu3", "mu4", "mu5", "w0_0", "w0_1", "a0_0", "a0_1", "k_k", "k_a", "r_k", "one_less_k_a")
SQRT_E = float(np.exp(-0.5))


class Turns:

    def __init__(self, names):
        self.names, self.done = names, 0

    def of(self, name, rnd):
        return rnd * len(self.names) + self.names.index(name) + 1

    def mark(self, ins, sem, name):
        assert self.names[self.done % len(self.names)] == name, (name, self.names[self.done % len(self.names)])
        self.done += 1
        ins.then_inc(sem, 1)


def rwkv(core, layer):
    nc, ins = core.nc, core.ins
    with ExitStack() as held:
        sb = lambda name, shape, dt=F32: held.enter_context(nc.sbuf_tensor(name, shape, dt))
        dram = lambda name, shape: nc.dram_tensor(name, shape, F32, kind="Internal").ap()
        r_dram, k_dram = dram("r_channels", [KD, P, TA]), dram("k_channels", [KD, P, TA])
        v_dram, y_dram = dram("v_rows", [TA, D]), dram("y_rows_rwkv", [T, D])
        params = sb("channel_params", [P, len(PARAMS), KD])
        tw = sb("decay_lora", [P, TA])
        ta = sb("a_lora", [P, TA])
        tg = sb("gate_lora", [P, T])
        tg2 = sb("gate_lora_rest", [GLORA - P, T])
        bonus = sb("bonus", [P, NT, 2 * KD])
        with nc.sbuf_tensor("h_turned_rwkv", [P, KD, TA], F32) as hT:
            norm_turn(core, list(range(NTA)), [mod_row(core, layer, t >= NT, 1) for t in range(NTA)],
                      [mod_row(core, layer, t >= NT, 0) for t in range(NTA)], 1e-6, hT)
            projections(core, hT, params, tw, ta, tg, tg2, r_dram, k_dram, v_dram)
        recurrence(core, params, tw, ta, bonus, r_dram, k_dram, v_dram, y_dram)
        rwkv_out(core, layer, tg, tg2, bonus, v_dram, y_dram)


def projections(core, hT, params, tw, ta, tg, tg2, r_dram, k_dram, v_dram):
    nc, ins = core.nc, core.ins
    ps = core.ps
    HT2 = TA // 2
    with ExitStack() as held:
        sb = lambda name, shape, dt=F32: held.enter_context(nc.sbuf_tensor(name, shape, dt))
        xx = sb("shift_minus_h", [P, KD, TA])
        mix = sb("mixed", [P, 2, KD, TA])
        wring = sb("proj_weights", [P, 2, KD, HALF])
        stage = sb("proj_out", [P, 4, HALF])
        w1 = sb("lora_w1", [P, KD, P])
        a1 = sb("lora_a1", [P, KD, P])
        g1 = sb("lora_g1", [P, KD, GLORA])
        s = held.enter_context(signals(nc, "params_in small_in w_in0 w_in1 xx_ready mix_ready lora_sum lora_done product moved stored0 stored1 stored2 stored3 dve_chain", core.soft))
        params_in, small_in, w_in0, w_in1, xx_ready, mix_ready, lora_sum, lora_done, product, moved, st0, st1, st2, st3, chain_s = s
        w_in, stored = [w_in0, w_in1], [st0, st1, st2, st3]
        WIDE = [("rw_wv", 0), ("rw_wv", 1), ("rw_wr", 0), ("rw_wr", 1), ("rw_wk", 0), ("rw_wk", 1)]
        MIXES = [1, 4, 5, 3, 0, 2]
        SUMS = [("v", n, t, 0) for n in range(2) for t in range(NTA)]
        for kind, first in (("r", 2), ("k", 4)):
            SUMS += [(kind, first + n, m, half) for n in range(2) for m in range(4) for half in range(2)]

        with nc.Block() as block:
            @block.gpsimd
            def _(pool):
                with nc.allow_non_contiguous_dma(reason="vectors laid out by channel on partitions"):
                    col = lambda ap: ap.rearrange("a (k p) -> p a k", p=P)
                    pool.dma_start(params[:, 0:6, :], col(ins["rw_mu"][0])).then_inc(params_in, 16)
                    pool.dma_start(params[:, 6:8, :], col(ins["rw_w0"][0])).then_inc(params_in, 16)
                    pool.dma_start(params[:, 8:10, :], col(ins["rw_a0"][0])).then_inc(params_in, 16)
                    pool.dma_start(params[:, 10:11, :], col(ins["rw_k_k"])).then_inc(params_in, 16)
                    pool.dma_start(params[:, 11:12, :], col(ins["rw_k_a"])).then_inc(params_in, 16)
                    pool.dma_start(params[:, 12:13, :], col(ins["rw_r_k"].rearrange("a h k -> a (h k)"))).then_inc(params_in, 16)
                pool.wait_ge(params_in, 96)

            @block.sync
            def _(sp):
                for z in range(DIRS):
                    sp.dma_start(w1[:, :, z * LORA:(z + 1) * LORA], ins["rw_w1"][0, z].rearrange("(k p) r -> p k r", p=P)).then_inc(small_in, 16)
                    sp.dma_start(a1[:, :, z * LORA:(z + 1) * LORA], ins["rw_a1"][0, z].rearrange("(k p) r -> p k r", p=P)).then_inc(small_in, 16)
                sp.dma_start(g1[:, :, :], ins["rw_g1"][0].rearrange("(k p) r -> p k r", p=P)).then_inc(small_in, 16)
                ends = [max(i for i, g in enumerate(SUMS) if g[1] == n) + 1 for n in range(len(WIDE))]
                for n, (name, half) in enumerate(WIDE):
                    if n >= 2:
                        sp.wait_ge(product, ends[n - 2])
                    sp.dma_start(wring[:, n % 2, :, :], ins[name][0].rearrange("(k p) n -> p k n", p=P)[:, :, half * HALF:(half + 1) * HALF]).then_inc(w_in[n % 2], 16)

            @block.scalar
            def _(act):
                for n, dst in enumerate((tw, ta)):
                    for half in range(2):
                        act.wait_ge(lora_sum, 2 * n + half + 1)
                        act.activation(dst[:, half * HT2:(half + 1) * HT2], ps[:, 2 * n + half, 0:HT2], (ACT.Tanh, ACT.Copy)[n]).then_inc(lora_done, 1)
                act.wait_ge(lora_sum, 6)
                act.activation(tg[:, :], ps[:, 4, :], ACT.Sigmoid).then_inc(lora_done, 1)
                act.activation(tg2[:, :], ps[0:GLORA - P, 5, :], ACT.Sigmoid).then_inc(lora_done, 1)
                for i, (kind, n, m, half) in enumerate(SUMS):
                    act.wait_ge(product, i + 1)
                    if i >= 4:
                        act.wait_ge(stored[i % 4], 16 * (i // 4))
                    width = HALF if kind == "v" else HT2
                    act.activation(stage[:, i % 4, 0:width], ps[:, i % 8, 0:width], ACT.Copy).then_inc(moved, 1)
                    act.wait_ge(moved, i + 1)
                    if kind == "v":
                        dst = v_dram[m * P:(m + 1) * P, n * HALF:(n + 1) * HALF]
                    else:
                        dst = (r_dram if kind == "r" else k_dram)[(n % 2) * 4 + m, :, half * HT2:(half + 1) * HT2]
                    act.dma_start(dst, stage[:, i % 4, 0:width]).then_inc(stored[i % 4], 16)
                for q in range(4):
                    act.wait_ge(stored[q], 16 * len(SUMS[q::4]))

            @block.vector
            def _(dve):
                do = Chain(dve, chain_s)
                do(dve.tensor_scalar(xx[:, :, :], hT[:, :, :], -1.0, None, ALU.mult))
                grid = lambda ap, k0: ap[:, k0:k0 + 2, 0:T].rearrange("p k (h w) -> p k h w", w=GRID_W)

                def add(dst, src):
                    return dve.tensor_tensor(dst, dst, src, ALU.add)

                for k in range(2):
                    one = lambda ap, k0: ap[:, k0 + k, 0:T].rearrange("p (h w) -> p h w", w=GRID_W)
                    add(one(xx, 0)[:, :, 1:], one(hT, 0)[:, :, :-1])
                    add(one(xx, 2)[:, :, :-1], one(hT, 2)[:, :, 1:])
                add(xx[:, 4:6, GRID_W:T], hT[:, 4:6, 0:T - GRID_W])
                add(xx[:, 6:8, 0:T - GRID_W], hT[:, 6:8, GRID_W:T])
                add(xx[:, 0:4, T + 1:TA], hT[:, 0:4, T:TA - 1])
                do(add(xx[:, 4:8, T:TA - 1], hT[:, 4:8, T + 1:TA]))
                dve.wait_ge(params_in, 96)
                dve.tensor_scalar(params[:, 13, :], params[:, 11, :], -1.0, 1.0, ALU.mult, ALU.add)
                for n, mu in enumerate(MIXES):
                    if n == 2:
                        dve.wait_ge(lora_sum, 2)
                    if n == 3:
                        dve.wait_ge(lora_sum, 4)
                    if n == 4:
                        dve.wait_ge(lora_sum, 6)
                    if n == 5:
                        dve.wait_ge(product, 2 * NTA)
                    for k in range(KD):
                        dve.scalar_tensor_tensor(mix[:, n % 2, k, :], xx[:, k, :], params[:, mu, k:k + 1], hT[:, k, :],
                                                 ALU.mult, ALU.add).then_inc(mix_ready, 1)

            @block.tensor
            def _(pe):
                pe.wait_ge(small_in, 80)
                for n, w in enumerate((w1, a1)):
                    pe.wait_ge(mix_ready, KD * (n + 1))
                    for half in range(2):
                        for k in range(KD):
                            last = pe.matmul(ps[:, 2 * n + half, 0:HT2], w[:, k, :], mix[:, n % 2, k, half * HT2:(half + 1) * HT2], start=k == 0, stop=k == KD - 1)
                        last.then_inc(lora_sum, 1)
                pe.wait_ge(mix_ready, KD * 3)
                for bank, cols in ((4, slice(0, P)), (5, slice(P, GLORA))):
                    n = cols.stop - cols.start
                    for k in range(KD):
                        last = pe.matmul(ps[0:n, bank, :], g1[:, k, cols], mix[:, 0, k, 0:T], start=k == 0, stop=k == KD - 1)
                    last.then_inc(lora_sum, 1)
                pe.wait_ge(lora_done, 6)
                for i, (kind, n, m, half) in enumerate(SUMS):
                    j = {"v": 3, "r": 4, "k": 5}[kind]
                    pe.wait_ge(mix_ready, KD * (j + 1))
                    pe.wait_ge(w_in[n % 2], 16 * (n // 2 + 1))
                    if i >= 8:
                        pe.wait_ge(moved, i - 7)
                    for k in range(KD):
                        if kind == "v":
                            last = pe.matmul(ps[:, i % 8, :], mix[:, 1, k, m * P:(m + 1) * P], wring[:, n % 2, k, :], start=k == 0, stop=k == KD - 1)
                        else:
                            last = pe.matmul(ps[:, i % 8, 0:HT2], wring[:, n % 2, k, m * P:(m + 1) * P], mix[:, j % 2, k, half * HT2:(half + 1) * HT2],
                                             start=k == 0, stop=k == KD - 1)
                    last.then_inc(product, 1)


def recurrence(core, params, tw, ta, bonus, r_dram, k_dram, v_dram, y_dram):
    nc, ins = core.nc, core.ins
    with ExitStack() as held:
        sb = lambda name, shape, dt=F32: held.enter_context(nc.sbuf_tensor(name, shape, dt))
        con = sb("scan_masks", [P, SCAN_CONST.shape[1]])
        b = {
            "AR": sb("a_and_r", [P, DIRS, NTA, 2, P]),
            "B": sb("b_scaled", [P, DIRS, TA]), "K": sb("k_scaled", [P, DIRS, TA]),
            "Bt": sb("b_to_end", [P, DIRS, TA]), "Kt": sb("k_to_end", [P, DIRS, TA]),
            "V": sb("v_tokens_two_heads", [P, NTA, P]),
            "F": sb("state_factor", [P, DIRS, CHUNKS, P]), "G": sb("state_addend", [P, DIRS, CHUNKS, P]),
            "Q": sb("state_reader", [P, DIRS, T]),
            "Y": sb("y_two_heads", [P, NT, P]),
        }
        c_ = lambda name, n=1: con[:, SCAN_WHERE[name][0]:SCAN_WHERE[name][0] + n * SCAN_WHERE[name][1]]
        with signals(nc, "scan_const_in") as (const_in,):
            with nc.Block() as block:
                @block.sync
                def _(sp):
                    sp.dma_start(con[:, :], ins["scan_const"]).then_inc(const_in, 16)
                    sp.wait_ge(const_in, 16)
        with nc.Fori(0, KD) as c:
            prepare(core, c, c_, b, params, tw, ta, bonus, r_dram, k_dram, v_dram)
            chunk_matrices(core, c_, b)
            scan(core, c, b, y_dram)


def prepare(core, c, c_, b, params, tw, ta, bonus, r_dram, k_dram, v_dram):
    nc, ins = core.nc, core.ins
    ps = core.ps
    H2 = TA // 2
    with ExitStack() as held:
        sb = lambda name, shape, dt=F32: held.enter_context(nc.sbuf_tensor(name, shape, dt))
        r, k = sb("r_two_heads", [P, TA]), sb("k_two_heads", [P, TA])
        w2, a2 = sb("lora_w2", [P, P]), sb("lora_a2", [P, P])
        pc = sb("params_here", [P, len(PARAMS)])
        kk, kk2, norm = sb("kk", [P, TA]), sb("kk_squared", [P, TA]), sb("kk_norm", [P, TA])
        lg, a = sb("log_decay", [P, DIRS, TA]), sb("a_gate", [P, DIRS, TA])
        cum, before = sb("log_decay_sum", [P, TA]), sb("log_decay_before", [P, TA])
        tot = sb("log_decay_whole", [P, CHUNKS])
        e_cum, e_neg, e_bef = sb("exp_cum", [P, TA]), sb("exp_minus_cum", [P, TA]), sb("exp_before", [P, TA])
        e_tot = sb("exp_whole", [P, DIRS, CHUNKS])
        tmp, km, kms = sb("tmp_two_heads", [P, TA]), sb("k_mod", [P, TA]), sb("k_mod_sum", [P, TA])
        s = held.enter_context(signals(nc, "rk_in lora_in v_in lora_sum sig_done kk_ready norm_sum norm_sq norm_root dve_chain cum_ready exps_done exps_used bk_ready ends_ready prod_ready bonus_sum bonus_out pool_chain"))
        rk_in, lora_in, v_in, lora_sum, sig_done, kk_ready, norm_sum, norm_sq, norm_root, chain_s, cum_ready, exps_done, exps_used, bk_ready, ends_ready, prod_ready, bonus_sum, bonus_out, pool_s = s
        by_chunk = lambda ap: ap.rearrange("p (c t) -> p c t", t=CHUNK)
        spread = lambda ap: ap.unsqueeze(2).to_broadcast([P, CHUNKS, CHUNK])
        with nc.Block() as block:
            @block.sync
            def _(sp):
                sp.dma_start(r[:, :], r_dram[bass.ds(c, 1)].rearrange("a p t -> p (a t)")).then_inc(rk_in, 16)
                sp.dma_start(k[:, :], k_dram[bass.ds(c, 1)].rearrange("a p t -> p (a t)")).then_inc(rk_in, 16)
                sp.dma_start(w2[:, :], ins["rw_w2"][0].rearrange("z r d -> (z r) d")[:, bass.ds(c * P, P)]).then_inc(lora_in, 16)
                sp.dma_start(a2[:, :], ins["rw_a2"][0].rearrange("z r d -> (z r) d")[:, bass.ds(c * P, P)]).then_inc(lora_in, 16)
                sp.dma_start(b["V"][:, :, :], v_dram.rearrange("(t p) d -> p t d", p=P)[:, :, bass.ds(c * P, P)]).then_inc(v_in, 16)
                sp.wait_ge(v_in, 16)

            @block.tensor
            def _(pe):
                pe.wait_ge(lora_in, 32)
                for n, (w, src) in enumerate(((w2, tw), (a2, ta))):
                    for z in range(DIRS):
                        part = slice(z * LORA, (z + 1) * LORA)
                        for half in range(2):
                            pe.matmul(ps[:, 4 * n + 2 * z + half, 0:H2], w[part, :], src[part, half * H2:(half + 1) * H2], start=True, stop=True).then_inc(lora_sum, 1)
                pe.wait_ge(kk_ready, 1)
                pe.wait_ge(sig_done, 2)
                for half in range(2):
                    last = pe.matmul(ps[:, half, 0:H2], c_("head_ones"), kk2[:, half * H2:(half + 1) * H2], start=True, stop=True)
                last.then_inc(norm_sum, 1)
                pe.wait_ge(prod_ready, 1)
                pe.wait_ge(sig_done, 8)
                for t in range(NT):
                    last = pe.matmul(ps[:, 2, 2 * t:2 * t + 2], kk2[:, t * P:(t + 1) * P], c_("head_pick"), start=True, stop=True)
                last.then_inc(bonus_sum, 1)

            @block.scalar
            def _(act):
                act.wait_ge(cum_ready, 1)
                for n, (dst, at) in enumerate(((lg, 6), (a, 8))):
                    for z in range(DIRS):
                        for half in range(2):
                            act.wait_ge(lora_sum, 4 * n + 2 * z + half + 1)
                            act.activation(dst[:, z, half * H2:(half + 1) * H2], ps[:, 4 * n + 2 * z + half, 0:H2], ACT.Sigmoid,
                                           bias=pc[:, at + z:at + z + 1]).then_inc(sig_done, 1)
                act.wait_ge(norm_sq, 1)
                act.activation(norm[:, :], norm[:, :], ACT.Sqrt).then_inc(norm_root, 1)
                for z in range(DIRS):
                    act.wait_ge(cum_ready, z + 2)
                    if z:
                        act.wait_ge(exps_used, 1)
                    act.activation(e_cum[:, :], cum[:, :], ACT.Exp)
                    act.activation(e_neg[:, :], cum[:, :], ACT.Exp, scale=-1.0)
                    act.activation(e_tot[:, z, :], tot[:, :], ACT.Exp)
                    act.activation(e_bef[:, :], before[:, :], ACT.Exp).then_inc(exps_done, 1)

            @block.vector
            def _(dve):
                do = Chain(dve, chain_s)
                do(dve.tensor_copy(pc[:, :], params[:, :, bass.ds(c, 1)].rearrange("p n a -> p (n a)")))
                dve.sem_inc(cum_ready, 1)
                col = lambda name: pc[:, PARAMS.index(name):PARAMS.index(name) + 1]
                dve.wait_ge(rk_in, 32)
                do(dve.tensor_scalar(kk[:, :], k[:, :], col("k_k"), None, ALU.mult))
                do(dve.tensor_tensor(kk2[:, :], kk[:, :], kk[:, :], ALU.mult))
                dve.sem_inc(kk_ready, 1)
                dve.wait_ge(norm_sum, 1)
                do(dve.tensor_scalar(norm[:, :].rearrange("p (h t) -> p h t", h=2), ps[:, 0:2, 0:H2], 1e-12, None, ALU.add))
                dve.sem_inc(norm_sq, 1)
                dve.wait_ge(norm_root, 1)
                do(dve.reciprocal(norm[:, :], norm[:, :]))
                do(dve.tensor_tensor(kk[:, :], kk[:, :], norm[:, :], ALU.mult))
                for z in range(DIRS):
                    L = lg[:, z, :]
                    dve.wait_ge(sig_done, 2 * z + 2)
                    do(dve.tensor_scalar(L, L, -SQRT_E, None, ALU.mult))
                    do(dve.tensor_tensor_scan(cum[:, :], c_("scan_keep"), L, 0.0, ALU.mult, ALU.add))
                    do(dve.tensor_copy(tot[:, :], by_chunk(cum[:, :])[:, :, CHUNK - 1]))
                    if z:
                        do(dve.tensor_tensor(cum[:, :], L, cum[:, :], ALU.subtract))
                        do(dve.tensor_tensor(by_chunk(cum[:, :]), by_chunk(cum[:, :]), spread(tot[:, :]), ALU.add))
                    do(dve.tensor_tensor(before[:, :], cum[:, :], L, ALU.subtract))
                    dve.sem_inc(cum_ready, 1)
                    dve.wait_ge(sig_done, 4 + 2 * z + 2)
                    do(dve.tensor_scalar(tmp[:, :], a[:, z, :], col("k_a"), col("one_less_k_a"), ALU.mult, ALU.add))
                    do(dve.tensor_tensor(km[:, :], k[:, :], tmp[:, :], ALU.mult))
                    if z == 0:
                        do(dve.tensor_copy(kms[:, :], km[:, :]))
                    else:
                        do(dve.tensor_tensor(kms[:, :], kms[:, :], km[:, :], ALU.add))
                    do(dve.tensor_tensor(tmp[:, :], kk[:, :], a[:, z, :], ALU.mult))
                    dve.wait_ge(exps_done, z + 1)
                    ar = b["AR"][:, z, :, :, :]
                    tiles = lambda ap: ap.rearrange("p (t c) -> p t c", c=P)
                    dve.tensor_tensor(b["B"][:, z, :], tmp[:, :], e_neg[:, :], ALU.mult)
                    do(dve.tensor_tensor(b["K"][:, z, :], km[:, :], e_neg[:, :], ALU.mult))
                    dve.sem_inc(bk_ready, 1)
                    dve.scalar_tensor_tensor(ar[:, :, 0, :], tiles(kk[:, :]), -1.0, tiles(e_bef[:, :]), ALU.mult, ALU.mult)
                    do(dve.tensor_tensor(ar[:, :, 1, :], tiles(r[:, :]), tiles(e_cum[:, :]), ALU.mult))
                    dve.sem_inc(exps_used, 1)
                do(dve.scalar_tensor_tensor(kk2[:, :], kms[:, :], col("r_k"), r[:, :], ALU.mult, ALU.mult))
                dve.sem_inc(prod_ready, 1)
                dve.wait_ge(bonus_sum, 1)
                do(dve.tensor_copy(bonus[:, :, bass.ds(c * 2, 2)], ps[:, 2, 0:2 * NT].rearrange("p (t h) -> p t h", h=2)))

            @block.gpsimd
            def _(pool):
                do = Chain(pool, pool_s)
                for z in range(DIRS):
                    pool.wait_ge(bk_ready, z + 1)
                    for src, dst in (("B", "Bt"), ("K", "Kt")):
                        pool.tensor_tensor(by_chunk(b[dst][:, z, :]), by_chunk(b[src][:, z, :]), spread(e_tot[:, z, :]), ALU.mult)
                    do(pool.tensor_tensor(b["F"][:, z, :, :], core.c("ident").unsqueeze(1).to_broadcast([P, CHUNKS, P]),
                                          e_tot[:, z, :].unsqueeze(2).to_broadcast([P, CHUNKS, P]), ALU.mult))


def chunk_matrices(core, c_, b):
    nc, ps = core.nc, core.ps
    PAIRS = [(4, 5), (0, 1), (2, 3)]
    with ExitStack() as held:
        sb = lambda name, shape, dt=F32: held.enter_context(nc.sbuf_tensor(name, shape, dt))
        two = lambda name, shape: [sb(f"{name}{h}", shape) for h in range(2)]
        LR, MR = two("l_and_rb", [P, 4, 2, P]), two("m_and_rk", [P, 4, 2, P])
        LQ = two("l_quarters", [P, LEVELS - 1, 4, P])
        X, XT, Z = two("inverse", [P, 4, P]), two("inverse_turned", [P, 4, P]), two("step", [P, 4, P])
        AM = two("a_and_mv", [P, 4, 2, 64])
        WU = sb("w_and_u", [P, 4, 2, 2, 64])
        Bk, Kk = sb("b_tokens", [P, 4, P]), sb("k_tokens", [P, 4, P])
        fm = sb("factor_masked", [P, 4, P])
        lv = range(1, LEVELS)
        PE = Turns(["P1_0", "P1_1", "P2_0", "P2_1", "X0_0", "X0_1", "TA", "TB", "MV_0", "MV_1"]
                   + [f"{x}{n}_{h}" for n in lv for x in ("Z", "XT", "X") for h in range(2) if not (x == "X" and n == LEVELS - 1)]
                   + ["TK", "WU_0", "WU_1", "YC_0", "YC_1", "Q", "F", "G"])
        DVE = Turns(["LR_0", "LR_1", "MR_0", "MR_1"]
                    + [f"{x}{n}_{h}" for n in lv for x in ("XT", "X") for h in range(2) if not (x == "X" and n == LEVELS - 1)]
                    + ["Q", "F", "G"])
        ACTS = Turns(["X0_0", "X0_1", "TA", "TB", "MV_0", "MV_1"] + [f"Z{n}_{h}" for n in lv for h in range(2)]
                     + ["TK", "WU_0", "WU_1", "YC_0", "YC_1"])
        POOL = Turns(["XT0_0", "XT0_1"] + [f"LQ{n}_{h}" for n in lv for h in range(2)])
        s = held.enter_context(signals(nc, "products by_dve by_act by_pool dve_chain pool_chain"))
        products, by_dve, by_act, by_pool, chain_s, pool_s = s
        units = [(z, ti) for z in range(DIRS) for ti in range(2)]
        with nc.Block() as block:
            @block.tensor
            def _(pe):
                for rnd, pair in enumerate(PAIRS):
                    lat = pair[0] < NT
                    tok = lambda ti: slice(pair[ti] * P, (pair[ti] + 1) * P)
                    wait = lambda sem, order, name, back=0: pe.wait_ge(sem, order.of(name, rnd - back)) if rnd >= back else None
                    row = [slice(0, 64), slice(64, 128)]
                    for h in range(2):
                        if h == 0:
                            wait(by_dve, DVE, "G", 1)
                            wait(by_act, ACTS, "YC_1", 1)
                        for u, (z, ti) in enumerate(units):
                            last = pe.matmul(ps[:, 4 * h + u // 2, (u % 2) * 256:(u % 2) * 256 + 256], b["B"][row[h], z, tok(ti)],
                                             b["AR"][row[h], z, pair[ti], :, :].rearrange("p a c -> p (a c)"), start=True, stop=True)
                        PE.mark(last, products, f"P1_{h}")
                    for h in range(2):
                        for u, (z, ti) in enumerate(units):
                            last = pe.matmul(ps[:, 4 * h + 2 + u // 2, (u % 2) * 256:(u % 2) * 256 + 256], b["K"][row[h], z, tok(ti)],
                                             b["AR"][row[h], z, pair[ti], :, :].rearrange("p a c -> p (a c)"), start=True, stop=True)
                        PE.mark(last, products, f"P2_{h}")
                    for h in range(2):
                        wait(by_pool, POOL, f"XT0_{h}")
                        wait(by_dve, DVE, f"LR_{h}")
                        for u in range(4):
                            last = pe.transpose(ps[:, 4 * h, u * P:(u + 1) * P], XT[h][:, u, :], core.c("ident"))
                        PE.mark(last, products, f"X0_{h}")
                    wait(by_dve, DVE, "MR_1")
                    for name, bank in (("TA", 2), ("TB", 6)):
                        for u, (z, ti) in enumerate(units):
                            src = b["AR"][:, z, pair[ti], 0, :] if name == "TA" else b["Bt"][:, z, tok(ti)]
                            last = pe.transpose(ps[:, bank, u * P:(u + 1) * P], src, core.c("ident"))
                        PE.mark(last, products, name)
                    for h in range(2):
                        wait(by_act, ACTS, ("TA", "TB")[h])
                        for u, (z, ti) in enumerate(units):
                            last = pe.matmul(ps[:, 4 * h + 2, u * 64:(u + 1) * 64], MR[h][:, u, 0, :], b["V"][:, pair[ti], h * 64:(h + 1) * 64], start=True, stop=True)
                        PE.mark(last, products, f"MV_{h}")
                    for n in lv:
                        for h in range(2):
                            if n == 1:
                                wait(by_act, ACTS, f"X0_{h}")
                            else:
                                wait(by_dve, DVE, f"X{n - 1}_{h}")
                            wait(by_pool, POOL, f"LQ{n}_{h}")
                            for u in range(4):
                                last = pe.matmul(ps[:, 4 * h + 1, u * P:(u + 1) * P], LQ[h][:, n - 1, u, :], X[h][:, u, :], start=True, stop=True)
                            PE.mark(last, products, f"Z{n}_{h}")
                        for h in range(2):
                            wait(by_act, ACTS, f"Z{n}_{h}")
                            for u in range(4):
                                last = pe.matmul(ps[:, 4 * h + 3, u * P:(u + 1) * P], Z[h][:, u, :], XT[h][:, u, :], start=True, stop=True)
                            PE.mark(last, products, f"XT{n}_{h}")
                        if n < LEVELS - 1:
                            for h in range(2):
                                for u in range(4):
                                    last = pe.matmul(ps[:, 4 * h, u * P:(u + 1) * P], XT[h][:, u, :], Z[h][:, u, :], start=True, stop=True)
                                PE.mark(last, products, f"X{n}_{h}")
                    wait(by_act, ACTS, "MV_0")
                    for u, (z, ti) in enumerate(units):
                        last = pe.transpose(ps[:, 2, u * P:(u + 1) * P], b["Kt"][:, z, tok(ti)], core.c("ident"))
                    PE.mark(last, products, "TK")
                    for h in range(2):
                        wait(by_dve, DVE, f"XT{LEVELS - 1}_{h}")
                        wait(by_act, ACTS, f"MV_{h}")
                        for u in range(4):
                            last = pe.matmul(ps[:, 4 * h + 1, u * P:(u + 1) * P], XT[h][:, u, :], AM[h][:, u, :, :].rearrange("p a c -> p (a c)"), start=True, stop=True)
                        PE.mark(last, products, f"WU_{h}")
                    for h in range(2):
                        wait(by_act, ACTS, f"WU_{h}")
                        for ti in range(2):
                            for z in range(DIRS):
                                u = z * 2 + ti
                                pe.matmul(ps[:, 4 * h + 3, ti * 64:(ti + 1) * 64], LR[h][:, u, 1, :], WU[:, u, 1, h, :], start=z == 0, stop=False)
                                last = pe.matmul(ps[:, 4 * h + 3, ti * 64:(ti + 1) * 64], MR[h][:, u, 1, :], b["V"][:, pair[ti], h * 64:(h + 1) * 64], start=False, stop=z == 1)
                        PE.mark(last, products, f"YC_{h}")
                    for h in range(2):
                        for u in range(4):
                            last = pe.matmul(ps[64 * h:64 * h + 64, 0, u * P:(u + 1) * P], WU[:, u, 0, h, :], LR[h][:, u, 1, :], start=True, stop=True)
                    PE.mark(last, products, "Q")
                    wait(by_act, ACTS, "YC_1")
                    wait(by_act, ACTS, "TK")
                    for cc in range(2):
                        for u in range(4):
                            last = pe.matmul(ps[:, 3 + 4 * cc, u * P:(u + 1) * P], WU[row[cc], u, 0, :, :].rearrange("p h k -> p (h k)"), Bk[row[cc], u, :], start=True, stop=True)
                    PE.mark(last, products, "F")
                    for cc in range(2):
                        for u, (z, ti) in enumerate(units):
                            pe.matmul(ps[:, 4 + cc, u * P:(u + 1) * P], Bk[row[cc], u, :], WU[row[cc], u, 1, :, :].rearrange("p h k -> p (h k)"), start=True, stop=False)
                            last = pe.matmul(ps[:, 4 + cc, u * P:(u + 1) * P], Kk[row[cc], u, :], b["V"][row[cc], pair[ti], :], start=False, stop=True)
                    PE.mark(last, products, "G")

            @block.vector
            def _(dve):
                do = Chain(dve, chain_s)
                for rnd, pair in enumerate(PAIRS):
                    for name, dst, bank in (("P1", LR, 0), ("P2", MR, 2)):
                        for h in range(2):
                            dve.wait_ge(products, PE.of(f"{name}_{h}", rnd))
                            for z in range(DIRS):
                                last = dve.tensor_tensor(dst[h][:, 2 * z:2 * z + 2, :, :].rearrange("p t a c -> p t (a c)"),
                                                         ps[:, 4 * h + bank + z, :].rearrange("p (t n) -> p t n", t=2),
                                                         c_(f"lt{z}", 2).unsqueeze(1).to_broadcast([P, 2, 256]), ALU.mult)
                            DVE.mark(last, by_dve, ("LR" if name == "P1" else "MR") + f"_{h}")
                    for n in lv:
                        for h in range(2):
                            dve.wait_ge(products, PE.of(f"XT{n}_{h}", rnd))
                            if n < LEVELS - 1:
                                dve.wait_ge(products, PE.of(f"X{n}_{h}", rnd))
                            x = XT[h][:, :, :].rearrange("p u c -> p (u c)")
                            DVE.mark(dve.tensor_tensor(x, ps[:, 4 * h + 3, :], x, ALU.add), by_dve, f"XT{n}_{h}")
                        if n < LEVELS - 1:
                            for h in range(2):
                                x = X[h][:, :, :].rearrange("p u c -> p (u c)")
                                DVE.mark(dve.tensor_tensor(x, ps[:, 4 * h, :], x, ALU.add), by_dve, f"X{n}_{h}")
                    dve.wait_ge(products, PE.of("Q", rnd))
                    if pair[0] < NT:
                        for ti in range(2):
                            t0 = pair[ti] * P
                            last = dve.tensor_tensor(b["Q"][:, :, t0:t0 + P], ps[:, 0, :].rearrange("p (z t c) -> p z t c", z=2, t=2)[:, :, ti, :],
                                                     b["AR"][:, :, pair[ti], 1, :], ALU.add)
                        DVE.mark(last, by_dve, "Q")
                    else:
                        dve.wait_ge(by_dve, DVE.done)
                        DVE.done += 1
                        dve.sem_inc(by_dve, 1)
                    dve.wait_ge(products, PE.of("F", rnd))
                    fold = lambda ap: ap.rearrange("p (z t c) -> p z t c", z=2, t=2)
                    ones4 = c_("head_ones").unsqueeze(1).to_broadcast([P, 4, P])
                    for cc in range(2):
                        do(dve.tensor_tensor(fm[:, :, :], ps[:, 3 + 4 * cc, :].rearrange("p (u c) -> p u c", u=4), ones4, ALU.mult))
                        for z in range(DIRS):
                            at = b["F"][:, z, 2 * pair[0] + cc:2 * pair[1] + cc + 1:2, :]
                            last = dve.tensor_tensor(at, at, fm[:, 2 * z:2 * z + 2, :], ALU.add)
                        if cc == 0:
                            do(last)
                    DVE.mark(last, by_dve, "F")
                    dve.wait_ge(products, PE.of("G", rnd))
                    for cc in range(2):
                        for z in range(DIRS):
                            last = dve.tensor_tensor(b["G"][:, z, 2 * pair[0] + cc:2 * pair[1] + cc + 1:2, :],
                                                     ps[:, 4 + cc, 256 * z:256 * z + 256].rearrange("p (t c) -> p t c", t=2),
                                                     c_("head_ones").unsqueeze(1).to_broadcast([P, 2, P]), ALU.mult)
                    DVE.mark(last, by_dve, "G")

            @block.scalar
            def _(act):
                copy = lambda dst, src: act.activation(dst, src, ACT.Copy)
                for rnd, pair in enumerate(PAIRS):
                    need = lambda name: act.wait_ge(products, PE.of(name, rnd))
                    for h in range(2):
                        need(f"X0_{h}")
                        ACTS.mark(copy(X[h][:, :, :].rearrange("p u c -> p (u c)"), ps[:, 4 * h, :]), by_act, f"X0_{h}")
                    need("TA")
                    for h in range(2):
                        last = copy(AM[h][:, :, 0, :], ps[:, 2, :].rearrange("p (u h c) -> p u h c", u=4, h=2)[:, :, h, :])
                    ACTS.mark(last, by_act, "TA")
                    need("TB")
                    ACTS.mark(copy(Bk[:, :, :].rearrange("p u c -> p (u c)"), ps[:, 6, :]), by_act, "TB")
                    for h in range(2):
                        need(f"MV_{h}")
                        ACTS.mark(copy(AM[h][:, :, 1, :], ps[:, 4 * h + 2, 0:256].rearrange("p (u c) -> p u c", u=4)), by_act, f"MV_{h}")
                    for n in lv:
                        for h in range(2):
                            need(f"Z{n}_{h}")
                            ACTS.mark(copy(Z[h][:, :, :].rearrange("p u c -> p (u c)"), ps[:, 4 * h + 1, :]), by_act, f"Z{n}_{h}")
                    need("TK")
                    ACTS.mark(copy(Kk[:, :, :].rearrange("p u c -> p (u c)"), ps[:, 2, :]), by_act, "TK")
                    for h in range(2):
                        need(f"WU_{h}")
                        ACTS.mark(copy(WU[:, :, :, h, :], ps[:, 4 * h + 1, :].rearrange("p (u a c) -> p u a c", u=4, a=2)), by_act, f"WU_{h}")
                    for h in range(2):
                        need(f"YC_{h}")
                        if pair[0] < NT:
                            ACTS.mark(copy(b["Y"][:, pair[0]:pair[1] + 1, h * 64:(h + 1) * 64], ps[:, 4 * h + 3, 0:P].rearrange("p (t c) -> p t c", t=2)), by_act, f"YC_{h}")
                        else:
                            act.wait_ge(by_act, ACTS.done)
                            ACTS.done += 1
                            act.sem_inc(by_act, 1)

            @block.gpsimd
            def _(pool):
                do = Chain(pool, pool_s)
                pm = lambda n: c_(f"q1_{n}", 2).rearrange("p (z c) -> p z c", z=2)
                four = lambda ap: ap.rearrange("p (z t) c -> p z t c", z=2)
                for rnd, pair in enumerate(PAIRS):
                    for h in range(2):
                        pool.wait_ge(by_dve, DVE.of(f"LR_{h}", rnd))
                        for ti in range(2):
                            last = pool.tensor_tensor(four(XT[h][:, :, :])[:, :, ti, :], four(LR[h][:, :, 0, :])[:, :, ti, :], pm(0), ALU.mult)
                        do(last)
                        POOL.mark(pool.tensor_tensor(XT[h][:, :, :], XT[h][:, :, :], core.c("ident").unsqueeze(1).to_broadcast([P, 4, P]), ALU.add),
                                  by_pool, f"XT0_{h}")
                    for n in lv:
                        for h in range(2):
                            for ti in range(2):
                                last = pool.tensor_tensor(four(LQ[h][:, n - 1, :, :])[:, :, ti, :], four(LR[h][:, :, 0, :])[:, :, ti, :], pm(n), ALU.mult)
                            POOL.mark(last, by_pool, f"LQ{n}_{h}")


def scan(core, c, b, y_dram):
    nc, ps = core.nc, core.ps
    ctx_chunks, lat_chunks = list(range(2 * NT, 2 * NTA)), list(range(2 * NT))
    ORDER = [ctx_chunks + lat_chunks, ctx_chunks[::-1] + lat_chunks[::-1]]
    NC = len(ctx_chunks)
    with ExitStack() as held:
        S = held.enter_context(nc.sbuf_tensor("state", [P, DIRS, P], F32))
        s = held.enter_context(signals(nc, "state_set read0 read1 stepped0 stepped1 state0 state1 y_added stored"))
        state_set, read0, read1, step0, step1, state0, state1, y_added, stored = s
        read, stepped, state = [read0, read1], [step0, step1], [state0, state1]
        with nc.Block() as block:
            @block.tensor
            def _(pe):
                pe.wait_ge(state_set, 1)
                for j in range(CHUNKS):
                    for z in range(DIRS):
                        ch = ORDER[z][j]
                        if j:
                            pe.wait_ge(state[z], j)
                        if j >= NC:
                            if j > NC:
                                pe.wait_ge(y_added, (j - NC - 1) * DIRS + z + 1)
                            lo = 64 * (ch % 2)
                            pe.matmul(ps[lo:lo + 64, z, 0:P], b["Q"][:, z, ch * CHUNK:(ch + 1) * CHUNK], S[:, z, :], start=True, stop=True).then_inc(read[z], 1)
                        if j < CHUNKS - 1:
                            pe.matmul(ps[:, 2 + z, 0:P], b["F"][:, z, ch, :], S[:, z, :], start=True, stop=True).then_inc(stepped[z], 1)

            @block.vector
            def _(dve):
                dve.memset(S[:, :, :], 0.0).then_inc(state_set, 1)
                for j in range(CHUNKS):
                    for z in range(DIRS):
                        ch = ORDER[z][j]
                        if j < CHUNKS - 1:
                            dve.wait_ge(stepped[z], j + 1)
                            dve.tensor_tensor(S[:, z, :], ps[:, 2 + z, 0:P], b["G"][:, z, ch, :], ALU.add).then_inc(state[z], 1)
                        if j >= NC:
                            lo = 64 * (ch % 2)
                            dve.wait_ge(read[z], j - NC + 1)
                            if j > NC or z:
                                dve.wait_ge(y_added, (j - NC) * DIRS + z)
                            at = b["Y"][lo:lo + 64, ch // 2, :]
                            dve.tensor_tensor(at, ps[lo:lo + 64, z, 0:P], at, ALU.add).then_inc(y_added, 1)

            @block.sync
            def _(sp):
                sp.wait_ge(y_added, DIRS * (CHUNKS - NC))
                sp.dma_start(y_dram.rearrange("(t p) d -> p t d", p=P)[:, :, bass.ds(c * P, P)], b["Y"][:, :, :]).then_inc(stored, 16)
                sp.wait_ge(stored, 16)


def rwkv_out(core, layer, tg, tg2, bonus, v_dram, y_dram):
    nc, ins, ps = core.nc, core.ins, core.ps
    HEADS = 2 * KD
    with ExitStack() as held:
        sb = lambda name, shape, dt=F32: held.enter_context(nc.sbuf_tensor(name, shape, dt))
        wo = sb("wo", [P, KD, D])
        g2 = sb("gate_w2", [P, D])
        g2b = sb("gate_w2_rest", [GLORA - P, D])
        spread = sb("head_gain_bias", [P, 3, D])
        y, v = sb("y_here", [P, 2, D]), sb("v_here", [P, 2, D])
        sq = sb("y_squared", [P, D])
        m = sb("head_stats", [P, 4, HEADS])
        yT = sb("y_turned", [P, 2, KD, P])
        s = held.enter_context(signals(nc, "wo_in small_in y_in0 y_in1 gate_sum centred squares var_ready root_ready y_ready y_turned yt_low yt_high out_sum x_added dve_chain"))
        wo_in, small_in, y_in0, y_in1, gate_sum, centred, squares, var_ready, root_ready, y_ready, y_turned, yt_low, yt_high, out_sum, x_added, chain_s = s
        y_in = [y_in0, y_in1]
        heads = lambda ap: ap.rearrange("p (h k) -> p h k", k=64)
        per = lambda ap: ap.unsqueeze(2).to_broadcast([P, HEADS, 64])
        with nc.Block() as block:
            @block.sync
            def _(sp):
                for n, (ap, at) in enumerate(((ins["rw_ln_g"], 0), (ins["rw_ln_b"], 0), mod_row(core, layer, 0, 2))):
                    sp.dma_start(spread[:, n, :], rows(ap, at, D)).then_inc(small_in, 16)
                sp.dma_start(g2[:, :], ins["rw_g2"][0, 0:P, :]).then_inc(small_in, 16)
                sp.dma_start(g2b[:, :], ins["rw_g2"][0, P:GLORA, :]).then_inc(small_in, 16)
                for t in range(NT):
                    if t >= 2:
                        sp.wait_ge(y_turned, 2 * (t - 1))
                        sp.wait_ge(x_added, 2 * (t - 1))
                    sp.dma_start(y[:, t % 2, :], y_dram[t * P:(t + 1) * P, :]).then_inc(y_in[t % 2], 16)
                    sp.dma_start(v[:, t % 2, :], v_dram[t * P:(t + 1) * P, :]).then_inc(y_in[t % 2], 16)
                    if t == 0:
                        sp.dma_start(wo[:, :, :], ins["rw_wo"][0].rearrange("(k p) n -> p k n", p=P)).then_inc(wo_in, 16)

            @block.tensor
            def _(pe):
                pe.wait_ge(small_in, 80)
                for t in range(NT):
                    if t:
                        pe.wait_ge(y_ready, t)
                    for half in range(2):
                        cols = slice(half * HALF, (half + 1) * HALF)
                        pe.matmul(ps[:, half, :], tg[:, t * P:(t + 1) * P], g2[:, cols], start=True, stop=False)
                        last = pe.matmul(ps[:, half, :], tg2[:, t * P:(t + 1) * P], g2b[:, cols], start=False, stop=True)
                    last.then_inc(gate_sum, 1)
                    pe.wait_ge(y_ready, t + 1)
                    if t:
                        pe.wait_ge(yt_low, t)
                        pe.wait_ge(yt_high, t)
                    for half in range(2):
                        for k in range(4):
                            c0 = (half * 4 + k) * P
                            last = pe.transpose(ps[:, 2 + half, k * P:(k + 1) * P], y[:, t % 2, c0:c0 + P], core.c("ident"))
                        last.then_inc(y_turned, 1)
                    pe.wait_ge(yt_low, t + 1)
                    pe.wait_ge(yt_high, t + 1)
                    if t == 0:
                        pe.wait_ge(wo_in, 16)
                    if t >= 2:
                        pe.wait_ge(x_added, 2 * (t - 1))
                    for half in range(2):
                        for k in range(KD):
                            last = pe.matmul(ps[:, 4 + 2 * (t % 2) + half, :], yT[:, t % 2, k, :], wo[:, k, half * HALF:(half + 1) * HALF], start=k == 0, stop=k == KD - 1)
                        last.then_inc(out_sum, 1)

            @block.scalar
            def _(act):
                for t in range(NT):
                    act.wait_ge(centred, t + 1)
                    act.activation(sq[:, :], y[:, t % 2, :], ACT.Square).then_inc(squares, 1)
                    act.wait_ge(var_ready, t + 1)
                    act.activation(m[:, 2, :], m[:, 1, :], ACT.Sqrt).then_inc(root_ready, 1)
                    act.wait_ge(y_turned, 2 * t + 2)
                    act.activation(yT[:, t % 2, 4:8, :].rearrange("p k c -> p (k c)"), ps[:, 3, :], ACT.Copy).then_inc(yt_high, 1)

            @block.vector
            def _(dve):
                do = Chain(dve, chain_s)
                dve.wait_ge(small_in, 80)
                for t in range(NT):
                    Y, V = y[:, t % 2, :], v[:, t % 2, :]
                    dve.wait_ge(y_in[t % 2], 32 * (t // 2 + 1))
                    do(dve.tensor_reduce(m[:, 0, :], heads(Y), AX, ALU.add))
                    do(dve.tensor_scalar(m[:, 0, :], m[:, 0, :], 1.0 / 64, None, ALU.mult))
                    do(dve.tensor_tensor(heads(Y), heads(Y), per(m[:, 0, :]), ALU.subtract))
                    dve.sem_inc(centred, 1)
                    do(dve.tensor_tensor(heads(V), heads(V), per(bonus[:, t, :]), ALU.mult))
                    dve.wait_ge(squares, t + 1)
                    do(dve.tensor_reduce(m[:, 1, :], heads(sq[:, :]), AX, ALU.add))
                    do(dve.tensor_scalar(m[:, 1, :], m[:, 1, :], 1.0 / 64, 64e-5, ALU.mult, ALU.add))
                    dve.sem_inc(var_ready, 1)
                    dve.wait_ge(root_ready, t + 1)
                    do(dve.reciprocal(m[:, 3, :], m[:, 2, :]))
                    do(dve.tensor_tensor(heads(Y), heads(Y), per(m[:, 3, :]), ALU.mult))
                    do(dve.tensor_tensor(Y, Y, spread[:, 0, :], ALU.mult))
                    do(dve.tensor_tensor(Y, Y, spread[:, 1, :], ALU.add))
                    do(dve.tensor_tensor(Y, Y, V, ALU.add))
                    dve.wait_ge(gate_sum, t + 1)
                    dve.tensor_tensor(Y.rearrange("p (h n) -> p h n", h=2), Y.rearrange("p (h n) -> p h n", h=2), ps[:, 0:2, :], ALU.mult).then_inc(y_ready, 1)
                    dve.wait_ge(y_turned, 2 * t + 1)
                    dve.tensor_copy(yT[:, t % 2, 0:4, :].rearrange("p k c -> p (k c)"), ps[:, 2, :]).then_inc(yt_low, 1)
                    for half in range(2):
                        cols = slice(half * HALF, (half + 1) * HALF)
                        dve.wait_ge(out_sum, 2 * t + half + 1)
                        do(dve.tensor_tensor(V[:, cols], ps[:, 4 + 2 * (t % 2) + half, :], spread[:, 2, cols], ALU.mult))
                        dve.tensor_tensor(core.x[:, t, cols], core.x[:, t, cols], V[:, cols], ALU.add).then_inc(x_added, 1)


HD = 64
A_HEADS, B_HEADS, C_HEADS = 8, 8, 16
AB_IN = 3328
C_Q, C_KV, ROPE = 256, 128, 32
QK = HD + ROPE
C_FIRST = C_Q + C_KV + ROPE
BUCKETS, MAX_DISTANCE = 32, 2048
SPAN = T + P


def attention_constants():
    dist = (T - 1) - np.arange(SPAN)
    d = np.maximum(dist, 0)
    exact = BUCKETS // 2
    large = exact + (np.log(np.maximum(d, 1).astype(np.float32) / np.float32(exact)) / np.float32(np.log(MAX_DISTANCE / exact))
                     * np.float32(BUCKETS - exact)).astype(np.int32)
    bucket = np.where(d < exact, d, np.minimum(large, BUCKETS - 1))
    one_hot = (np.arange(BUCKETS)[:, None] == bucket[None, :])
    near = np.where((dist >= 0) & (dist <= 128), 0.0, NEG)
    count = (dist <= 128).astype(int) + (dist % 4 == 0) + (dist % 16 == 0)
    times = np.where((dist >= 0) & (count > 0), np.log(np.maximum(count, 1)), NEG)
    buckets = np.stack([np.concatenate([one_hot, near[None]]), np.concatenate([one_hot, times[None]])], 1)
    i = np.arange(P)[:, None]
    flip = (i + np.arange(P)[None, :] == P - 1)
    causal = np.where(np.arange(T)[None, :] - (T - P) <= i, 0.0, NEG)
    freq = np.tile((10000.0 ** (-np.arange(0, ROPE, 2, dtype=np.float32) / ROPE)).astype(np.float32), (P, 1))
    return (np.ascontiguousarray(buckets.reshape(BUCKETS + 1, -1), np.float32),
            np.ascontiguousarray(np.concatenate([flip, causal, freq], 1), np.float32))


BUCKET_CONST, ATT_CONST = attention_constants()


def norm_in_place(core, gain, dst=None):
    nc = core.nc
    with ExitStack() as held:
        tag = "last" if dst is not None else "mid"
        sb = lambda name, shape, dt=F32: held.enter_context(nc.sbuf_tensor(f"{name}_{tag}", shape, dt))
        g = sb("gain_spread", [P, D])
        junk = sb("squares", [P, D])
        ss = sb("sum_squares", [P, NT])
        s = held.enter_context(signals(nc, "gain_in squared rooted root_ready x_ready stored dve_chain act_chain"))
        gain_in, squared, rooted, root_ready, x_ready, stored, chain_s, act_s = s
        with nc.Block() as block:
            @block.sync
            def _(sp):
                sp.dma_start(g[:, :], rows(*gain, D)).then_inc(gain_in, 16)
                if dst is not None:
                    for t in range(NT):
                        sp.wait_ge(x_ready, t + 1)
                        sp.dma_start(dst[t * P:(t + 1) * P, :], core.x[:, t, :]).then_inc(stored, 16)
                    sp.wait_ge(stored, 16 * NT)

            @block.scalar
            def _(act):
                do = Chain(act, act_s)
                for t in range(NT):
                    do(act.activation(junk[:, :], core.x[:, t, :], ACT.Square, accum_out=ss[:, t:t + 1]))
                act.sem_inc(squared, 1)
                act.wait_ge(rooted, 1)
                act.activation(ss[:, :], ss[:, :], ACT.Sqrt).then_inc(root_ready, 1)

            @block.vector
            def _(dve):
                do = Chain(dve, chain_s)
                dve.wait_ge(squared, 1)
                dve.tensor_scalar(ss[:, :], ss[:, :], 1.0 / D, 1e-6, ALU.mult, ALU.add).then_inc(rooted, 1)
                dve.wait_ge(root_ready, 1)
                do(dve.reciprocal(ss[:, :], ss[:, :]))
                dve.wait_ge(gain_in, 16)
                for t in range(NT):
                    x = core.x[:, t, :]
                    dve.scalar_tensor_tensor(x, x, ss[:, t:t + 1], g[:, :], ALU.mult, ALU.mult).then_inc(x_ready, 1)


def attention(core, tag, units, sinks):
    nc, ps = core.nc, core.ps
    n = len(units)
    with ExitStack() as held:
        sb = lambda name, shape, dt=F32: held.enter_context(nc.sbuf_tensor(f"{name}_{tag}", shape, dt))
        s = sb("scores", [P, 3, HALF])
        pT = sb("probs_turned", [P, 2, HALF])
        stat = sb("row_stats", [P, n, 4])
        MAXI, DEN, SINK, INV = range(4)
        sems = held.enter_context(signals(nc, "scores_sum scored max_ready probs_ready probs_turned pt_ready pv_sum o_ready dve_chain"))
        scores_sum, scored, max_ready, probs_ready, probs_turned, pt_ready, pv_sum, o_ready, chain_s = sems
        width = lambda i: units[i][1].shape[1]
        with nc.Block() as block:
            @block.tensor
            def _(pe):
                for i in range(n + 3):
                    if i < n:
                        q, k = units[i][0], units[i][1]
                        if i >= 2:
                            pe.wait_ge(scored, i - 1)
                        pe.matmul(ps[:, i % 2, 0:width(i)], q, k, start=True, stop=True).then_inc(scores_sum, 1)
                    j = i - 2
                    if 0 <= j < n:
                        pe.wait_ge(probs_ready, j + 1)
                        if j >= 2:
                            pe.wait_ge(pt_ready, j - 1)
                        for b in range(width(j) // P):
                            last = pe.transpose(ps[:, 2 + j % 2, b * P:(b + 1) * P], s[:, j % 3, b * P:(b + 1) * P], core.c("ident"))
                        last.then_inc(probs_turned, 1)
                    j = i - 3
                    if 0 <= j < n:
                        values = units[j][4]
                        pe.wait_ge(pt_ready, j + 1)
                        if j >= 2:
                            pe.wait_ge(o_ready, j - 1)
                        for b, v in enumerate(values):
                            last = pe.matmul(ps[:, 4 + j % 2, 0:HD], pT[:, j % 2, b * P:(b + 1) * P], v, start=b == 0, stop=b == len(values) - 1)
                        last.then_inc(pv_sum, 1)

            @block.vector
            def _(dve):
                do = Chain(dve, chain_s)
                for i in range(n + 3):
                    if i < n:
                        _, _, bias, scale, _, sink, _ = units[i]
                        x = s[:, i % 3, 0:width(i)]
                        m = stat[:, i, MAXI:MAXI + 1]
                        dve.wait_ge(scores_sum, i + 1)
                        if i >= 3:
                            dve.wait_ge(probs_turned, i - 2)
                        dve.scalar_tensor_tensor(x, ps[:, i % 2, 0:width(i)], scale, bias, ALU.mult, ALU.add).then_inc(scored, 1)
                        dve.wait_ge(scored, i + 1)
                        do(dve.tensor_reduce(m, x, AX, ALU.max))
                        if sink is None:
                            dve.tensor_scalar(m, m, -1.0, None, ALU.mult).then_inc(max_ready, 1)
                        else:
                            dve.tensor_scalar(m, m, sink, -1.0, ALU.max, ALU.mult).then_inc(max_ready, 1)
                    j = i - 3
                    if 0 <= j < n:
                        den, inv = stat[:, j, DEN:DEN + 1], stat[:, j, INV:INV + 1]
                        dve.wait_ge(pv_sum, j + 1)
                        if units[j][5] is not None:
                            do(dve.tensor_tensor(den, den, stat[:, j, SINK:SINK + 1], ALU.add))
                        do(dve.reciprocal(inv, den))
                        dve.tensor_scalar(units[j][6], ps[:, 4 + j % 2, 0:HD], inv, None, ALU.mult).then_inc(o_ready, 1)

            @block.scalar
            def _(act):
                for i in range(n + 2):
                    if i < n:
                        x, sink = s[:, i % 3, 0:width(i)], units[i][5]
                        act.wait_ge(max_ready, i + 1)
                        if sink is not None:
                            act.activation(stat[:, i, SINK:SINK + 1], sink, ACT.Exp, bias=stat[:, i, MAXI:MAXI + 1])
                        act.activation(x, x, ACT.Exp, bias=stat[:, i, MAXI:MAXI + 1], accum_out=stat[:, i, DEN:DEN + 1]).then_inc(probs_ready, 1)
                    j = i - 2
                    if 0 <= j < n:
                        act.wait_ge(probs_turned, j + 1)
                        if j >= 2:
                            act.wait_ge(pv_sum, j - 1)
                        act.activation(pT[:, j % 2, 0:width(j)], ps[:, 2 + j % 2, 0:width(j)], ACT.Copy).then_inc(pt_ready, 1)


def gated_out(core, tag, o, z, w_out):
    nc, ps = core.nc, core.ps
    with ExitStack() as held:
        sb = lambda name, shape, dt=F32: held.enter_context(nc.sbuf_tensor(f"{name}_{tag}", shape, dt))
        w = sb("w_out", [P, KD, D])
        oT = sb("o_turned", [P, 2, KD, P])
        s = held.enter_context(signals(nc, "w_in gated turned low high out_sum added"))
        w_in, gated, turned, low, high, out_sum, added = s
        with nc.Block() as block:
            @block.sync
            def _(sp):
                sp.dma_start(w[:, :, :], w_out.rearrange("(k p) n -> p k n", p=P)).then_inc(w_in, 16)

            @block.tensor
            def _(pe):
                for t in range(NT):
                    pe.wait_ge(gated, t + 1)
                    if t:
                        pe.wait_ge(low, t)
                        pe.wait_ge(high, t)
                    for half in range(2):
                        for k in range(4):
                            c0 = (half * 4 + k) * P
                            last = pe.transpose(ps[:, half, k * P:(k + 1) * P], o[:, t, c0:c0 + P], core.c("ident"))
                        last.then_inc(turned, 1)
                    pe.wait_ge(low, t + 1)
                    pe.wait_ge(high, t + 1)
                    if t == 0:
                        pe.wait_ge(w_in, 16)
                    if t >= 2:
                        pe.wait_ge(added, 2 * (t - 1))
                    for half in range(2):
                        for k in range(KD):
                            last = pe.matmul(ps[:, 4 + 2 * (t % 2) + half, :], oT[:, t % 2, k, :], w[:, k, half * HALF:(half + 1) * HALF], start=k == 0, stop=k == KD - 1)
                        last.then_inc(out_sum, 1)

            @block.scalar
            def _(act):
                for t in range(NT):
                    act.wait_ge(turned, 2 * t + 2)
                    act.activation(oT[:, t % 2, 4:8, :].rearrange("p k c -> p (k c)"), ps[:, 1, :], ACT.Copy).then_inc(high, 1)

            @block.vector
            def _(dve):
                for t in range(NT):
                    dve.tensor_tensor(o[:, t, :], o[:, t, :], z[:, t, :], ALU.mult).then_inc(gated, 1)
                for t in range(NT):
                    dve.wait_ge(turned, 2 * t + 1)
                    dve.tensor_copy(oT[:, t % 2, 0:4, :].rearrange("p k c -> p (k c)"), ps[:, 0, :]).then_inc(low, 1)
                    for half in range(2):
                        x = core.x[:, t, half * HALF:(half + 1) * HALF]
                        dve.wait_ge(out_sum, 2 * t + half + 1)
                        dve.tensor_tensor(x, x, ps[:, 4 + 2 * (t % 2) + half, :], ALU.add).then_inc(added, 1)


def window_layer(core):
    nc, ins, ps = core.nc, core.ins, core.ps
    with ExitStack() as held:
        sb = lambda name, shape, dt=F32: held.enter_context(nc.sbuf_tensor(name, shape, dt))
        e_dram = nc.dram_tensor("bias_by_distance", [2, A_HEADS, SPAN], F32, kind="Internal").ap()
        NQ, NK = 8, 6
        qT, kT = sb("q_channels_ab", [P, NQ, T]), sb("k_channels_ab", [P, NK, T])
        v, z = sb("v_tokens_ab", [P, NT, P + B_HEADS * HD]), sb("z_tokens_ab", [P, NT, D])
        bias = sb("bias_tables", [P, 2, A_HEADS, T])
        sinks = sb("sinks", [P, A_HEADS])
        with nc.sbuf_tensor("h_turned_ab", [P, KD, T], F32) as hT:
            norm_turn(core, list(range(NT)), [(ins["norm_w_2"], 0)] * NT, [None] * NT, 1e-6, hT)
            window_inputs(core, hT, qT, kT, v, z, bias, sinks, e_dram)
        o = sb("o_tokens_ab", [P, NT, D])
        units = []
        for h in range(A_HEADS + B_HEADS):
            for t in range(NT):
                row = slice(64 * (h % 2), 64 * (h % 2) + 64)
                a = h < A_HEADS
                first = max(t - 1, 0) if a else 0
                kb = h // 4 if a else 2 + (h - A_HEADS) // 2
                hh = h if a else h - A_HEADS
                vc = (h // 4) * HD if a else P + hh * HD
                u0 = (NT - 1 - t + first) * P
                units.append((qT[row, h // 2, t * P:(t + 1) * P], kT[row, kb, first * P:(t + 1) * P],
                              bias[:, 0 if a else 1, hh, u0:T], float(HD) ** -0.5, [v[:, j, vc:vc + HD] for j in range(first, t + 1)],
                              sinks[:, h:h + 1] if a else None, o[:, t, h * HD:(h + 1) * HD]))
        attention(core, "ab", units, sinks)
        gated_out(core, "ab", o, z, ins["ab_w_out_2"][0])


def window_inputs(core, hT, qT, kT, v, z, bias, sinks, e_dram):
    nc, ins, ps = core.nc, core.ins, core.ps
    with ExitStack() as held:
        sb = lambda name, shape, dt=F32: held.enter_context(nc.sbuf_tensor(name, shape, dt))
        RING = 2
        ring = sb("ab_weights", [P, RING, KD, HALF])
        rel = sb("rel_bias_rows", [BUCKETS + 1, 2 * A_HEADS])
        hot = sb("bucket_rows", [BUCKETS + 1, 2, SPAN])
        con = sb("flip_const", [P, P])
        by_dist = sb("by_distance", [A_HEADS, 2, SPAN])
        slid = sb("slid_rows", [P, 2, T])
        s = held.enter_context(signals(nc, "rel_in hot_in one_set w_in0 w_in1 product moved e_sum e_moved e_out slid_in0 slid_in1 table_sum table_ready"))
        rel_in, hot_in, one_set, w_in0, w_in1, product, moved, e_sum, e_moved, e_out, slid_in0, slid_in1, table_sum, table_ready = s
        w_in, slid_in = [w_in0, w_in1], [slid_in0, slid_in1]
        w = ins["ab_w_in_2"][0].rearrange("(k p) n -> p k n", p=P)
        LOADS = [[(0, 512, 0)], [(512, 64, 0), (512, 64, 64), (576, 64, 128), (576, 64, 192), (640, 128, 256)],
                 [(768, 512, 0)], [(1280, 512, 0)], [(1792, 512, 0)], [(2304, 512, 0)], [(2816, 512, 0)]]
        SUMS = [(0, "ch", m * P, P, qT[:, m, :]) for m in range(4)]
        SUMS += [(1, "ch", m * P, P, kT[:, m, :]) for m in range(2)]
        SUMS += [(1, t, 256, P, v[:, t, 0:P]) for t in range(NT)]
        SUMS += [(2, "ch", m * P, P, qT[:, 4 + m, :]) for m in range(4)]
        SUMS += [(3, "ch", m * P, P, kT[:, 2 + m, :]) for m in range(4)]
        SUMS += [(4, t, 0, HALF, v[:, t, P:P + HALF]) for t in range(NT)]
        SUMS += [(5 + n, t, 0, HALF, z[:, t, n * HALF:(n + 1) * HALF]) for n in range(2) for t in range(NT)]
        last_of = lambda n: max(i for i, x in enumerate(SUMS) if x[0] == n) + 1
        arrived = lambda n: 16 * sum(len(LOADS[q]) for q in range(n % RING, n + 1, RING))
        with nc.Block() as block:
            @block.gpsimd
            def _(pool):
                pool.memset(rel[BUCKETS:BUCKETS + 1, :], 1.0).then_inc(one_set, 1)

            @block.sync
            def _(sp):
                sp.dma_start(rel[0:BUCKETS, :], ins["rel_bias_2"]).then_inc(rel_in, 16)
                sp.dma_start(hot[:, :, :].rearrange("b a n -> b (a n)"), ins["bucket_const"]).then_inc(rel_in, 16)
                sp.dma_start(con[:, :], ins["att_const"][:, 0:P]).then_inc(rel_in, 16)
                sp.dma_start(sinks[:, :], rows(ins["ab_sinks_2"], 0, A_HEADS)).then_inc(rel_in, 16)
                for n, parts in enumerate(LOADS):
                    if n >= RING:
                        sp.wait_ge(product, last_of(n - RING))
                    for c0, cols, at in parts:
                        sp.dma_start(ring[:, n % RING, :, at:at + cols], w[:, :, c0:c0 + cols]).then_inc(w_in[n % RING], 16)
                    if n == 1:
                        sp.wait_ge(e_moved, 4)
                        sp.dma_start(e_dram.rearrange("a h n -> h a n"), by_dist[:, :, :]).then_inc(e_out, 16)
                        sp.wait_ge(e_out, 16)
                for g in range(2 * A_HEADS):
                    if g >= 2:
                        sp.wait_ge(table_sum, g - 1)
                    sp.dma_start(slid[:, g % 2, :], bass.AP(tensor=e_dram.tensor, offset=g * SPAN, ap=[[1, P], [1, T]])).then_inc(slid_in[g % 2], 16)

            @block.tensor
            def _(pe):
                pe.wait_ge(rel_in, 64)
                pe.wait_ge(one_set, 1)
                for a in range(2):
                    for half in range(2):
                        n = SPAN // 2
                        pe.matmul(ps[0:A_HEADS, 2 * a + half, 0:n], rel[:, a * A_HEADS:(a + 1) * A_HEADS], hot[:, a, half * n:(half + 1) * n],
                                  start=True, stop=True).then_inc(e_sum, 1)
                pe.wait_ge(e_moved, 4)
                for i, (n, kind, at, cols, dst) in enumerate(SUMS):
                    pe.wait_ge(w_in[n % RING], arrived(n))
                    if i >= 8:
                        pe.wait_ge(moved, i - 7)
                    for k in range(KD):
                        if kind == "ch":
                            last = pe.matmul(ps[:, i % 8, :], ring[:, n % RING, k, at:at + cols], hT[:, k, :], start=k == 0, stop=k == KD - 1)
                        else:
                            last = pe.matmul(ps[:, i % 8, 0:cols], hT[:, k, kind * P:(kind + 1) * P], ring[:, n % RING, k, at:at + cols], start=k == 0, stop=k == KD - 1)
                    last.then_inc(product, 1)
                pe.wait_ge(moved, len(SUMS))
                for g in range(2 * A_HEADS):
                    pe.wait_ge(slid_in[g % 2], 16 * (g // 2 + 1))
                    if g >= 8:
                        pe.wait_ge(table_ready, g - 7)
                    pe.matmul(ps[:, g % 8, :], con[:, :], slid[:, g % 2, :], start=True, stop=True).then_inc(table_sum, 1)

            @block.scalar
            def _(act):
                for i, (n, kind, at, cols, dst) in enumerate(SUMS):
                    act.wait_ge(product, i + 1)
                    src = ps[:, i % 8, :] if kind == "ch" else ps[:, i % 8, 0:cols]
                    act.activation(dst, src, ACT.Silu if n >= 5 else ACT.Copy).then_inc(moved, 1)

            @block.vector
            def _(dve):
                for j in range(4):
                    n = SPAN // 2
                    dve.wait_ge(e_sum, j + 1)
                    dve.tensor_copy(by_dist[:, j // 2, (j % 2) * n:(j % 2 + 1) * n], ps[0:A_HEADS, j, 0:n]).then_inc(e_moved, 1)
                for g in range(2 * A_HEADS):
                    dve.wait_ge(table_sum, g + 1)
                    dve.tensor_copy(bias[:, g // A_HEADS, g % A_HEADS, :], ps[:, g % 8, :]).then_inc(table_ready, 1)


def latent_layer(core):
    nc, ins, ps = core.nc, core.ins, core.ps
    with ExitStack() as held:
        sb = lambda name, shape, dt=F32: held.enter_context(nc.sbuf_tensor(name, shape, dt))
        qT, kT = sb("q_channels_c", [QK, C_HEADS, T]), sb("k_channels_c", [QK, C_HEADS, T])
        v, z = sb("v_tokens_c", [P, NT, D]), sb("z_tokens_c", [P, NT, D])
        con = sb("att_masks", [P, ATT_CONST.shape[1]])
        with nc.sbuf_tensor("h_turned_c", [P, KD, T], F32) as hT:
            norm_turn(core, list(range(NT)), [(ins["norm_w_2"], D)] * NT, [None] * NT, 1e-6, hT)
            latent_inputs(core, hT, qT, kT, v, z, con)
        o = sb("o_tokens_c", [P, NT, D])
        units = []
        for h in range(C_HEADS):
            for t in range(NT):
                u0 = (NT - 1 - t) * P
                units.append((qT[:, h, t * P:(t + 1) * P], kT[:, h, 0:(t + 1) * P], con[:, P + u0:P + T], float(QK) ** -0.5,
                              [v[:, j, h * HD:(h + 1) * HD] for j in range(t + 1)], None, o[:, t, h * HD:(h + 1) * HD]))
        attention(core, "c", units, None)
        gated_out(core, "c", o, z, ins["c_w_out_2"][0])


def latent_inputs(core, hT, qT, kT, v, z, con):
    nc, ins, ps = core.nc, core.ins, core.ps
    HF = ROPE // 2
    with ExitStack() as held:
        sb = lambda name, shape, dt=F32: held.enter_context(nc.sbuf_tensor(name, shape, dt))
        wc = sb("c_w_first", [P, KD, C_FIRST])
        wz = wc
        wq = sb("c_w_q", [P, 2, C_HEADS * QK])
        wkv = sb("c_w_kv", [P, C_HEADS * 2 * HD])
        gains = sb("c_gains", [P, C_Q + C_KV])
        pos_i, pos = sb("pos_int", [P, NT], I32), sb("pos_float", [P, NT])
        ang, turns_i, turns = sb("angle", [P, NT, 2, HF]), sb("turns_int", [P, NT, 2, HF], I32), sb("turns", [P, NT, 2, HF])
        cs = sb("sin_cos", [P, NT, 2, HF])
        first = sb("c_first", [P, NT, C_FIRST])
        junk = sb("c_squares", [P, C_Q])
        ss = sb("c_sum_squares", [P, NT, 2])
        cT = sb("c_turned", [P, 3, T])
        kpe = sb("k_pe", [P, NT, ROPE])
        tq, tk = sb("q_tokens", [P, C_HEADS, QK]), sb("k_tokens_c", [P, C_HEADS, QK])
        rot = sb("rotated", [P, 4, C_HEADS, HF])
        s = held.enter_context(signals(nc, "small_in pos_in wc_in wq_in first_sum first_done ang_ready trig_done squared rooted root_ready c_ready c_turned c_moved z_in z_sum z_done q_sum kv_sum kv_moved v_moved q_ready k_ready q_turned k_turned qT_done kT_done dve_chain act_chain", core.soft))
        (small_in, pos_in, wc_in, wq_in, first_sum, first_done, ang_ready, trig_done, squared, rooted, root_ready, c_ready, c_turned, c_moved,
         z_in, z_sum, z_done, q_sum, kv_sum, kv_moved, v_moved, q_ready, k_ready, q_turned, k_turned, qT_done, kT_done, chain_s, act_s) = s
        w = ins["c_w_in_2"][0].rearrange("(k p) n -> p k n", p=P)
        Z0 = C_FIRST
        ZP = [(0, 384), (384, 384), (768, 256)]
        with nc.Block() as block:
            @block.gpsimd
            def _(pool):
                with nc.allow_non_contiguous_dma(reason="512 positions, by token on partitions"):
                    pool.dma_start(pos_i[:, :], ins["positions_2"].rearrange("a (t p) -> p (a t)", p=P)).then_inc(pos_in, 16)

            @block.sync
            def _(sp):
                sp.dma_start(wc[:, :, :], w[:, :, 0:C_FIRST]).then_inc(wc_in, 16)
                sp.dma_start(con[:, :], ins["att_const"]).then_inc(small_in, 16)
                sp.dma_start(gains[:, 0:C_Q], rows(ins["c_q_norm_2"], 0, C_Q)).then_inc(small_in, 16)
                sp.dma_start(gains[:, C_Q:], rows(ins["c_kv_norm_2"], 0, C_KV)).then_inc(small_in, 16)
                sp.dma_start(wq[:, :, :], ins["c_w_qb_2"][0].rearrange("(k p) n -> p k n", p=P)).then_inc(wq_in, 16)
                sp.dma_start(wkv[:, :], ins["c_w_kvb_2"][0]).then_inc(wq_in, 16)
                for n, (c0, cols) in enumerate(ZP):
                    if n == 0:
                        sp.wait_ge(first_sum, NT)
                    else:
                        sp.wait_ge(z_sum, NT * n)
                    sp.dma_start(wz[:, :, 0:cols], w[:, :, Z0 + c0:Z0 + c0 + cols]).then_inc(z_in, 16)

            @block.tensor
            def _(pe):
                pe.wait_ge(wc_in, 16)
                for t in range(NT):
                    for k in range(KD):
                        last = pe.matmul(ps[:, t, 0:C_FIRST], hT[:, k, t * P:(t + 1) * P], wc[:, k, :], start=k == 0, stop=k == KD - 1)
                    last.then_inc(first_sum, 1)
                step = 0
                for n, (c0, cols) in enumerate(ZP):
                    pe.wait_ge(z_in, 16 * (n + 1))
                    for t in range(NT):
                        if step >= 4:
                            pe.wait_ge(z_done, step - 3)
                        for k in range(KD):
                            last = pe.matmul(ps[:, 4 + step % 4, 0:cols], hT[:, k, t * P:(t + 1) * P], wz[:, k, 0:cols], start=k == 0, stop=k == KD - 1)
                        last.then_inc(z_sum, 1)
                        step += 1
                pe.wait_ge(c_ready, 1)
                pe.wait_ge(first_done, NT)
                for j in range(3):
                    for t in range(NT):
                        last = pe.transpose(ps[:, j, t * P:(t + 1) * P], first[:, t, j * P:(j + 1) * P], core.c("ident"))
                last.then_inc(c_turned, 1)
                pe.wait_ge(c_moved, 1)
                pe.wait_ge(wq_in, 32)
                pe.wait_ge(z_done, step)
                for t in range(NT):
                    tok = slice(t * P, (t + 1) * P)
                    if t:
                        pe.wait_ge(q_ready, t)
                        pe.wait_ge(kT_done, 4 * t)
                        pe.wait_ge(qT_done, 4 * t)
                    for n in range(3):
                        for k in range(2):
                            last = pe.matmul(ps[:, n, :], cT[:, k, tok], wq[:, k, n * HALF:(n + 1) * HALF], start=k == 0, stop=k == 1)
                    last.then_inc(q_sum, 1)
                    for n in range(4):
                        last = pe.matmul(ps[:, 3 + n, :], cT[:, 2, tok], wkv[:, n * HALF:(n + 1) * HALF], start=True, stop=True)
                    last.then_inc(kv_sum, 1)
                    for src, ready, turned, done in ((tq, q_ready, q_turned, qT_done), (tk, k_ready, k_turned, kT_done)):
                        pe.wait_ge(ready, t + 1)
                        if src is tk:
                            pe.wait_ge(v_moved, t + 1)
                            pe.wait_ge(qT_done, 4 * t + 4)
                        for g in range(4):
                            bank = g if src is tq else 4 + g
                            if src is tq and g == 3:
                                pe.wait_ge(kv_moved, t + 1)
                                pe.wait_ge(v_moved, t + 1)
                            for h in range(4):
                                last = pe.transpose(ps[0:QK, bank, h * P:(h + 1) * P], src[:, 4 * g + h, :], core.c("ident"))
                            last.then_inc(turned, 1)

            @block.scalar
            def _(act):
                do = Chain(act, act_s)
                for t in range(NT):
                    act.wait_ge(first_sum, t + 1)
                    act.activation(first[:, t, :], ps[:, t, 0:C_FIRST], ACT.Copy).then_inc(first_done, 1)
                act.wait_ge(first_done, NT)
                for t in range(NT):
                    for j, (a, b) in enumerate(((0, C_Q), (C_Q, C_Q + C_KV))):
                        do(act.activation(junk[:, 0:b - a], first[:, t, a:b], ACT.Square, accum_out=ss[:, t, j:j + 1]))
                act.sem_inc(squared, 1)
                act.wait_ge(rooted, 1)
                act.activation(ss[:, :, :], ss[:, :, :], ACT.Sqrt).then_inc(root_ready, 1)
                act.wait_ge(ang_ready, 1)
                act.activation(cs[:, :, :, :], ang[:, :, :, :], ACT.Sin).then_inc(trig_done, 1)
                step = 0
                for n, (c0, cols) in enumerate(ZP):
                    for t in range(NT):
                        step += 1
                        act.wait_ge(z_sum, step)
                        act.activation(z[:, t, c0:c0 + cols], ps[:, 4 + (step - 1) % 4, 0:cols], ACT.Silu).then_inc(z_done, 1)
                for t in range(NT):
                    tok = slice(t * P, (t + 1) * P)
                    act.wait_ge(kv_sum, t + 1)
                    for n in range(4):
                        last = act.activation(v[:, t, n * 256:(n + 1) * 256].rearrange("p (h c) -> p h c", h=4),
                                              ps[:, 3 + n, :].rearrange("p (h a c) -> p h a c", h=4, a=2)[:, :, 1, :], ACT.Copy)
                    last.then_inc(v_moved, 1)
                    for g in range(4):
                        act.wait_ge(q_turned, 4 * t + g + 1)
                        act.activation(qT[:, 4 * g:4 * g + 4, tok], ps[0:QK, g, :].rearrange("p (h c) -> p h c", h=4), ACT.Copy).then_inc(qT_done, 1)

            @block.vector
            def _(dve):
                do = Chain(dve, chain_s)
                dve.wait_ge(pos_in, 16)
                dve.wait_ge(small_in, 48)
                do(dve.tensor_copy(pos[:, :], pos_i[:, :]))
                freq = con[:, P + T:P + T + HF]
                A0 = ang[:, :, 0, :]
                do(dve.tensor_tensor(A0, freq.unsqueeze(1).to_broadcast([P, NT, HF]), pos[:, :].unsqueeze(2).to_broadcast([P, NT, HF]), ALU.mult))
                C1, C2 = 6.28125, 1.9353071795e-3
                HALF_PI = float(np.pi / 2)
                do(dve.tensor_scalar(turns[:, :, 0, :], A0, float(1 / (2 * np.pi)), None, ALU.mult))
                do(dve.tensor_scalar(turns[:, :, 1, :], A0, float(1 / (2 * np.pi)), 0.25, ALU.mult, ALU.add))
                do(dve.tensor_scalar(turns[:, :, :, :], turns[:, :, :, :], 12582912.0, None, ALU.add))
                do(dve.tensor_scalar(turns[:, :, :, :], turns[:, :, :, :], -12582912.0, None, ALU.add))
                do(dve.tensor_copy(ang[:, :, 1, :], A0))
                do(dve.scalar_tensor_tensor(ang[:, :, :, :].rearrange("p t a f -> p (t a f)"), turns[:, :, :, :].rearrange("p t a f -> p (t a f)"), -C1,
                                            ang[:, :, :, :].rearrange("p t a f -> p (t a f)"), ALU.mult, ALU.add))
                do(dve.scalar_tensor_tensor(ang[:, :, :, :].rearrange("p t a f -> p (t a f)"), turns[:, :, :, :].rearrange("p t a f -> p (t a f)"), -C2,
                                            ang[:, :, :, :].rearrange("p t a f -> p (t a f)"), ALU.mult, ALU.add))
                do(dve.tensor_scalar(ang[:, :, 1, :], ang[:, :, 1, :], HALF_PI, None, ALU.add))
                do(dve.tensor_scalar(ang[:, :, :, :], ang[:, :, :, :], 3.1415925, -3.1415925, ALU.min, ALU.max))
                dve.sem_inc(ang_ready, 1)
                dve.wait_ge(squared, 1)
                do(dve.tensor_scalar(ss[:, :, 0], ss[:, :, 0], 1.0 / C_Q, 1e-6, ALU.mult, ALU.add))
                do(dve.tensor_scalar(ss[:, :, 1], ss[:, :, 1], 1.0 / C_KV, 1e-6, ALU.mult, ALU.add))
                dve.sem_inc(rooted, 1)
                dve.wait_ge(root_ready, 1)
                do(dve.reciprocal(ss[:, :, :], ss[:, :, :]))
                for t in range(NT):
                    for j, (a, b) in enumerate(((0, C_Q), (C_Q, C_Q + C_KV))):
                        f = first[:, t, a:b]
                        last = dve.scalar_tensor_tensor(f, f, ss[:, t, j:j + 1], gains[:, a:b], ALU.mult, ALU.mult)
                do(last)
                dve.sem_inc(c_ready, 1)
                dve.wait_ge(trig_done, 1)
                sin, cos = cs[:, :, 0, :], cs[:, :, 1, :]
                k1, k2 = first[:, :, C_Q + C_KV:C_Q + C_KV + HF], first[:, :, C_Q + C_KV + HF:C_FIRST]
                tmp = turns[:, :, 0, :]
                do(dve.tensor_tensor(kpe[:, :, 0:HF], k1, cos, ALU.mult))
                do(dve.tensor_tensor(tmp, k2, sin, ALU.mult))
                do(dve.tensor_tensor(kpe[:, :, 0:HF], kpe[:, :, 0:HF], tmp, ALU.subtract))
                do(dve.tensor_tensor(kpe[:, :, HF:], k1, sin, ALU.mult))
                do(dve.tensor_tensor(tmp, k2, cos, ALU.mult))
                do(dve.tensor_tensor(kpe[:, :, HF:], kpe[:, :, HF:], tmp, ALU.add))
                dve.wait_ge(c_turned, 1)
                do(dve.tensor_copy(cT[:, :, :], ps[:, 0:3, :]))
                dve.sem_inc(c_moved, 1)
                for t in range(NT):
                    tok = slice(t * P, (t + 1) * P)
                    per = lambda ap: ap.unsqueeze(1).to_broadcast([P, C_HEADS, HF])
                    dve.wait_ge(q_sum, t + 1)
                    if t:
                        dve.wait_ge(q_turned, 4 * t)
                        dve.wait_ge(k_turned, 4 * t)
                    do(dve.tensor_copy(tq[:, :, :].rearrange("p h c -> p (h c)").rearrange("p (n c) -> p n c", n=3), ps[:, 0:3, :]))
                    q1, q2 = tq[:, :, HD:HD + HF], tq[:, :, HD + HF:QK]
                    do(dve.tensor_tensor(rot[:, 0, :, :], q1, per(cos[:, t, :]), ALU.mult))
                    do(dve.tensor_tensor(rot[:, 1, :, :], q2, per(sin[:, t, :]), ALU.mult))
                    do(dve.tensor_tensor(rot[:, 2, :, :], q1, per(sin[:, t, :]), ALU.mult))
                    do(dve.tensor_tensor(rot[:, 3, :, :], q2, per(cos[:, t, :]), ALU.mult))
                    do(dve.tensor_tensor(q1, rot[:, 0, :, :], rot[:, 1, :, :], ALU.subtract))
                    do(dve.tensor_tensor(q2, rot[:, 2, :, :], rot[:, 3, :, :], ALU.add))
                    dve.sem_inc(q_ready, 1)
                    dve.wait_ge(v_moved, t + 1)
                    for n in range(4):
                        last = dve.tensor_copy(tk[:, 4 * n:4 * n + 4, 0:HD], ps[:, 3 + n, :].rearrange("p (h a c) -> p h a c", h=4, a=2)[:, :, 0, :])
                    do(last)
                    dve.sem_inc(kv_moved, 1)
                    do(dve.tensor_copy(tk[:, :, HD:QK], kpe[:, t, :].unsqueeze(1).to_broadcast([P, C_HEADS, ROPE])))
                    dve.sem_inc(k_ready, 1)
                    for g in range(4):
                        dve.wait_ge(k_turned, 4 * t + g + 1)
                        dve.tensor_copy(kT[:, 4 * g:4 * g + 4, tok], ps[0:QK, 4 + g, :].rearrange("p (h c) -> p h c", h=4)).then_inc(kT_done, 1)


def build(nc, ins, out):
    with ExitStack() as held:
        core = Core(nc, held, ins)
        load_start(core)
        modulation(core)
        with nc.sbuf_tensor("h_turned_gmlp", [P, KD, TA], F32) as hT:
            norm_turn(core, list(range(NTA)), [mod_row(core, 0, t >= NT, 1) for t in range(NTA)],
                      [mod_row(core, 0, t >= NT, 0) for t in range(NTA)], 1e-6, hT)
            gmlp(core, hT)
        moe(core, 0, NTA)
        rwkv(core, 1)
        moe(core, 1, NT)
        norm_in_place(core, (ins["final_g"], 0))
        window_layer(core)
        latent_layer(core)
        norm_in_place(core, (ins["final_norm_2"], 0), dst=out)


INPUTS = ("x c ctx c_ctx ada_w ada_b norm1_g norm2_g final_g ga_w_in ga_b_in ga_ln_g ga_ln_b ga_w_s ga_b_s ga_w_out ga_b_out "
          "rw_mu rw_wr rw_wk rw_wv rw_wo rw_w0 rw_w1 rw_w2 rw_a0 rw_a1 rw_a2 rw_g1 rw_g2 rw_k_k rw_k_a rw_r_k rw_ln_g rw_ln_b "
          "moe_w_grp moe_b_grp moe_w_exp moe_b_exp moe_w_gate moe_w_up moe_w_down positions_2 norm_w_2 rel_bias_2 ab_w_in_2 "
          "ab_sinks_2 ab_w_out_2 c_w_in_2 c_q_norm_2 c_w_qb_2 c_kv_norm_2 c_w_kvb_2 c_w_out_2 final_norm_2").split()


def kernel(**inputs):
    import numpy as _np
    import concourse.bacc as _bacc
    from concourse import mybir as _mybir
    from concourse.bass_utils import run_bass_kernel_spmd as _run

    nc = _bacc.Bacc("TRN2", target_bir_lowering=False, num_devices=1)
    given = {name: _np.ascontiguousarray(inputs[name]) for name in INPUTS}
    given["const"], given["scan_const"] = CONST, SCAN_CONST
    given["bucket_const"], given["att_const"] = BUCKET_CONST, ATT_CONST
    for layer, tiles in ((0, NTA), (1, NT)):
        given[f"cells{layer}"], given[f"entries{layer}"] = tables(tiles)
    arrays, ins = {}, {}
    for name, a in given.items():
        arrays[f"in_{name}_dram"] = a
        ins[name] = nc.dram_tensor(f"in_{name}_dram", a.shape, _mybir.dt.from_np(a.dtype), kind="ExternalInput").ap()
    out = nc.dram_tensor("out_0_dram", (T, D), _mybir.dt.float32, kind="ExternalOutput").ap()
    build(nc, ins, out)
    r = _run(nc, [arrays], core_ids=[0])
    return r.results[0]["out_0_dram"].reshape(1, T, D)
```

```python
from contextlib import ExitStack, contextmanager

import numpy as np

import concourse.bass as bass
from concourse import mybir

P = 128
F32 = mybir.dt.float32
I32 = mybir.dt.int32
U32 = mybir.dt.uint32
ALU = mybir.AluOpType
ACT = mybir.ActivationFunctionType
AX = mybir.AxisListType.X

D = 1024
KD = D // P
T = 512
TC = 256
NT = T // P
NTA = (T + TC) // P
TA = T + TC
W = 2 * D
KW = W // P
NMOD = 6
NEG = -1.0e30
HALF = 512


@contextmanager
def signals(nc, names, soft=None):
    soft = soft or {}
    with ExitStack() as held:
        sems = [soft[n] if n in soft else held.enter_context(nc.semaphore(n)) for n in names.split()]
        hard = [s for n, s in zip(names.split(), sems) if n not in soft]
        yield sems
        with nc.Block() as block:
            @block.sync
            def _(sp):
                for s in hard:
                    sp.sem_clear(s)

            if len(hard) < len(sems):
                @block.gpsimd
                def _(pool):
                    pool.dma_reset()
                    for n in names.split():
                        if n in soft:
                            pool.sem_clear(soft[n])


class Chain:

    def __init__(self, eng, sem):
        self.eng, self.sem, self.n = eng, sem, 0

    def __call__(self, ins):
        self.n += 1
        ins.then_inc(self.sem, 1)
        self.eng.wait_ge(self.sem, self.n)

    def restart(self):
        self.eng.sem_clear(self.sem)
        self.n = 0


def rows(ap, offset, n, parts=P):
    return bass.AP(tensor=ap.tensor, offset=ap.offset + offset, ap=[[0, parts], [1, n]])


def side_by_side(parts):
    where, cols, at = {}, [], 0
    for k, v in parts.items():
        where[k] = (at, v.shape[1])
        at += v.shape[1]
        cols.append(np.asarray(v, np.float32))
    return where, np.ascontiguousarray(np.concatenate(cols, 1))


def constants():
    i, j = np.meshgrid(np.arange(P), np.arange(P), indexing="ij")
    return side_by_side({"ident": i == j, "before": i < j, "ones": np.ones((P, P)), "iota": np.tile(np.arange(32), (P, 1))})


def scan_constants():
    i, j = np.meshgrid(np.arange(P), np.arange(P), indexing="ij")
    same = (i // CHUNK) == (j // CHUNK)
    parts = {
        "head_ones": i // 64 == j // 64, "head_pick": i[:, :2] // 64 == j[:, :2],
        "lt0": same & (i < j), "le0": same & (i <= j), "lt1": same & (i > j), "le1": same & (i >= j),
        "scan_keep": np.tile((np.arange(TA) % CHUNK != 0), (P, 1)),
    }
    size, n = 2, 0
    while size <= CHUNK:
        quarter = (i // size == j // size) & (i % size >= size // 2) & (j % size < size // 2)
        parts[f"q1_{n}"], parts[f"q0_{n}"] = quarter.T, quarter
        size, n = 2 * size, n + 1
    return side_by_side(parts)


CHUNK = 64
NB0 = 32 + (2 * TA) // P
NB1 = 32 + (2 * T) // P
WHERE, CONST = constants()
SCAN_WHERE, SCAN_CONST = scan_constants()


class Core:

    def __init__(self, nc, held, ins):
        self.nc, self.ins = nc, ins
        sb = lambda name, shape, dt=F32: held.enter_context(nc.sbuf_tensor(name, shape, dt))
        self.x = sb("x_tokens", [P, NTA, D])
        self.const = sb("const_cols", [P, CONST.shape[1]])
        self.ps = held.enter_context(nc.psum_tensor("banks", [P, 8, HALF], F32))
        self.calls = 0
        self.soft = {n: held.enter_context(nc.semaphore(n)) for n in
                     "cols_in params_in pos_in x_in x_in0 x_in1 y_out y_out0 y_out1 scattered".split()}
        self.mods = nc.dram_tensor("mods", [2, 2, NMOD, D], F32, kind="Internal").ap()

    def c(self, name, parts=P):
        at, n = WHERE[name]
        return self.const[0:parts, at:at + n]


def load_start(core):
    nc, ins = core.nc, core.ins
    with signals(nc, "loaded") as (loaded,):
        with nc.Block() as block:
            @block.sync
            def _(sp):
                sp.dma_start(core.x[:, 0:NT, :], ins["x"].rearrange("a (t p) d -> p (a t) d", p=P)).then_inc(loaded, 16)
                sp.dma_start(core.x[:, NT:NTA, :], ins["ctx"].rearrange("a (t p) d -> p (a t) d", p=P)).then_inc(loaded, 16)
                sp.dma_start(core.const[:, :], ins["const"]).then_inc(loaded, 16)
                sp.wait_ge(loaded, 48)


def modulation(core):
    nc, ins = core.nc, core.ins
    RING = 3
    GROUPS, ROWS = 4, 32
    QW = D // GROUPS
    with ExitStack() as held:
        sb = lambda name, shape, dt=F32: held.enter_context(nc.sbuf_tensor(name, shape, dt))
        c_rows = sb("c_rows", [2, D])
        c_cols = sb("c_cols", [P, KD, ROWS])
        wring = sb("ada_ring", [P, RING, KD, D])
        out = sb("mod_rows", [P, 2, NMOD, QW])
        gain = sb("gain_rows", [P, 4, QW])
        sems = held.enter_context(signals(nc, "c_in silu_done c_turned c_ready cleared bias_in w_in0 w_in1 w_in2 w_used product taken dve_chain scaled stored"))
        c_in, silu_done, c_turned, c_ready, cleared, bias_in, w0, w1, w2, w_used, product, taken, chain_s, scaled, stored = sems
        w_in = [w0, w1, w2]
        block_rows = lambda j: slice(ROWS * j, ROWS * j + 2)
        with nc.Block() as block:
            @block.sync
            def _(sp):
                sp.dma_start(c_rows[0:1, :], ins["c"]).then_inc(c_in, 16)
                sp.dma_start(c_rows[1:2, :], ins["c_ctx"].rearrange("(a d) -> a d", a=1)).then_inc(c_in, 16)
                for layer in range(2):
                    src = ins["ada_w"][layer].rearrange("(k p) n -> p k n", p=P)
                    with sp.Fori(0, NMOD // RING) as i:
                        for r in range(RING):
                            sp.wait_ge(w_used, i * RING + (layer * NMOD + r + 1))
                            sp.dma_start(wring[:, r, :, :], src[:, :, bass.ds(i * (RING * D) + r * D, D)]).then_inc(w_in[r], 16)
                sp.wait_ge(scaled, 1)
                for layer in range(2):
                    for j in range(GROUPS):
                        sp.dma_start(core.mods[layer][:, :, j * QW:(j + 1) * QW], out[block_rows(j), layer, :, :]).then_inc(stored, 16)
                sp.wait_ge(stored, 32 * GROUPS)

            @block.scalar
            def _(act):
                act.wait_ge(cleared, 1)
                for layer in range(2):
                    for j in range(GROUPS):
                        at = j * QW
                        act.dma_start(out[block_rows(j), layer, :, :], bass.AP(tensor=ins["ada_b"].tensor, offset=ins["ada_b"].offset + layer * NMOD * D + at,
                                                                               ap=[[0, 2], [D, NMOD], [1, QW]])).then_inc(bias_in, 16)
                        act.dma_start(gain[block_rows(j), layer, :], rows(ins["norm1_g"], layer * D + at, QW, 2)).then_inc(bias_in, 16)
                        act.dma_start(gain[block_rows(j), 2 + layer, :], rows(ins["norm2_g"], layer * D + at, QW, 2)).then_inc(bias_in, 16)
                act.wait_ge(c_in, 32)
                act.activation(c_rows[:, :], c_rows[:, :], ACT.Silu).then_inc(silu_done, 1)

            @block.tensor
            def _(pe):
                pe.wait_ge(silu_done, 1)
                for k in range(KD):
                    last = pe.transpose(core.ps[:, 0, 2 * k:2 * k + 2], c_rows[:, k * P:(k + 1) * P], core.c("ident", 2)[:, 0:2])
                last.then_inc(c_turned, 1)
                pe.sem_inc(w_used, RING)
                pe.wait_ge(c_ready, 1)
                for layer in range(2):
                    with pe.Fori(0, NMOD // RING) as i:
                        for r in range(RING):
                            pe.wait_ge(w_in[r], i * 16 + (layer * (NMOD // RING) + 1) * 16)
                            pe.wait_ge(taken, i * RING + (layer * NMOD + r + 1))
                            for k in range(KD):
                                for j in range(GROUPS):
                                    last = pe.matmul(core.ps[j * ROWS:(j + 1) * ROWS, 1 + r, 0:QW], c_cols[:, k, :], wring[:, r, k, j * QW:(j + 1) * QW],
                                                     start=k == 0, stop=k == KD - 1)
                                    if k == KD - 1:
                                        last.then_inc(product, 1)
                            pe.wait_ge(product, i * (RING * GROUPS) + (layer * NMOD + r + 1) * GROUPS)
                            pe.sem_inc(w_used, 1)

            @block.vector
            def _(dve):
                chain = Chain(dve, chain_s)
                dve.memset(out[:, :, :, :], 0.0)
                dve.memset(c_cols[:, :, :], 0.0)
                chain(dve.memset(gain[:, :, :], 0.0))
                dve.sem_inc(cleared, 1)
                dve.wait_ge(c_turned, 1)
                dve.tensor_copy(c_cols[:, :, 0:2], core.ps[:, 0, 0:2 * KD].rearrange("p (k s) -> p k s", s=2)).then_inc(c_ready, 1)
                dve.wait_ge(bias_in, 16 * 6 * GROUPS)
                dve.sem_inc(taken, RING)
                for layer in range(2):
                    with dve.Fori(0, NMOD // RING) as i:
                        for r in range(RING):
                            dve.wait_ge(product, i * (RING * GROUPS) + (layer * NMOD + r + 1) * GROUPS)
                            here = out[:, layer, bass.ds(i * RING + r, 1), :].rearrange("p a c -> p (a c)")
                            dve.tensor_tensor(here, core.ps[:, 1 + r, 0:QW], here, ALU.add).then_inc(taken, 1)
                dve.wait_ge(taken, RING + 2 * NMOD)
                for layer in range(2):
                    for half in range(2):
                        scale = out[:, layer, 1 + 3 * half, :]
                        chain(dve.scalar_tensor_tensor(scale, scale, 1.0, gain[:, 2 * half + layer, :], ALU.add, ALU.mult))
                dve.sem_inc(scaled, 1)


def norm_turn(core, tiles, gains, shifts, eps, hT, keep=None, then_load=None):
    nc = core.nc
    n = len(tiles)
    name = lambda row: (row[0].tensor.name, row[0].offset + row[1])
    core.calls += 1
    tag = core.calls
    srcs = list({name(row): row for row in gains + shifts if row is not None}.values())
    place = {name(row): k for k, row in enumerate(srcs)}
    with ExitStack() as held:
        sb = lambda name, shape, dt=F32: held.enter_context(nc.sbuf_tensor(f"{name}_{tag}", shape, dt))
        spread = sb("spread_rows", [P, len(srcs), D])
        h = sb("h_tokens", [P, 2, D])
        junk = sb("squares", [P, D])
        ss = sb("sum_squares", [P, n])
        rs = sb("rstd", [P, n])
        sems = held.enter_context(signals(nc, "spread_in squared rooted rstd_ready scaled h_ready turned moved_low moved_high kept0 kept1 dve_chain act_chain"))
        spread_in, squared, rooted, rstd_ready, scaled, h_ready, turned, moved_low, moved_high, kept0, kept1, chain_s, act_s = sems
        kept = [kept0, kept1]
        with nc.Block() as block:
            @block.sync
            def _(sp):
                for k, (ap, at) in enumerate(srcs):
                    sp.dma_start(spread[:, k, :], rows(ap, at, D)).then_inc(spread_in, 16)
                if then_load is not None:
                    sp.wait_ge(h_ready, n)
                    then_load(sp)
                if keep is not None:
                    sp.wait_ge(kept[0], 16 * ((n + 1) // 2))
                    sp.wait_ge(kept[1], 16 * (n // 2))

            @block.scalar
            def _(act):
                chain = Chain(act, act_s)
                for j, t in enumerate(tiles):
                    chain(act.activation(junk[:, :], core.x[:, t, :], ACT.Square, accum_out=ss[:, j:j + 1]))
                act.sem_inc(squared, 1)
                act.wait_ge(rooted, 1)
                act.activation(rs[:, :], ss[:, :], ACT.Sqrt).then_inc(rstd_ready, 1)
                for j, t in enumerate(tiles):
                    if keep is not None:
                        act.wait_ge(h_ready, j + 1)
                        act.dma_start(keep[t * P:(t + 1) * P, :], h[:, j % 2, :]).then_inc(kept[j % 2], 16)
                    act.wait_ge(turned, 2 * j + 2)
                    act.activation(hT[:, 4:8, t * P:(t + 1) * P], core.ps[:, 2 * (j % 2) + 1, :].rearrange("p (k c) -> p k c", k=4),
                                   ACT.Copy).then_inc(moved_high, 1)

            @block.vector
            def _(dve):
                chain = Chain(dve, chain_s)
                dve.wait_ge(squared, 1)
                dve.tensor_scalar(ss[:, :], ss[:, :], 1.0 / D, eps, ALU.mult, ALU.add).then_inc(rooted, 1)
                dve.wait_ge(rstd_ready, 1)
                chain(dve.reciprocal(rs[:, :], rs[:, :]))
                dve.wait_ge(spread_in, 16 * len(srcs))

                def evacuate(j):
                    dve.wait_ge(turned, 2 * j + 1)
                    dve.tensor_copy(hT[:, 0:4, tiles[j] * P:(tiles[j] + 1) * P],
                                    core.ps[:, 2 * (j % 2), :].rearrange("p (k c) -> p k c", k=4)).then_inc(moved_low, 1)

                for j, t in enumerate(tiles):
                    if j >= 2:
                        dve.wait_ge(turned, 2 * (j - 1))
                        if keep is not None:
                            dve.wait_ge(kept[j % 2], 16 * (j // 2))
                    g, s = place[name(gains[j])], shifts[j]
                    op = dve.scalar_tensor_tensor(h[:, j % 2, :], core.x[:, t, :], rs[:, j:j + 1], spread[:, g, :], ALU.mult, ALU.mult)
                    if s is not None:
                        chain(op)
                        op = dve.tensor_tensor(h[:, j % 2, :], h[:, j % 2, :], spread[:, place[name(s)], :], ALU.add)
                    op.then_inc(h_ready, 1)
                    if j >= 1:
                        evacuate(j - 1)
                evacuate(n - 1)

            @block.tensor
            def _(pe):
                for j in range(n):
                    pe.wait_ge(h_ready, j + 1)
                    if j >= 2:
                        pe.wait_ge(moved_low, j - 1)
                        pe.wait_ge(moved_high, j - 1)
                    for half in range(2):
                        for k in range(4):
                            c0 = (half * 4 + k) * P
                            last = pe.transpose(core.ps[:, 2 * (j % 2) + half, k * P:(k + 1) * P], h[:, j % 2, c0:c0 + P], core.c("ident"))
                        last.then_inc(turned, 1)


def mod_row(core, layer, stream, m):
    return (core.mods, ((layer * 2 + stream) * NMOD + m) * D)


def tables(nt):
    nb = 32 + 2 * nt
    lane = np.arange(P, dtype=np.int32)
    cells = np.zeros((P, nb, 2), np.int32)
    cells[:, :, 1] = 2 * nt * P + lane[:, None]
    entries = np.zeros((P, 2, nt, 2), np.int32)
    for c in range(2):
        for t in range(nt):
            entries[:, c, t, 0] = t * P + lane
            entries[:, c, t, 1] = (c * nt + t) * P + lane
    return cells.reshape(P, -1), entries.reshape(P, -1)



def gmlp(core, hT):
    nc, ins = core.nc, core.ins
    w_in = ins["ga_w_in"][0].rearrange("(k p) n -> p k n", p=P)
    w_out = ins["ga_w_out"][0].rearrange("(k p) n -> p k n", p=P)
    N = 2 * W // HALF
    NU = N // 2
    TOK = TA // 2
    with ExitStack() as held:
        sb = lambda name, shape, dt=F32: held.enter_context(nc.sbuf_tensor(name, shape, dt))
        uT = sb("u_channels", [P, KW, TA])
        v = sb("v_tokens", [P, NTA, W])
        wring = sb("gmlp_weights", [P, 2, KD, HALF])
        b_u = sb("b_u_cols", [P, KW])
        b_v = sb("b_v_spread", [P, W])
        ws = sb("spatial", [P, KW, P])
        wsT = ws
        bs = sb("spatial_bias", [1, KW, P])
        stats = sb("v_stats", [P, NTA, W // HALF, 6])
        mv = sb("v_mean_var", [P, NTA, 2])
        eps = sb("ln_eps", [P, NTA])
        ln_g = hT[:, 0:2, :].rearrange("p k t -> p (k t)")[:, 0:1536]
        flat = hT[:, :, :].rearrange("p k t -> p (k t)")
        ln_g, ln_b = flat[:, 0:W], flat[:, W:2 * W]
        b_o, gt_l, gt_c = (flat[:, n * D:(n + 1) * D] for n in range(3))
        sems = held.enter_context(signals(nc, "consts_in cols_in w0_in w1_in u_sum u_done v_sum v_biased v_done dve_chain act_chain ws_turned ws_ready", core.soft))
        consts_in, cols_in, w0_in, w1_in, u_sum, u_done, v_sum, v_biased, v_done, chain_s, act_s, ws_turned, ws_ready = sems
        w_arrived = [w0_in, w1_in]

        with nc.Block() as block:
            @block.sync
            def _(sp):
                sp.dma_start(ws[:, :, :], ins["ga_w_s"][0].rearrange("g p q -> p g q")).then_inc(consts_in, 16)
                sp.dma_start(bs[:, :, :], ins["ga_b_s"]).then_inc(consts_in, 16)
                sp.dma_start(b_v[:, :], rows(ins["ga_b_in"], W, W)).then_inc(consts_in, 16)
                for n in range(N):
                    if n >= 2:
                        if n - 2 < NU:
                            sp.wait_ge(u_sum, 8 * (n - 1))
                        else:
                            sp.wait_ge(v_sum, NTA * (n - 2 - NU + 1))
                    sp.dma_start(wring[:, n % 2, :, :], w_in[:, :, n * HALF:(n + 1) * HALF]).then_inc(w_arrived[n % 2], 16)

            @block.gpsimd
            def _(pool):
                with nc.allow_non_contiguous_dma(reason="2048 bias values, one by one"):
                    pool.dma_start(b_u[:, :], ins["ga_b_in"][0, 0:W].rearrange("(k p) -> p k", p=P)).then_inc(cols_in, 16)

            @block.tensor
            def _(pe):
                pe.wait_ge(consts_in, 48)
                for g in range(KW):
                    pe.transpose(core.ps[:, g // 4, (g % 4) * P:(g % 4 + 1) * P], ws[:, g, :], core.c("ident")).then_inc(ws_turned, 1)
                pe.wait_ge(ws_ready, 1)
                step = 0
                for n in range(NU):
                    pe.wait_ge(w_arrived[n % 2], 16 * (n // 2 + 1))
                    for m in range(4):
                        for half in range(2):
                            if step >= 8:
                                pe.wait_ge(u_done, step - 7)
                            for k in range(KD):
                                last = pe.matmul(core.ps[:, step % 8, 0:TOK], wring[:, n % 2, k, m * P:(m + 1) * P],
                                                 hT[:, k, half * TOK:(half + 1) * TOK], start=k == 0, stop=k == KD - 1)
                            last.then_inc(u_sum, 1)
                            step += 1
                pe.wait_ge(u_done, step)
                step = 0
                for n in range(NU, N):
                    pe.wait_ge(w_arrived[n % 2], 16 * (n // 2 + 1))
                    for t in range(NTA):
                        if step >= 8:
                            pe.wait_ge(v_biased, step - 7)
                        for k in range(KD):
                            last = pe.matmul(core.ps[:, step % 8, :], hT[:, k, t * P:(t + 1) * P], wring[:, n % 2, k, :],
                                             start=k == 0, stop=k == KD - 1)
                        last.then_inc(v_sum, 1)
                        step += 1

            @block.scalar
            def _(act):
                act.wait_ge(cols_in, 16)
                step = 0
                for n in range(NU):
                    for m in range(4):
                        for half in range(2):
                            step += 1
                            act.wait_ge(u_sum, step)
                            g = n * 4 + m
                            act.activation(uT[:, g, half * TOK:(half + 1) * TOK], core.ps[:, (step - 1) % 8, 0:TOK], ACT.Gelu,
                                           bias=b_u[:, g:g + 1]).then_inc(u_done, 1)
                step = 0
                for n in range(NU):
                    for t in range(NTA):
                        step += 1
                        act.wait_ge(v_biased, step)
                        part = v[:, t, n * HALF:(n + 1) * HALF]
                        act.activation(part, part, ACT.Gelu).then_inc(v_done, 1)

            @block.vector
            def _(dve):
                for g in range(4):
                    dve.wait_ge(ws_turned, 4 * g + 4)
                    chain_op = dve.tensor_copy(ws[:, 4 * g:4 * g + 4, :].rearrange("p g q -> p (g q)"), core.ps[:, g, :])
                chain_op.then_inc(ws_ready, 1)
                dve.wait_ge(consts_in, 48)

                def stat(step):
                    n, t = divmod(step, NTA)
                    dve.wait_ge(v_done, step + 1)
                    dve.bn_stats(stats[:, t, n, :], v[:, t, n * HALF:(n + 1) * HALF])

                for step in range(NU * NTA):
                    n, t = divmod(step, NTA)
                    dve.wait_ge(v_sum, step + 1)
                    dve.tensor_tensor(v[:, t, n * HALF:(n + 1) * HALF], core.ps[:, step % 8, :], b_v[:, n * HALF:(n + 1) * HALF],
                                      ALU.add).then_inc(v_biased, 1)
                    if step >= 2:
                        stat(step - 2)
                stat(NU * NTA - 2)
                stat(NU * NTA - 1)

        sems = held.enter_context(signals(nc, "ln_in varied rooted v_ready mixed multiplied wo_in0 wo_in1 out_sum added rows_in"))
        ln_in, varied, rooted, v_ready, mixed, multiplied, wo_in0, wo_in1, out_sum, added, rows_in = sems
        wo_in = [wo_in0, wo_in1]
        GB = KW // 4
        with nc.Block() as block:
            @block.sync
            def _(sp):
                sp.dma_start(ln_g, rows(ins["ga_ln_g"], 0, W)).then_inc(ln_in, 16)
                sp.dma_start(ln_b, rows(ins["ga_ln_b"], 0, W)).then_inc(ln_in, 16)
                for n in range(4):
                    if n >= 2:
                        sp.wait_ge(out_sum, n - 1)
                    half, rest = divmod(n, 2)
                    sp.dma_start(wring[:, n % 2, :, :], w_out[:, rest * KD:(rest + 1) * KD, half * HALF:(half + 1) * HALF]).then_inc(wo_in[n % 2], 16)
                    if n == 1:
                        sp.wait_ge(v_ready, NTA)
                        sp.dma_start(b_o, rows(ins["ga_b_out"], 0, D)).then_inc(rows_in, 16)
                        for dst, s in ((gt_l, 0), (gt_c, 1)):
                            ap, at = mod_row(core, 0, s, 2)
                            sp.dma_start(dst, rows(ap, at, D)).then_inc(rows_in, 16)

            @block.scalar
            def _(act):
                act.wait_ge(varied, 1)
                act.activation(eps[:, :], eps[:, :], ACT.Sqrt).then_inc(rooted, 1)

            @block.vector
            def _(dve):
                chain = Chain(dve, chain_s)
                for t in range(NTA):
                    last = dve.bn_aggr(mv[:, t, :], stats[:, t, :, :].rearrange("p n s -> p (n s)"))
                chain(last)
                dve.tensor_scalar(eps[:, :], mv[:, :, 1], 1e-5, None, ALU.add).then_inc(varied, 1)
                dve.wait_ge(rooted, 1)
                chain(dve.reciprocal(eps[:, :], eps[:, :]))
                dve.wait_ge(ln_in, 32)

                def multiply(t):
                    for b in range(GB):
                        dve.wait_ge(mixed, t * GB + b + 1)
                        part = uT[:, 4 * b:4 * b + 4, t * P:(t + 1) * P]
                        dve.tensor_tensor(part, part, core.ps[:, (t * GB + b) % 8, :].rearrange("p (g q) -> p g q", g=4),
                                          ALU.mult).then_inc(multiplied, 1)

                for t in range(NTA):
                    chain(dve.tensor_scalar(v[:, t, :], v[:, t, :], mv[:, t, 0:1], eps[:, t:t + 1], ALU.subtract, ALU.mult))
                    chain(dve.tensor_tensor(v[:, t, :], v[:, t, :], ln_g, ALU.mult))
                    dve.tensor_tensor(v[:, t, :], v[:, t, :], ln_b, ALU.add).then_inc(v_ready, 1)
                    if t >= 1:
                        multiply(t - 1)
                multiply(NTA - 1)
                dve.wait_ge(rows_in, 48)
                for half in range(2):
                    dve.wait_ge(out_sum, 2 * half + 2)
                    cols = slice(half * HALF, (half + 1) * HALF)
                    for t in range(NTA):
                        y = v[:, t, cols]
                        chain(dve.tensor_tensor(y, core.ps[:, (half * NTA + t) % 8, :], b_o[:, cols], ALU.add))
                        chain(dve.tensor_tensor(y, y, (gt_l if t < NT else gt_c)[:, cols], ALU.mult))
                        dve.tensor_tensor(core.x[:, t, cols], core.x[:, t, cols], y, ALU.add).then_inc(added, 1)

            @block.tensor
            def _(pe):
                for t in range(NTA):
                    pe.wait_ge(v_ready, t + 1)
                    for b in range(GB):
                        step = t * GB + b
                        if step >= 8:
                            pe.wait_ge(multiplied, step - 7)
                        bank = core.ps[:, step % 8, :]
                        pe.matmul(bank, core.c("ones", 1), bs[:, 4 * b:4 * b + 4, :].rearrange("a g q -> a (g q)"), start=True, stop=False)
                        for g in range(4):
                            last = pe.matmul(bank[:, g * P:(g + 1) * P], v[:, t, (4 * b + g) * P:(4 * b + g + 1) * P], wsT[:, 4 * b + g, :],
                                             start=False, stop=g == 3)
                        last.then_inc(mixed, 1)
                pe.wait_ge(multiplied, NTA * GB)
                for half in range(2):
                    for rest in range(2):
                        pe.wait_ge(wo_in[rest], 16 * (half + 1))
                        for t in range(NTA):
                            bank = (half * NTA + t) % 8
                            if half and t >= 2 and rest == 0:
                                pe.wait_ge(added, t - 1)
                            for k in range(KD):
                                last = pe.matmul(core.ps[:, bank, :], uT[:, rest * KD + k, t * P:(t + 1) * P], wring[:, rest, k, :],
                                                 start=rest == 0 and k == 0, stop=rest == 1 and k == KD - 1)
                        last.then_inc(out_sum, 1)


E = 32
EG = 8
NG = 4
F = 512
KF = F // P
ROUTER = NG + E


def moe(core, layer, nt):
    nc, ins = core.nc, core.ins
    tl = nt * P
    nb = E + 2 * nt
    with ExitStack() as held:
        sb = lambda name, shape, dt=F32: held.enter_context(nc.sbuf_tensor(f"{name}_{layer}", shape, dt))
        h_rows = nc.dram_tensor(f"h_rows_{layer}", [tl, D], F32, kind="Internal").ap()
        cells = nc.dram_tensor(f"cells_{layer}", [P * nb, 2], I32, kind="Internal").ap()
        y_rows = nc.dram_tensor(f"y_rows_{layer}", [2 * tl + P, D], F32, kind="Internal").ap()
        wg = sb("w_gate_ring", [P, 2, KD, F])
        wu = sb("w_up_ring", [P, 2, KD, F])
        wd = sb("w_down_ring", [P, 2, KF, D])
        weights = sb("choice_weights", [P, 2, nt])
        index = sb("cell_index", [P, nb, 2], I32)
        beyond = sb("blocks_beyond", [P, 2 * nt + 1], I32)
        gate_src = ins["moe_w_gate"][layer].rearrange("e (k p) f -> e p k f", p=P)
        up_src = ins["moe_w_up"][layer].rearrange("e (k p) f -> e p k f", p=P)
        down_src = ins["moe_w_down"][layer].rearrange("e (k p) d -> e p k d", p=P)
        gate_in, gate_in1, up_in, up_in1, down_in, down_in1 = held.enter_context(
            signals(nc, "gate_in0 gate_in1 up_in0 up_in1 down_in0 down_in1"))
        gate_in, up_in, down_in = [gate_in, gate_in1], [up_in, up_in1], [down_in, down_in1]

        def first_weights(sp):
            for r in range(2):
                sp.dma_start(wg[:, r, :, :], gate_src[r]).then_inc(gate_in[r], 16)
                sp.dma_start(wu[:, r, :, :], up_src[r]).then_inc(up_in[r], 16)
                sp.dma_start(wd[:, r, :, :], down_src[r]).then_inc(down_in[r], 16)

        with nc.sbuf_tensor(f"h_turned_{layer}", [P, KD, tl], F32) as hT:
            norm_turn(core, list(range(nt)), [mod_row(core, layer, t >= NT, 4) for t in range(nt)],
                      [mod_row(core, layer, t >= NT, 3) for t in range(nt)], 1e-6, hT, keep=h_rows, then_load=first_weights)
            route(core, layer, nt, nb, hT, cells, weights, index, beyond)
        experts(core, layer, nb, h_rows, y_rows, index, wg, wu, wd, gate_src, up_src, down_src, gate_in, up_in, down_in)
        experts_beyond(core, layer, nt, h_rows, y_rows, index, beyond, wg, wu, wd, gate_src, up_src, down_src)
        combine(core, layer, nt, y_rows, weights)


def route(core, layer, nt, nb, hT, cells, weights, index, beyond):
    nc, ins = core.nc, core.ins
    with ExitStack() as held:
        sb = lambda name, shape, dt=F32: held.enter_context(nc.sbuf_tensor(f"{name}_{layer}", shape, dt))
        wr = sb("router_w", [P, KD, ROUTER])
        br = sb("router_b", [P, ROUTER])
        logits = sb("router_logits", [P, nt, ROUTER])
        grp = sb("grp", [P, 4, nt, NG])
        m = sb("maxima", [P, 12, nt])
        masked = sb("masked", [P, nt, E])
        hit = sb("hit", [P, nt, E])
        work = sb("work", [P, nt, E])
        one_hot = sb("one_hot", [P, 2, nt, E])
        both = sb("both", [P, nt, E])
        pos = sb("pos", [P, nt, E])
        count = sb("count", [P, 6, E])
        slot = sb("slot", [P, 6, nt])
        choice = sb("choice", [P, 2, nt])
        cell = sb("cell", [P, 2, nt], U32)
        entry = sb("entry", [P, 2, nt, 2], I32)
        s = held.enter_context(signals(nc, "router_in cells_set logit_sum dve_chain shifted exp_done second exp2_done chosen placed cells_ready entry_in scattered index_in", core.soft))
        router_in, cells_set, logit_sum, chain_s, shifted, exp_done, second, exp2_done, chosen, placed, cells_ready, entry_in, scattered, index_in = s
        iota = core.c("iota")
        per = lambda ap, n: ap.unsqueeze(2).to_broadcast([P, nt, n])
        over = lambda ap, n: ap.unsqueeze(1).to_broadcast([P, nt, n])
        with nc.Block() as block:
            @block.sync
            def _(sp):
                sp.dma_start(cells.rearrange("(p b) c -> p (b c)", p=P), ins[f"cells{layer}"]).then_inc(cells_set, 16)
                with nc.allow_non_contiguous_dma(reason="router weights: rows of 4 and 32 columns"):
                    sp.dma_start(wr[:, :, 0:NG], ins["moe_w_grp"][layer].rearrange("(k p) n -> p k n", p=P)).then_inc(router_in, 16)
                    sp.dma_start(wr[:, :, NG:], ins["moe_w_exp"][layer].rearrange("(k p) n -> p k n", p=P)).then_inc(router_in, 16)
                    sp.dma_start(br[:, 0:NG], rows(ins["moe_b_grp"], layer * NG, NG)).then_inc(router_in, 16)
                    sp.dma_start(br[:, NG:], rows(ins["moe_b_exp"], layer * E, E)).then_inc(router_in, 16)
                    sp.dma_start(entry[:, :, :, :].rearrange("p k t c -> p (k t c)"), ins[f"entries{layer}"]).then_inc(entry_in, 16)
                    sp.wait_ge(scattered, 16 * 2 * nt)
                    sp.dma_start(index[:, :, :].rearrange("p b c -> p (b c)"), cells.rearrange("(p b) c -> p (b c)", p=P)).then_inc(index_in, 16)
                    sp.wait_ge(index_in, 16)

            @block.tensor
            def _(pe):
                pe.wait_ge(router_in, 64)
                for t in range(nt):
                    for k in range(KD):
                        last = pe.matmul(core.ps[:, 0, t * ROUTER:(t + 1) * ROUTER], hT[:, k, t * P:(t + 1) * P], wr[:, k, :],
                                         start=k == 0, stop=k == KD - 1)
                last.then_inc(logit_sum, 1)
                pe.wait_ge(chosen, 1)
                for t in range(nt):
                    for u in range(t + 1):
                        pe.matmul(core.ps[:, 1, t * E:(t + 1) * E], core.c("before" if u == t else "ones"), both[:, u, :],
                                  start=u == 0, stop=u == t)
                for t in range(nt):
                    last = pe.matmul(core.ps[:, 2, 0:E], core.c("ones"), both[:, t, :], start=t == 0, stop=t == nt - 1)
                last.then_inc(placed, 1)

            @block.scalar
            def _(act):
                act.wait_ge(shifted, 1)
                act.activation(grp[:, 3, :, :], grp[:, 0, :, :], ACT.Exp).then_inc(exp_done, 1)
                act.wait_ge(second, 1)
                act.activation(m[:, 7, :], m[:, 6, :], ACT.Exp).then_inc(exp2_done, 1)

            @block.vector
            def _(dve):
                do = Chain(dve, chain_s)
                dve.wait_ge(logit_sum, 1)
                do(dve.tensor_tensor(logits[:, :, :], core.ps[:, 0, 0:nt * ROUTER].rearrange("p (t n) -> p t n", t=nt), over(br[:, :], ROUTER), ALU.add))
                gl, el = logits[:, :, 0:NG], logits[:, :, NG:]
                do(dve.tensor_reduce(m[:, 0, :], gl, AX, ALU.max))
                dve.tensor_tensor(grp[:, 0, :, :], gl, per(m[:, 0, :], NG), ALU.subtract).then_inc(shifted, 1)
                do(dve.tensor_tensor(grp[:, 1, :, :], gl, per(m[:, 0, :], NG), ALU.is_lt))
                do(dve.scalar_tensor_tensor(grp[:, 1, :, :], grp[:, 1, :, :], 100.0, over(iota[:, 0:NG], NG), ALU.mult, ALU.add))
                do(dve.tensor_reduce(m[:, 1, :], grp[:, 1, :, :], AX, ALU.min))
                do(dve.tensor_tensor(grp[:, 2, :, :], over(iota[:, 0:NG], NG), per(m[:, 1, :], NG), ALU.is_equal))
                dve.wait_ge(exp_done, 1)
                do(dve.tensor_reduce(m[:, 2, :], grp[:, 3, :, :], AX, ALU.add))
                do(dve.reciprocal(m[:, 3, :], m[:, 2, :]))
                do(dve.tensor_scalar(grp[:, 2, :, :], grp[:, 2, :, :], -1.0, -NEG, ALU.add, ALU.mult))
                for g in range(NG):
                    op = dve.tensor_tensor(masked[:, :, g * EG:(g + 1) * EG], el[:, :, g * EG:(g + 1) * EG], per(grp[:, 2, :, g], EG), ALU.add)
                do(op)
                for c in range(2):
                    top, at = m[:, 4 + c, :], choice[:, c, :]
                    do(dve.tensor_reduce(top, masked[:, :, :], AX, ALU.max))
                    do(dve.tensor_tensor(hit[:, :, :], masked[:, :, :], per(top, E), ALU.is_lt))
                    do(dve.scalar_tensor_tensor(hit[:, :, :], hit[:, :, :], 100.0, over(iota, E), ALU.mult, ALU.add))
                    do(dve.tensor_reduce(at, hit[:, :, :], AX, ALU.min))
                    do(dve.tensor_tensor(one_hot[:, c, :, :], over(iota, E), per(at, E), ALU.is_equal))
                    if c == 0:
                        do(dve.scalar_tensor_tensor(masked[:, :, :], one_hot[:, 0, :, :], 2 * NEG, masked[:, :, :], ALU.mult, ALU.add))
                dve.tensor_tensor(both[:, :, :], one_hot[:, 0, :, :], one_hot[:, 1, :, :], ALU.add).then_inc(chosen, 1)
                dve.tensor_tensor(m[:, 6, :], m[:, 5, :], m[:, 4, :], ALU.subtract).then_inc(second, 1)
                dve.wait_ge(exp2_done, 1)
                do(dve.tensor_scalar(m[:, 8, :], m[:, 7, :], 1.0, None, ALU.add))
                do(dve.reciprocal(m[:, 8, :], m[:, 8, :]))
                do(dve.tensor_tensor(weights[:, 0, :], m[:, 3, :], m[:, 8, :], ALU.mult))
                do(dve.tensor_tensor(weights[:, 1, :], weights[:, 0, :], m[:, 7, :], ALU.mult))
                dve.wait_ge(placed, 1)
                do(dve.tensor_copy(pos[:, :, :], core.ps[:, 1, 0:nt * E].rearrange("p (t e) -> p t e", t=nt)))
                do(dve.tensor_copy(count[:, 0, :], core.ps[:, 2, 0:E]))
                do(dve.tensor_scalar(count[:, 1, :], count[:, 0, :], float(P), None, ALU.is_gt))
                for b in range(2, nt):
                    do(dve.scalar_tensor_tensor(count[:, 1, :], count[:, 0, :], float(b * P), count[:, 1, :], ALU.is_gt, ALU.add))
                do(dve.tensor_tensor_scan(count[:, 2, :], core.c("ones")[:, 0:E], count[:, 1, :], 0.0, ALU.mult, ALU.add))
                do(dve.tensor_tensor(count[:, 3, :], count[:, 2, :], count[:, 1, :], ALU.subtract))
                do(dve.scalar_tensor_tensor(count[:, 3, :], count[:, 3, :], float(E - 1), iota, ALU.add, ALU.subtract))
                for b in range(2 * nt):
                    do(dve.tensor_scalar(count[:, 4, :], count[:, 2, :], float(b), None, ALU.is_le))
                    do(dve.tensor_reduce(slot[:, 0, 0:1], count[:, 4, :], AX, ALU.add))
                    do(dve.tensor_scalar(beyond[:, b + 1:b + 2], slot[:, 0, 0:1], float(E - 1), None, ALU.min))
                do(dve.tensor_copy(beyond[:, 0:1], count[:, 2, E - 1:E]))
                for c in range(2):
                    where, shift, blk, first, got = (slot[:, n, :] for n in range(5))
                    do(dve.tensor_tensor(work[:, :, :], pos[:, :, :], one_hot[:, c, :, :], ALU.mult))
                    do(dve.tensor_reduce(where, work[:, :, :], AX, ALU.add))
                    do(dve.tensor_tensor(work[:, :, :], one_hot[:, c, :, :], over(count[:, 3, :], E), ALU.mult))
                    do(dve.tensor_reduce(shift, work[:, :, :], AX, ALU.add))
                    do(dve.tensor_scalar(first, where, float(P), None, ALU.is_ge))
                    do(dve.tensor_copy(blk, first))
                    for b in range(2, nt):
                        do(dve.scalar_tensor_tensor(blk, where, float(b * P), blk, ALU.is_ge, ALU.add))
                    do(dve.scalar_tensor_tensor(where, blk, float(-P), where, ALU.mult, ALU.add))
                    do(dve.tensor_tensor(blk, blk, shift, ALU.add))
                    do(dve.tensor_tensor(blk, blk, first, ALU.mult))
                    do(dve.tensor_tensor(blk, blk, choice[:, c, :], ALU.add))
                    do(dve.scalar_tensor_tensor(got, where, float(nb), blk, ALU.mult, ALU.add))
                    do(dve.tensor_copy(cell[:, c, :], got))
                dve.sem_inc(cells_ready, 1)

            @block.gpsimd
            def _(pool):
                pool.wait_ge(cells_set, 16)
                pool.wait_ge(entry_in, 16)
                pool.wait_ge(cells_ready, 1)
                for c in range(2):
                    for t in range(nt):
                        pool.indirect_dma_start(cells, bass.IndirectOffsetOnAxis(ap=cell[:, c, t:t + 1], axis=0),
                                                entry[:, c, t, :], None).then_inc(scattered, 16)
                pool.wait_ge(scattered, 16 * 2 * nt)


def experts(core, layer, nb, h_rows, y_rows, index, wg, wu, wd, gate_src, up_src, down_src, gate_in, up_in, down_in):
    nc = core.nc
    ps = core.ps
    X_LOW, X_HIGH, G, U, H, Y = 0, 1, 2, 3, 4, 5
    with ExitStack() as held:
        sb = lambda name, shape, dt=F32: held.enter_context(nc.sbuf_tensor(f"{name}_{layer}", shape, dt))
        take = sb("take_rows", [P, 2], I32)
        put = sb("put_rows", [P, 2], I32)
        xs = sb("x_rows", [P, 2, D])
        xT = sb("x_turned", [P, 2, KD, P])
        sg = sb("silu_gate", [P, F])
        h = sb("hidden", [P, F])
        hT = sb("hidden_turned", [P, KF, P])
        ys = sb("y_out_rows", [P, 2, D])
        s = held.enter_context(signals(nc, "x_in0 x_in1 x_turned x_low x_high g_sum u_sum silu_done h_ready h_turned hT_ready y_sum y_low y_high y_free y_out0 y_out1 rows_out pool_chain", core.soft))
        x_in0, x_in1, x_turned, x_low, x_high, g_sum, u_sum, silu_done, h_ready, h_turned, hT_ready, y_sum, y_low, y_high, y_free, y_out0, y_out1, rows_out, pool_s = s
        x_in, y_out = [x_in0, x_in1], [y_out0, y_out1]
        LAST = E // 2 - 1

        def each_expert(eng, step, restart=None):
            with eng.Fori(0, LAST) as i:
                if restart is not None:
                    restart()
                for r in range(2):
                    step(i, r, True)
            for r in range(2):
                step(LAST, r, r == 0)

        with nc.Block() as block:
            @block.sync
            def _(sp):
                with sp.Fori(0, E // 2 - 1) as i:
                    for r in range(2):
                        sp.wait_ge(g_sum, 2 * i + (r + 1))
                        sp.dma_start(wg[:, r, :, :], gate_src[bass.ds(2 * i + (r + 2), 1)].rearrange("a p k f -> p (a k) f")).then_inc(gate_in[r], 16)
                        sp.wait_ge(u_sum, 2 * i + (r + 1))
                        sp.dma_start(wu[:, r, :, :], up_src[bass.ds(2 * i + (r + 2), 1)].rearrange("a p k f -> p (a k) f")).then_inc(up_in[r], 16)
                        sp.wait_ge(y_sum, 2 * i + (r + 1))
                        sp.dma_start(wd[:, r, :, :], down_src[bass.ds(2 * i + (r + 2), 1)].rearrange("a p k f -> p (a k) f")).then_inc(down_in[r], 16)

            @block.gpsimd
            def _(pool):
                do = Chain(pool, pool_s)

                def gather(r):
                    pool.indirect_dma_start(xs[:, r, :], None, h_rows, bass.IndirectOffsetOnAxis(ap=take[:, r:r + 1].bitcast(U32), axis=0)).then_inc(x_in[r], 16)

                def step(i, r, more):
                    if i is not LAST:
                        pool.wait_ge(x_turned, 2 * i + (r + 1))
                        do(pool.tensor_copy(take[:, r:r + 1], index[:, bass.ds(2 * i + (r + 2), 1), 0:1].rearrange("p a c -> p (a c)")))
                        gather(r)
                    do(pool.tensor_copy(put[:, r:r + 1], index[:, bass.ds(2 * i + r, 1), 1:2].rearrange("p a c -> p (a c)")))
                    pool.wait_ge(y_low, 2 * i + (r + 2))
                    pool.wait_ge(y_high, 2 * i + (r + 2))
                    pool.sem_inc(rows_out, 1)
                    pool.indirect_dma_start(y_rows, bass.IndirectOffsetOnAxis(ap=put[:, r:r + 1].bitcast(U32), axis=0), ys[:, r, :], None).then_inc(y_out[r], 16)
                    pool.wait_ge(y_out[r], i * 16 + 16)
                    pool.sem_inc(y_free, 1)

                for r in range(2):
                    do(pool.tensor_copy(take[:, r:r + 1], index[:, r, 0:1]))
                    gather(r)
                pool.sem_inc(y_free, 2)
                each_expert(pool, step, do.restart)

            @block.tensor
            def _(pe):
                def turn_x(r):
                    for k in range(KD):
                        last = pe.transpose(ps[:, X_LOW + k // 4, (k % 4) * P:(k % 4 + 1) * P], xs[:, r, k * P:(k + 1) * P], core.c("ident"))
                    last.then_inc(x_turned, 1)

                def gate(r):
                    for k in range(KD):
                        last = pe.matmul(ps[:, G, :], xT[:, r, k, :], wg[:, r, k, :], start=k == 0, stop=k == KD - 1)
                    last.then_inc(g_sum, 1)

                def step(i, r, more):
                    pe.wait_ge(up_in[r], i * 16 + 16)
                    pe.wait_ge(h_ready, 2 * i + (r + 1))
                    for k in range(KD):
                        last = pe.matmul(ps[:, U, :], xT[:, r, k, :], wu[:, r, k, :], start=k == 0, stop=k == KD - 1)
                    last.then_inc(u_sum, 1)
                    if more:
                        pe.wait_ge(x_in[1 - r], i * 16 + 16 * (r + 1))
                        turn_x(1 - r)
                    pe.wait_ge(h_ready, 2 * i + (r + 2))
                    for k in range(KF):
                        last = pe.transpose(ps[:, H, k * P:(k + 1) * P], h[:, k * P:(k + 1) * P], core.c("ident"))
                    last.then_inc(h_turned, 1)
                    if more:
                        pe.wait_ge(x_low, 2 * i + (r + 2))
                        pe.wait_ge(x_high, 2 * i + (r + 2))
                        pe.wait_ge(gate_in[1 - r], i * 16 + 16 * (r + 1))
                        pe.wait_ge(silu_done, 2 * i + (r + 1))
                        gate(1 - r)
                    pe.wait_ge(hT_ready, 2 * i + (r + 1))
                    pe.wait_ge(down_in[r], i * 16 + 16)
                    pe.wait_ge(y_low, 2 * i + (r + 1))
                    pe.wait_ge(y_high, 2 * i + (r + 1))
                    for half in range(2):
                        for k in range(KF):
                            last = pe.matmul(ps[:, Y + half, :], hT[:, k, :], wd[:, r, k, half * HALF:(half + 1) * HALF], start=k == 0, stop=k == KF - 1)
                    last.then_inc(y_sum, 1)

                pe.wait_ge(x_in[0], 16)
                turn_x(0)
                pe.wait_ge(x_low, 1)
                pe.wait_ge(x_high, 1)
                pe.wait_ge(gate_in[0], 16)
                gate(0)
                each_expert(pe, step)

            @block.scalar
            def _(act):
                def move_x(r):
                    act.activation(xT[:, r, 4:8, :].rearrange("p k c -> p (k c)"), ps[:, X_HIGH, :], ACT.Copy).then_inc(x_high, 1)

                def silu():
                    act.activation(sg[:, :], ps[:, G, :], ACT.Silu).then_inc(silu_done, 1)

                def step(i, r, more):
                    if more:
                        act.wait_ge(x_turned, 2 * i + (r + 2))
                        move_x(1 - r)
                    act.wait_ge(h_turned, 2 * i + (r + 1))
                    act.activation(hT[:, :, :].rearrange("p k c -> p (k c)"), ps[:, H, :], ACT.Copy).then_inc(hT_ready, 1)
                    if more:
                        act.wait_ge(g_sum, 2 * i + (r + 2))
                        act.wait_ge(h_ready, 2 * i + (r + 2))
                        silu()
                    act.wait_ge(y_sum, 2 * i + (r + 1))
                    act.wait_ge(y_free, 2 * i + (r + 1))
                    act.activation(ys[:, r, HALF:D], ps[:, Y + 1, :], ACT.Copy).then_inc(y_high, 1)

                act.sem_inc(y_high, 1)
                act.wait_ge(x_turned, 1)
                move_x(0)
                act.wait_ge(g_sum, 1)
                silu()
                each_expert(act, step)

            @block.vector
            def _(dve):
                def move_x(r):
                    dve.tensor_copy(xT[:, r, 0:4, :].rearrange("p k c -> p (k c)"), ps[:, X_LOW, :]).then_inc(x_low, 1)

                def step(i, r, more):
                    dve.wait_ge(u_sum, 2 * i + (r + 1))
                    dve.wait_ge(silu_done, 2 * i + (r + 1))
                    dve.tensor_tensor(h[:, :], sg[:, :], ps[:, U, :], ALU.mult).then_inc(h_ready, 1)
                    if more:
                        dve.wait_ge(x_turned, 2 * i + (r + 2))
                        move_x(1 - r)
                    dve.wait_ge(y_sum, 2 * i + (r + 1))
                    dve.wait_ge(y_free, 2 * i + (r + 1))
                    dve.tensor_copy(ys[:, r, 0:HALF], ps[:, Y, :]).then_inc(y_low, 1)

                dve.sem_inc(h_ready, 1)
                dve.sem_inc(y_low, 1)
                dve.wait_ge(x_turned, 1)
                move_x(0)
                each_expert(dve, step)


def experts_beyond(core, layer, nt, h_rows, y_rows, index, beyond, wg, wu, wd, gate_src, up_src, down_src):
    nc, ps = core.nc, core.ps
    with ExitStack() as held:
        sb = lambda name, shape, dt=F32: held.enter_context(nc.sbuf_tensor(f"{name}_b{layer}", shape, dt))
        lanes = sb("lanes", [P, 2], I32)
        number = sb("number", [P, 2], I32)
        xs = sb("x_rows", [P, D])
        xT = sb("x_turned", [P, KD, P])
        sg = sb("silu_gate", [P, F])
        h = sb("hidden", [P, F])
        hT = sb("hidden_turned", [P, KF, P])
        ys = sb("y_out_rows", [P, D])
        left = nc.values_load(beyond[0:1, 0:1], min_val=0, max_val=2 * nt)
        with nc.Fori(0, 2 * nt) as b:
            with nc.If(left > b):
                with signals(nc, "lanes_set x_in w_in x_turned x_moved gu_sum silu_done h_ready h_turned hT_ready y_sum y_ready y_out", core.soft) as (
                        lanes_set, x_in, w_in, x_turned, x_moved, gu_sum, silu_done, h_ready, h_turned, hT_ready, y_sum, y_ready, y_out):
                    with nc.Block() as block:
                        @block.sync
                        def _(sp):
                            e = sp.value_load(beyond[0:1, bass.ds(b + 1, 1)], min_val=0, max_val=E - 1)
                            sp.dma_start(wg[:, 0, :, :], gate_src[bass.ds(e, 1)].rearrange("a p k f -> p (a k) f")).then_inc(w_in, 16)
                            sp.dma_start(wu[:, 0, :, :], up_src[bass.ds(e, 1)].rearrange("a p k f -> p (a k) f")).then_inc(w_in, 16)
                            sp.dma_start(wd[:, 0, :, :], down_src[bass.ds(e, 1)].rearrange("a p k f -> p (a k) f")).then_inc(w_in, 16)

                        @block.gpsimd
                        def _(pool):
                            pool.tensor_copy(lanes[:, :], index[:, bass.ds(b + E, 1), :].rearrange("p a c -> p (a c)")).then_inc(lanes_set, 1)
                            pool.wait_ge(lanes_set, 1)
                            pool.indirect_dma_start(xs[:, :], None, h_rows, bass.IndirectOffsetOnAxis(ap=lanes[:, 0:1].bitcast(U32), axis=0)).then_inc(x_in, 16)
                            pool.wait_ge(y_ready, 2)
                            pool.indirect_dma_start(y_rows, bass.IndirectOffsetOnAxis(ap=lanes[:, 1:2].bitcast(U32), axis=0), ys[:, :], None).then_inc(y_out, 16)
                            pool.wait_ge(y_out, 16)

                        @block.tensor
                        def _(pe):
                            pe.wait_ge(x_in, 16)
                            for k in range(KD):
                                last = pe.transpose(ps[:, k // 4, (k % 4) * P:(k % 4 + 1) * P], xs[:, k * P:(k + 1) * P], core.c("ident"))
                            last.then_inc(x_turned, 1)
                            pe.wait_ge(x_moved, 2)
                            pe.wait_ge(w_in, 48)
                            for w, bank in ((wg, 2), (wu, 3)):
                                for k in range(KD):
                                    last = pe.matmul(ps[:, bank, :], xT[:, k, :], w[:, 0, k, :], start=k == 0, stop=k == KD - 1)
                            last.then_inc(gu_sum, 1)
                            pe.wait_ge(h_ready, 1)
                            for k in range(KF):
                                last = pe.transpose(ps[:, 4, k * P:(k + 1) * P], h[:, k * P:(k + 1) * P], core.c("ident"))
                            last.then_inc(h_turned, 1)
                            pe.wait_ge(hT_ready, 1)
                            for half in range(2):
                                for k in range(KF):
                                    last = pe.matmul(ps[:, 5 + half, :], hT[:, k, :], wd[:, 0, k, half * HALF:(half + 1) * HALF], start=k == 0, stop=k == KF - 1)
                            last.then_inc(y_sum, 1)

                        @block.scalar
                        def _(act):
                            act.wait_ge(gu_sum, 1)
                            act.activation(sg[:, :], ps[:, 2, :], ACT.Silu).then_inc(silu_done, 1)

                        @block.vector
                        def _(dve):
                            dve.wait_ge(x_turned, 1)
                            for half in range(2):
                                dve.tensor_copy(xT[:, 4 * half:4 * half + 4, :].rearrange("p k c -> p (k c)"), ps[:, half, :]).then_inc(x_moved, 1)
                            dve.wait_ge(silu_done, 1)
                            dve.tensor_tensor(h[:, :], sg[:, :], ps[:, 3, :], ALU.mult).then_inc(h_ready, 1)
                            dve.wait_ge(h_turned, 1)
                            dve.tensor_copy(hT[:, :, :].rearrange("p k c -> p (k c)"), ps[:, 4, :]).then_inc(hT_ready, 1)
                            dve.wait_ge(y_sum, 1)
                            for half in range(2):
                                dve.tensor_copy(ys[:, half * HALF:(half + 1) * HALF], ps[:, 5 + half, :]).then_inc(y_ready, 1)


def combine(core, layer, nt, y_rows, weights):
    nc = core.nc
    tl = nt * P
    with ExitStack() as held:
        sb = lambda name, shape, dt=F32: held.enter_context(nc.sbuf_tensor(f"{name}_{layer}", shape, dt))
        y = sb("y_back", [P, 2, 2, D])
        gt = sb("gate_spread", [P, 2, D])
        s = held.enter_context(signals(nc, "gate_rows_in y_in0 y_in1 y_added dve_chain"))
        gate_rows_in, y_in0, y_in1, y_added, chain_s = s
        y_in = [y_in0, y_in1]
        with nc.Block() as block:
            @block.sync
            def _(sp):
                for st in range(2):
                    ap, at = mod_row(core, layer, st, 5)
                    sp.dma_start(gt[:, st, :], rows(ap, at, D)).then_inc(gate_rows_in, 16)
                for t in range(nt):
                    if t >= 2:
                        sp.wait_ge(y_added, t - 1)
                    sp.dma_start(y[:, t % 2, :, :], y_rows[0:2 * tl, :].rearrange("(c t p) d -> t p c d", c=2, p=P)[t]).then_inc(y_in[t % 2], 16)

            @block.vector
            def _(dve):
                do = Chain(dve, chain_s)
                dve.wait_ge(gate_rows_in, 32)
                for t in range(nt):
                    dve.wait_ge(y_in[t % 2], 16 * (t // 2 + 1))
                    y1, y2 = y[:, t % 2, 0, :], y[:, t % 2, 1, :]
                    do(dve.tensor_scalar(y1, y1, weights[:, 0, t:t + 1], None, ALU.mult))
                    do(dve.scalar_tensor_tensor(y1, y2, weights[:, 1, t:t + 1], y1, ALU.mult, ALU.add))
                    do(dve.tensor_tensor(y1, y1, gt[:, int(t >= NT), :], ALU.mult))
                    dve.tensor_tensor(core.x[:, t, :], core.x[:, t, :], y1, ALU.add).then_inc(y_added, 1)


DIRS = 2
LORA = 64
GLORA = 160
GRID_W = 64
GRID_H = T // GRID_W
CHUNKS = TA // CHUNK
LEVELS = 6
PARAMS = ("mu0", "mu1", "mu2", "mu3", "mu4", "mu5", "w0_0", "w0_1", "a0_0", "a0_1", "k_k", "k_a", "r_k", "one_less_k_a")
SQRT_E = float(np.exp(-0.5))


class Turns:

    def __init__(self, names):
        self.names, self.done = names, 0

    def of(self, name, rnd):
        return rnd * len(self.names) + self.names.index(name) + 1

    def mark(self, ins, sem, name):
        assert self.names[self.done % len(self.names)] == name, (name, self.names[self.done % len(self.names)])
        self.done += 1
        ins.then_inc(sem, 1)

    def skip(self, eng, sem, name):
        assert self.names[self.done % len(self.names)] == name, (name, self.names[self.done % len(self.names)])
        eng.wait_ge(sem, self.done)
        self.done += 1
        eng.sem_inc(sem, 1)


def run(steps):
    for _ in steps:
        pass


def rwkv(core, layer):
    nc, ins = core.nc, core.ins
    with ExitStack() as held:
        sb = lambda name, shape, dt=F32: held.enter_context(nc.sbuf_tensor(name, shape, dt))
        dram = lambda name, shape: nc.dram_tensor(name, shape, F32, kind="Internal").ap()
        r_dram, k_dram = dram("r_channels", [KD, P, TA]), dram("k_channels", [KD, P, TA])
        v_dram, y_dram = dram("v_rows", [TA, D]), dram("y_rows_rwkv", [T, D])
        x_parked = dram("x_parked", [T, D])
        params = sb("channel_params", [P, len(PARAMS), KD])
        tw = sb("decay_lora", [P, TA])
        ta = sb("a_lora", [P, TA])
        tg = sb("gate_lora", [P, T])
        tg2 = sb("gate_lora_rest", [GLORA - P, T])
        bonus = sb("bonus", [P, NT, 2 * KD])
        with nc.sbuf_tensor("h_turned_rwkv", [P, KD, TA], F32) as hT:
            norm_turn(core, list(range(NTA)), [mod_row(core, layer, t >= NT, 1) for t in range(NTA)],
                      [mod_row(core, layer, t >= NT, 0) for t in range(NTA)], 1e-6, hT)
            projections(core, hT, params, tw, ta, tg, tg2, r_dram, k_dram, v_dram, x_parked)
        recurrence(core, params, tw, ta, bonus, r_dram, k_dram, v_dram, y_dram)
        rwkv_out(core, layer, tg, tg2, bonus, v_dram, y_dram, x_parked)


def projections(core, hT, params, tw, ta, tg, tg2, r_dram, k_dram, v_dram, x_parked):
    nc, ins = core.nc, core.ins
    ps = core.ps
    HT2 = TA // 2
    with ExitStack() as held:
        sb = lambda name, shape, dt=F32: held.enter_context(nc.sbuf_tensor(name, shape, dt))
        xx = sb("shift_minus_h", [P, KD, TA])
        mix = sb("mixed", [P, 2, KD, TA])
        wring = sb("proj_weights", [P, 2, KD, HALF])
        stage = sb("proj_out", [P, 4, HALF])
        w1 = sb("lora_w1", [P, KD, P])
        a1 = sb("lora_a1", [P, KD, P])
        g1 = sb("lora_g1", [P, KD, GLORA])
        s = held.enter_context(signals(nc, "params_in small_in w_in0 w_in1 xx_ready mix_ready lora_sum lora_done product moved stored0 stored1 stored2 stored3 dve_chain x_stored", core.soft))
        params_in, small_in, w_in0, w_in1, xx_ready, mix_ready, lora_sum, lora_done, product, moved, st0, st1, st2, st3, chain_s, x_stored = s
        w_in, stored = [w_in0, w_in1], [st0, st1, st2, st3]
        WIDE = [("rw_wv", 0), ("rw_wv", 1), ("rw_wr", 0), ("rw_wr", 1), ("rw_wk", 0), ("rw_wk", 1)]
        MIXES = [1, 4, 5, 3, 0, 2]
        SUMS = [("v", n, t, 0) for n in range(2) for t in range(NTA)]
        for kind, first in (("r", 2), ("k", 4)):
            SUMS += [(kind, first + n, m, half) for n in range(2) for m in range(4) for half in range(2)]

        with nc.Block() as block:
            @block.gpsimd
            def _(pool):
                with nc.allow_non_contiguous_dma(reason="vectors laid out by channel on partitions"):
                    col = lambda ap: ap.rearrange("a (k p) -> p a k", p=P)
                    pool.dma_start(params[:, 0:6, :], col(ins["rw_mu"][0])).then_inc(params_in, 16)
                    pool.dma_start(params[:, 6:8, :], col(ins["rw_w0"][0])).then_inc(params_in, 16)
                    pool.dma_start(params[:, 8:10, :], col(ins["rw_a0"][0])).then_inc(params_in, 16)
                    pool.dma_start(params[:, 10:11, :], col(ins["rw_k_k"])).then_inc(params_in, 16)
                    pool.dma_start(params[:, 11:12, :], col(ins["rw_k_a"])).then_inc(params_in, 16)
                    pool.dma_start(params[:, 12:13, :], col(ins["rw_r_k"].rearrange("a h k -> a (h k)"))).then_inc(params_in, 16)
                pool.wait_ge(params_in, 96)

            @block.sync
            def _(sp):
                for z in range(DIRS):
                    sp.dma_start(w1[:, :, z * LORA:(z + 1) * LORA], ins["rw_w1"][0, z].rearrange("(k p) r -> p k r", p=P)).then_inc(small_in, 16)
                    sp.dma_start(a1[:, :, z * LORA:(z + 1) * LORA], ins["rw_a1"][0, z].rearrange("(k p) r -> p k r", p=P)).then_inc(small_in, 16)
                sp.dma_start(g1[:, :, :], ins["rw_g1"][0].rearrange("(k p) r -> p k r", p=P)).then_inc(small_in, 16)
                ends = [max(i for i, g in enumerate(SUMS) if g[1] == n) + 1 for n in range(len(WIDE))]
                for n, (name, half) in enumerate(WIDE):
                    if n >= 2:
                        sp.wait_ge(product, ends[n - 2])
                    sp.dma_start(wring[:, n % 2, :, :], ins[name][0].rearrange("(k p) n -> p k n", p=P)[:, :, half * HALF:(half + 1) * HALF]).then_inc(w_in[n % 2], 16)
                    if n == 1:
                        sp.dma_start(x_parked.rearrange("(t p) d -> p t d", p=P), core.x[:, 0:NT, :]).then_inc(x_stored, 16)
                sp.wait_ge(x_stored, 16)

            @block.scalar
            def _(act):
                for n, dst in enumerate((tw, ta)):
                    for half in range(2):
                        act.wait_ge(lora_sum, 2 * n + half + 1)
                        act.activation(dst[:, half * HT2:(half + 1) * HT2], ps[:, 2 * n + half, 0:HT2], (ACT.Tanh, ACT.Copy)[n]).then_inc(lora_done, 1)
                act.wait_ge(lora_sum, 6)
                act.activation(tg[:, :], ps[:, 4, :], ACT.Sigmoid).then_inc(lora_done, 1)
                act.activation(tg2[:, :], ps[0:GLORA - P, 5, :], ACT.Sigmoid).then_inc(lora_done, 1)
                for i, (kind, n, m, half) in enumerate(SUMS):
                    act.wait_ge(product, i + 1)
                    if i >= 4:
                        act.wait_ge(stored[i % 4], 16 * (i // 4))
                    width = HALF if kind == "v" else HT2
                    act.activation(stage[:, i % 4, 0:width], ps[:, i % 8, 0:width], ACT.Copy).then_inc(moved, 1)
                    act.wait_ge(moved, i + 1)
                    if kind == "v":
                        dst = v_dram[m * P:(m + 1) * P, n * HALF:(n + 1) * HALF]
                    else:
                        dst = (r_dram if kind == "r" else k_dram)[(n % 2) * 4 + m, :, half * HT2:(half + 1) * HT2]
                    act.dma_start(dst, stage[:, i % 4, 0:width]).then_inc(stored[i % 4], 16)
                for q in range(4):
                    act.wait_ge(stored[q], 16 * len(SUMS[q::4]))

            @block.vector
            def _(dve):
                do = Chain(dve, chain_s)
                do(dve.tensor_scalar(xx[:, :, :], hT[:, :, :], -1.0, None, ALU.mult))
                grid = lambda ap, k0: ap[:, k0:k0 + 2, 0:T].rearrange("p k (h w) -> p k h w", w=GRID_W)

                def add(dst, src):
                    return dve.tensor_tensor(dst, dst, src, ALU.add)

                for k in range(2):
                    one = lambda ap, k0: ap[:, k0 + k, 0:T].rearrange("p (h w) -> p h w", w=GRID_W)
                    add(one(xx, 0)[:, :, 1:], one(hT, 0)[:, :, :-1])
                    add(one(xx, 2)[:, :, :-1], one(hT, 2)[:, :, 1:])
                add(xx[:, 4:6, GRID_W:T], hT[:, 4:6, 0:T - GRID_W])
                add(xx[:, 6:8, 0:T - GRID_W], hT[:, 6:8, GRID_W:T])
                add(xx[:, 0:4, T + 1:TA], hT[:, 0:4, T:TA - 1])
                do(add(xx[:, 4:8, T:TA - 1], hT[:, 4:8, T + 1:TA]))
                dve.wait_ge(params_in, 96)
                dve.tensor_scalar(params[:, 13, :], params[:, 11, :], -1.0, 1.0, ALU.mult, ALU.add)
                for n, mu in enumerate(MIXES):
                    if n == 2:
                        dve.wait_ge(lora_sum, 2)
                    if n == 3:
                        dve.wait_ge(lora_sum, 4)
                    if n == 4:
                        dve.wait_ge(lora_sum, 6)
                    if n == 5:
                        dve.wait_ge(product, 2 * NTA)
                    for k in range(KD):
                        dve.scalar_tensor_tensor(mix[:, n % 2, k, :], xx[:, k, :], params[:, mu, k:k + 1], hT[:, k, :],
                                                 ALU.mult, ALU.add).then_inc(mix_ready, 1)

            @block.tensor
            def _(pe):
                pe.wait_ge(small_in, 80)
                for n, w in enumerate((w1, a1)):
                    pe.wait_ge(mix_ready, KD * (n + 1))
                    for half in range(2):
                        for k in range(KD):
                            last = pe.matmul(ps[:, 2 * n + half, 0:HT2], w[:, k, :], mix[:, n % 2, k, half * HT2:(half + 1) * HT2], start=k == 0, stop=k == KD - 1)
                        last.then_inc(lora_sum, 1)
                pe.wait_ge(mix_ready, KD * 3)
                for bank, cols in ((4, slice(0, P)), (5, slice(P, GLORA))):
                    n = cols.stop - cols.start
                    for k in range(KD):
                        last = pe.matmul(ps[0:n, bank, :], g1[:, k, cols], mix[:, 0, k, 0:T], start=k == 0, stop=k == KD - 1)
                    last.then_inc(lora_sum, 1)
                pe.wait_ge(lora_done, 6)
                for i, (kind, n, m, half) in enumerate(SUMS):
                    j = {"v": 3, "r": 4, "k": 5}[kind]
                    pe.wait_ge(mix_ready, KD * (j + 1))
                    pe.wait_ge(w_in[n % 2], 16 * (n // 2 + 1))
                    if i >= 8:
                        pe.wait_ge(moved, i - 7)
                    for k in range(KD):
                        if kind == "v":
                            last = pe.matmul(ps[:, i % 8, :], mix[:, 1, k, m * P:(m + 1) * P], wring[:, n % 2, k, :], start=k == 0, stop=k == KD - 1)
                        else:
                            last = pe.matmul(ps[:, i % 8, 0:HT2], wring[:, n % 2, k, m * P:(m + 1) * P], mix[:, j % 2, k, half * HT2:(half + 1) * HT2],
                                             start=k == 0, stop=k == KD - 1)
                    last.then_inc(product, 1)


def recurrence(core, params, tw, ta, bonus, r_dram, k_dram, v_dram, y_dram):
    nc, ins = core.nc, core.ins
    with ExitStack() as held:
        sb = lambda name, shape, dt=F32: held.enter_context(nc.sbuf_tensor(name, shape, dt))
        con = sb("scan_masks", [P, SCAN_CONST.shape[1]])
        sets = [{
            "AR": sb(f"a_and_r{q}", [P, DIRS, NTA, 2, P]),
            "B": sb(f"b_scaled{q}", [P, DIRS, TA]), "K": sb(f"k_scaled{q}", [P, DIRS, TA]),
            "V": sb(f"v_tokens_two_heads{q}", [P, NTA, P]),
            "E": sb(f"exp_whole{q}", [P, DIRS, CHUNKS]),
        } for q in range(2)]
        out = {
            "F": sb("state_factor", [P, DIRS, CHUNKS, P]), "G": sb("state_addend", [P, DIRS, CHUNKS, P]),
            "Q": sb("state_reader", [P, DIRS, T]),
            "Y": sb("y_two_heads", [P, NT, P]),
        }
        c_ = lambda name, n=1: con[:, SCAN_WHERE[name][0]:SCAN_WHERE[name][0] + n * SCAN_WHERE[name][1]]
        with signals(nc, "scan_const_in") as (const_in,):
            with nc.Block() as block:
                @block.sync
                def _(sp):
                    sp.dma_start(con[:, :], ins["scan_const"]).then_inc(const_in, 16)
                    sp.wait_ge(const_in, 16)
        scratch = chunk_scratch(sb)
        state = sb("state", [P, DIRS, 2, P])
        prepare = Prepare(core, held, c_, params, tw, ta, bonus, r_dram, k_dram, v_dram)

        def two_heads(c, q, nxt):
            if nxt is not None:
                prepare.begin(nxt, sets[1 - q])
            chunks(core, c, c_, {**sets[q], **out}, scratch, Scan(core, {**sets[q], **out}, state), prepare if nxt is not None else None, y_dram)

        prepare.begin(0, sets[0])
        prepare.alone()
        with nc.Fori(0, KD // 2 - 1) as i:
            two_heads(i * 2, 0, i * 2 + 1)
            two_heads(i * 2 + 1, 1, i * 2 + 2)
        two_heads(KD - 2, 0, KD - 1)
        two_heads(KD - 1, 1, None)


class Prepare:
    SIGNALS = "rk_in lora_in v_in lora_sum sig_done kk_ready norm_sum norm_sq norm_root chain cum_ready exps_done exps_used prod_ready bonus_sum"

    def __init__(self, core, held, c_, params, tw, ta, bonus, r_dram, k_dram, v_dram):
        self.core, self.c_, self.params, self.tw, self.ta, self.bonus = core, c_, params, tw, ta, bonus
        self.r_dram, self.k_dram, self.v_dram = r_dram, k_dram, v_dram
        sb = lambda name, shape: held.enter_context(core.nc.sbuf_tensor(name, shape, F32))
        scratch = core.x[:, :, :].rearrange("p t d -> p (t d)")
        self.r, self.k, self.kk, self.kk2, self.km, self.kms, self.tmp, self.before = \
            (scratch[:, n * TA:(n + 1) * TA] for n in range(8))
        self.cum, self.e_neg = sb("log_decay_sum", [P, TA]), sb("exp_minus_cum", [P, TA])
        self.lg, self.a = sb("log_decay", [P, DIRS, TA]), sb("a_gate", [P, DIRS, TA])
        self.tot = sb("log_decay_whole", [P, CHUNKS])
        self.w2, self.a2 = sb("lora_w2", [P, P]), sb("lora_a2", [P, P])
        self.pc = sb("params_here", [P, len(PARAMS)])

    def begin(self, c, to):
        self.c, self.to = c, to

    def use(self, sems):
        self.s = dict(zip(self.SIGNALS.split(), sems))

    def alone(self):
        with signals(self.core.nc, self.SIGNALS) as sems:
            self.use(sems)
            with self.core.nc.Block() as block:
                @block.sync
                def _(sp):
                    self.load(sp)

                @block.tensor
                def _(pe):
                    run(self.on_tensor(pe))

                @block.scalar
                def _(act):
                    run(self.on_scalar(act))

                @block.vector
                def _(dve):
                    run(self.on_vector(dve))

    def load(self, sp):
        s, ins, c = self.s, self.core.ins, self.c
        sp.dma_start(self.r, self.r_dram[bass.ds(c, 1)].rearrange("a p t -> p (a t)")).then_inc(s["rk_in"], 16)
        sp.dma_start(self.k, self.k_dram[bass.ds(c, 1)].rearrange("a p t -> p (a t)")).then_inc(s["rk_in"], 16)
        sp.dma_start(self.w2[:, :], ins["rw_w2"][0].rearrange("z r d -> (z r) d")[:, bass.ds(c * P, P)]).then_inc(s["lora_in"], 16)
        sp.dma_start(self.a2[:, :], ins["rw_a2"][0].rearrange("z r d -> (z r) d")[:, bass.ds(c * P, P)]).then_inc(s["lora_in"], 16)
        sp.dma_start(self.to["V"][:, :, :], self.v_dram.rearrange("(t p) d -> p t d", p=P)[:, :, bass.ds(c * P, P)]).then_inc(s["v_in"], 16)
        sp.wait_ge(s["v_in"], 16)

    def on_tensor(self, pe):
        s, ps, H2 = self.s, self.core.ps, TA // 2
        pe.wait_ge(s["lora_in"], 32)
        for n, (w, src) in enumerate(((self.w2, self.tw), (self.a2, self.ta))):
            for z in range(DIRS):
                part = slice(z * LORA, (z + 1) * LORA)
                if n or z:
                    pe.wait_ge(s["sig_done"], 2 * (2 * n + z))
                for half in range(2):
                    pe.matmul(ps[:, 2 + 4 * half, 0:H2], w[part, :], src[part, half * H2:(half + 1) * H2], start=True, stop=True).then_inc(s["lora_sum"], 1)
                yield
        pe.wait_ge(s["kk_ready"], 1)
        pe.wait_ge(s["sig_done"], 8)
        for half in range(2):
            last = pe.matmul(ps[:, 2 + 4 * half, 0:H2], self.c_("head_ones"), self.kk2[:, half * H2:(half + 1) * H2], start=True, stop=True)
        last.then_inc(s["norm_sum"], 1)
        yield
        pe.wait_ge(s["prod_ready"], 1)
        for t in range(NT):
            last = pe.matmul(ps[:, 6, 2 * t:2 * t + 2], self.kk2[:, t * P:(t + 1) * P], self.c_("head_pick"), start=True, stop=True)
        last.then_inc(s["bonus_sum"], 1)
        yield

    def on_scalar(self, act):
        s, ps, H2, pc = self.s, self.core.ps, TA // 2, self.pc
        act.wait_ge(s["cum_ready"], 1)
        for n, (dst, at) in enumerate(((self.lg, 6), (self.a, 8))):
            for z in range(DIRS):
                for half in range(2):
                    act.wait_ge(s["lora_sum"], 4 * n + 2 * z + half + 1)
                    act.activation(dst[:, z, half * H2:(half + 1) * H2], ps[:, 2 + 4 * half, 0:H2], ACT.Sigmoid,
                                   bias=pc[:, at + z:at + z + 1]).then_inc(s["sig_done"], 1)
                yield
        act.wait_ge(s["norm_sq"], 1)
        act.activation(self.tmp, self.tmp, ACT.Sqrt).then_inc(s["norm_root"], 1)
        yield
        for z in range(DIRS):
            act.wait_ge(s["cum_ready"], z + 2)
            if z:
                act.wait_ge(s["exps_used"], 1)
            act.activation(self.e_neg[:, :], self.cum[:, :], ACT.Exp, scale=-1.0).then_inc(s["exps_done"], 1)
            yield
            act.activation(self.before, self.before, ACT.Exp).then_inc(s["exps_done"], 1)
            yield
            act.activation(self.to["E"][:, z, :], self.tot[:, :], ACT.Exp)
            act.wait_ge(s["exps_done"], 3 * z + 1)
            act.activation(self.cum[:, :], self.cum[:, :], ACT.Exp).then_inc(s["exps_done"], 1)
            yield

    def on_vector(self, dve):
        s, ps, H2, b, pc = self.s, self.core.ps, TA // 2, self.to, self.pc
        r, k, kk, kk2, km, kms, tmp, before = self.r, self.k, self.kk, self.kk2, self.km, self.kms, self.tmp, self.before
        cum, tot, lg, a = self.cum[:, :], self.tot[:, :], self.lg, self.a
        by_chunk = lambda ap: ap.rearrange("p (c t) -> p c t", t=CHUNK)
        spread = lambda ap: ap.unsqueeze(2).to_broadcast([P, CHUNKS, CHUNK])
        tiles = lambda ap: ap.rearrange("p (t c) -> p t c", c=P)
        col = lambda name: pc[:, PARAMS.index(name):PARAMS.index(name) + 1]
        do = Chain(dve, s["chain"])

        def sums(z):
            L = lg[:, z, :]
            dve.wait_ge(s["sig_done"], 2 * z + 2)
            do(dve.tensor_scalar(L, L, -SQRT_E, None, ALU.mult))
            yield
            do(dve.tensor_tensor_scan(cum, self.c_("scan_keep"), L, 0.0, ALU.mult, ALU.add))
            yield
            do(dve.tensor_copy(tot, by_chunk(cum)[:, :, CHUNK - 1]))
            if z:
                do(dve.tensor_tensor(cum, L, cum, ALU.subtract))
                yield
                do(dve.tensor_tensor(by_chunk(cum), by_chunk(cum), spread(tot), ALU.add))
                yield
            do(dve.tensor_tensor(before, cum, L, ALU.subtract))
            dve.sem_inc(s["cum_ready"], 1)
            yield

        def changed_k(z):
            dve.wait_ge(s["sig_done"], 4 + 2 * z + 2)
            do(dve.tensor_scalar(tmp, a[:, z, :], col("k_a"), col("one_less_k_a"), ALU.mult, ALU.add))
            yield
            do(dve.tensor_tensor(km, k, tmp, ALU.mult))
            yield
            if z == 0:
                do(dve.tensor_copy(kms, km))
            else:
                do(dve.tensor_tensor(kms, kms, km, ALU.add))
            yield

        def scaled(z):
            do(dve.tensor_tensor(tmp, kk, a[:, z, :], ALU.mult))
            yield
            ar = b["AR"][:, z, :, :, :]
            dve.wait_ge(s["exps_done"], 3 * z + 1)
            do(dve.tensor_tensor(b["B"][:, z, :], tmp, self.e_neg[:, :], ALU.mult))
            yield
            do(dve.tensor_tensor(b["K"][:, z, :], km, self.e_neg[:, :], ALU.mult))
            yield
            dve.wait_ge(s["exps_done"], 3 * z + 2)
            do(dve.scalar_tensor_tensor(ar[:, :, 0, :], tiles(kk), -1.0, tiles(before), ALU.mult, ALU.mult))
            yield
            dve.wait_ge(s["exps_done"], 3 * z + 3)
            do(dve.tensor_tensor(ar[:, :, 1, :], tiles(r), tiles(cum), ALU.mult))
            dve.sem_inc(s["exps_used"], 1)
            yield

        do(dve.tensor_copy(pc[:, :], self.params[:, :, bass.ds(self.c, 1)].rearrange("p n a -> p (n a)")))
        dve.sem_inc(s["cum_ready"], 1)
        dve.wait_ge(s["rk_in"], 32)
        do(dve.tensor_scalar(kk, k, col("k_k"), None, ALU.mult))
        yield
        do(dve.tensor_tensor(kk2, kk, kk, ALU.mult))
        dve.sem_inc(s["kk_ready"], 1)
        yield
        yield from sums(0)
        yield from changed_k(0)
        dve.wait_ge(s["norm_sum"], 1)
        for half in range(2):
            last = dve.tensor_scalar(tmp[:, half * H2:(half + 1) * H2], ps[:, 2 + 4 * half, 0:H2], 1e-12, None, ALU.add)
        do(last)
        dve.sem_inc(s["norm_sq"], 1)
        yield
        dve.wait_ge(s["norm_root"], 1)
        do(dve.reciprocal(tmp, tmp))
        yield
        do(dve.tensor_tensor(kk, kk, tmp, ALU.mult))
        yield
        yield from scaled(0)
        yield from sums(1)
        yield from changed_k(1)
        yield from scaled(1)
        do(dve.scalar_tensor_tensor(kk2, kms, col("r_k"), r, ALU.mult, ALU.mult))
        dve.sem_inc(s["prod_ready"], 1)
        yield
        dve.wait_ge(s["bonus_sum"], 1)
        do(dve.tensor_copy(self.bonus[:, :, bass.ds(self.c * 2, 2)], ps[:, 6, 0:2 * NT].rearrange("p (t h) -> p t h", h=2)))
        yield


class Scan:
    SIGNALS = "state_set late_go read0 read1 stepped0 stepped1 state0 state1 y_added0 y_added1"
    CTX, LAT = list(range(2 * NT, 2 * NTA)), list(range(2 * NT))
    ORDER = [CTX + LAT, CTX[::-1] + LAT[::-1]]
    NC = len(CTX)

    def __init__(self, core, b, S):
        self.ps, self.b, self.S = core.ps, b, S

    def use(self, sems):
        self.state_set, self.late_go = sems[0:2]
        self.read, self.stepped, self.state, self.y_added = (list(sems[n:n + 2]) for n in (2, 4, 6, 8))
        self.adds = [0, 0]

    def early(self, rnd, n):
        return [(z, n - 1) for z in range(DIRS)] if rnd == 1 else [(0, self.NC + n - 1)]

    def late(self):
        return [(z, j + 4 * (1 - z)) for j in range(self.NC, CHUNKS) for z in (1, 0) if j + 4 * (1 - z) < CHUNKS]

    def on_tensor(self, pe, z, j, bank):
        ps, b, S, NC, ch = self.ps, self.b, self.S, self.NC, self.ORDER[z][j]
        if j:
            pe.wait_ge(self.state[z], j)
        else:
            pe.wait_ge(self.state_set, 1)
        if j < CHUNKS - 1:
            pe.matmul(ps[:, 2 + 4 * z, 0:P], b["F"][:, z, ch, :], S[:, z, j % 2, :], start=True, stop=True).then_inc(self.stepped[z], 1)
        if j >= NC:
            lo = 64 * (ch % 2)
            if j > NC:
                pe.wait_ge(self.y_added[z], j - NC)
            pe.matmul(ps[lo:lo + 64, bank, 0:P], b["Q"][:, z, ch * CHUNK:(ch + 1) * CHUNK], S[:, z, j % 2, :], start=True, stop=True).then_inc(self.read[z], 1)

    def on_vector(self, dve, z, j):
        ps, b, S, NC, ch = self.ps, self.b, self.S, self.NC, self.ORDER[z][j]
        if j < CHUNKS - 1:
            dve.wait_ge(self.stepped[z], j + 1)
            dve.scalar_tensor_tensor(S[:, z, (j + 1) % 2, :], ps[:, 2 + 4 * z, 0:P], b["E"][:, z, ch:ch + 1], b["G"][:, z, ch, :], ALU.mult, ALU.add).then_inc(self.state[z], 1)
        if j >= NC:
            bank = 6 if z == 0 and j < NC + 4 else z
            lo = 64 * (ch % 2)
            at = b["Y"][lo:lo + 64, ch // 2, :]
            dve.wait_ge(self.read[z], j - NC + 1)
            for way in range(DIRS):
                if self.adds[way]:
                    dve.wait_ge(self.y_added[way], self.adds[way])
            self.adds[z] += 1
            dve.tensor_tensor(at, ps[lo:lo + 64, bank, 0:P], at, ALU.add).then_inc(self.y_added[z], 1)


def chunk_scratch(sb):
    two = lambda name, shape: [sb(f"{name}{h}", shape) for h in range(2)]
    LR, MR = two("l_and_rb", [P, 4, 2, P]), two("m_and_rk", [P, 4, 2, P])
    LQ = two("l_quarters", [P, 2, 4, P])
    X, XT, Z = two("inverse", [P, 4, P]), two("inverse_turned", [P, 4, P]), two("step", [P, 4, P])
    AM = two("a_and_mv", [P, 4, 2, 64])
    WU = sb("w_and_u", [P, 4, 2, 2, 64])
    Bk, Kk = sb("b_tokens", [P, 4, P]), sb("k_tokens", [P, 4, P])
    fm = sb("factor_masked", [P, 4, P])
    return LR, MR, LQ, X, XT, Z, AM, WU, Bk, Kk, fm


def chunks(core, c, c_, b, scratch, scan, prepare, y_dram):
    nc, ps = core.nc, core.ps
    PAIRS = [(4, 5), (0, 1), (2, 3)]
    with ExitStack() as held:
        LR, MR, LQ, X, XT, Z, AM, WU, Bk, Kk, fm = scratch
        lv = range(1, LEVELS)
        PE = Turns(["P1_0", "P1_1", "P2_0", "P2_1", "X0_0", "X0_1", "TA", "TB", "MV_0", "MV_1"]
                   + [f"{x}{n}_{h}" for n in lv for x in ("Z", "X", "XT") for h in range(2) if not (x == "X" and n == LEVELS - 1)]
                   + ["TK", "WU_0", "WU_1", "YC_0", "YC_1", "Q", "F", "G"])
        DVE = Turns(["LR_0", "LR_1", "MR_0", "MR_1"]
                    + [f"{x}{n}_{h}" for n in lv for x in ("X", "XT") for h in range(2) if not (x == "X" and n == LEVELS - 1)]
                    + ["Q", "F", "G"])
        ACTS = Turns(["X0_0", "X0_1", "TA", "TB", "MV_0", "MV_1"] + [f"Z{n}_{h}" for n in lv for h in range(2)]
                     + ["TK", "WU_0", "WU_1", "YC_0", "YC_1"])
        POOL = Turns(["XT0_0", "XT0_1"] + [f"LQ{n}_{h}" for n in lv for h in range(2)])
        s = held.enter_context(signals(nc, "products by_dve by_act by_pool dve_chain pool_chain y_stored " + Scan.SIGNALS + (" " + Prepare.SIGNALS if prepare else "")))
        products, by_dve, by_act, by_pool, chain_s, pool_s, y_stored = s[:7]
        rest = 7 + len(Scan.SIGNALS.split())
        scan.use(s[7:rest])
        if prepare:
            prepare.use(s[rest:])
        nothing = iter(())
        units = [(z, ti) for z in range(DIRS) for ti in range(2)]
        with nc.Block() as block:
            @block.sync
            def _(sp):
                if prepare:
                    prepare.load(sp)
                for z in range(DIRS):
                    sp.wait_ge(scan.y_added[z], 2 * NT)
                sp.dma_start(y_dram.rearrange("(t p) d -> p t d", p=P)[:, :, bass.ds(c * P, P)], b["Y"][:, :, :]).then_inc(y_stored, 16)
                sp.wait_ge(y_stored, 16)

            @block.tensor
            def _(pe):
                ahead = prepare.on_tensor(pe) if prepare else nothing
                for rnd, pair in enumerate(PAIRS):
                    lat = pair[0] < NT
                    tok = lambda ti: slice(pair[ti] * P, (pair[ti] + 1) * P)
                    wait = lambda sem, order, name, back=0: pe.wait_ge(sem, order.of(name, rnd - back)) if rnd >= back else None
                    row = [slice(0, 64), slice(64, 128)]
                    ar = slice(0, 2 if lat else 1)
                    wide = 2 * P if lat else P
                    for h in range(2):
                        if h == 0:
                            wait(by_dve, DVE, "G", 1)
                            wait(by_act, ACTS, "YC_1", 1)
                        for u, (z, ti) in enumerate(units):
                            last = pe.matmul(ps[:, 4 * h + u // 2, (u % 2) * 256:(u % 2) * 256 + wide], b["B"][row[h], z, tok(ti)],
                                             b["AR"][row[h], z, pair[ti], ar, :].rearrange("p a c -> p (a c)"), start=True, stop=True)
                        PE.mark(last, products, f"P1_{h}")
                    for h in range(2):
                        if h == 1 and rnd == 2:
                            pe.wait_ge(scan.state[1], scan.NC)
                        for u, (z, ti) in enumerate(units):
                            last = pe.matmul(ps[:, 4 * h + 2 + u // 2, (u % 2) * 256:(u % 2) * 256 + wide], b["K"][row[h], z, tok(ti)],
                                             b["AR"][row[h], z, pair[ti], ar, :].rearrange("p a c -> p (a c)"), start=True, stop=True)
                        PE.mark(last, products, f"P2_{h}")
                    for h in range(2):
                        wait(by_pool, POOL, f"XT0_{h}")
                        wait(by_dve, DVE, f"LR_{h}")
                        for u in range(4):
                            last = pe.transpose(ps[:, 4 * h, u * P:(u + 1) * P], XT[h][:, u, :], core.c("ident"))
                        PE.mark(last, products, f"X0_{h}")
                    wait(by_dve, DVE, "MR_1")
                    for name, bank in (("TA", 2), ("TB", 6)):
                        for u, (z, ti) in enumerate(units):
                            src = b["AR"][:, z, pair[ti], 0, :] if name == "TA" else b["B"][:, z, tok(ti)]
                            last = pe.transpose(ps[:, bank, u * P:(u + 1) * P], src, core.c("ident"))
                        PE.mark(last, products, name)
                    for h in range(2):
                        wait(by_act, ACTS, ("TA", "TB")[h])
                        for u, (z, ti) in enumerate(units):
                            last = pe.matmul(ps[:, 4 * h + 2, u * 64:(u + 1) * 64], MR[h][:, u, 0, :], b["V"][:, pair[ti], h * 64:(h + 1) * 64], start=True, stop=True)
                        PE.mark(last, products, f"MV_{h}")
                    for n in lv:
                        for h in range(2):
                            if n == 1:
                                wait(by_act, ACTS, f"X0_{h}")
                            else:
                                wait(by_dve, DVE, f"X{n - 1}_{h}")
                            wait(by_pool, POOL, f"LQ{n}_{h}")
                            for u in range(4):
                                last = pe.matmul(ps[:, 4 * h + 1, u * P:(u + 1) * P], LQ[h][:, n % 2, u, :], X[h][:, u, :], start=True, stop=True)
                            PE.mark(last, products, f"Z{n}_{h}")
                        if n < LEVELS - 1:
                            for h in range(2):
                                wait(by_act, ACTS, f"Z{n}_{h}")
                                if n > 1:
                                    wait(by_dve, DVE, f"XT{n - 1}_{h}")
                                for u in range(4):
                                    last = pe.matmul(ps[:, 4 * h, u * P:(u + 1) * P], XT[h][:, u, :], Z[h][:, u, :], start=True, stop=True)
                                PE.mark(last, products, f"X{n}_{h}")
                        for h in range(2):
                            wait(by_act, ACTS, f"Z{n}_{h}")
                            if n > 1:
                                wait(by_dve, DVE, f"XT{n - 1}_{h}")
                            for u in range(4):
                                last = pe.matmul(ps[:, 4 * h + 3, u * P:(u + 1) * P], Z[h][:, u, :], XT[h][:, u, :], start=True, stop=True)
                            PE.mark(last, products, f"XT{n}_{h}")
                        if rnd == 0:
                            if n == 1 and prepare:
                                wait(by_act, ACTS, "MV_0")
                                wait(by_act, ACTS, "MV_1")
                            next(ahead, None)
                        elif n < LEVELS - 1:
                            if n == 1:
                                wait(by_act, ACTS, "MV_0")
                                wait(by_act, ACTS, "MV_1")
                            for z, j in scan.early(rnd, n):
                                scan.on_tensor(pe, z, j, 6)
                        elif rnd == 2 and prepare:
                            pe.wait_ge(scan.y_added[0], 4)
                            next(ahead)
                    wait(by_act, ACTS, "MV_0")
                    if rnd:
                        pe.wait_ge(scan.state[0], 4 * rnd)
                    if rnd == 0 and prepare:
                        pe.wait_ge(prepare.s["norm_sq"], 1)
                    for u, (z, ti) in enumerate(units):
                        last = pe.transpose(ps[:, 2, u * P:(u + 1) * P], b["K"][:, z, tok(ti)], core.c("ident"))
                    PE.mark(last, products, "TK")
                    for h in range(2):
                        wait(by_dve, DVE, f"XT{LEVELS - 1}_{h}")
                        wait(by_act, ACTS, f"MV_{h}")
                        for u in range(4):
                            last = pe.matmul(ps[:, 4 * h + 1, u * P:(u + 1) * P], XT[h][:, u, :], AM[h][:, u, :, :].rearrange("p a c -> p (a c)"), start=True, stop=True)
                        PE.mark(last, products, f"WU_{h}")
                    for h in range(2):
                        wait(by_act, ACTS, f"WU_{h}")
                        if not lat:
                            PE.skip(pe, products, f"YC_{h}")
                            continue
                        for ti in range(2):
                            for z in range(DIRS):
                                u = z * 2 + ti
                                pe.matmul(ps[:, 4 * h + 3, ti * 64:(ti + 1) * 64], LR[h][:, u, 1, :], WU[:, u, 1, h, :], start=z == 0, stop=False)
                                last = pe.matmul(ps[:, 4 * h + 3, ti * 64:(ti + 1) * 64], MR[h][:, u, 1, :], b["V"][:, pair[ti], h * 64:(h + 1) * 64], start=False, stop=z == 1)
                        PE.mark(last, products, f"YC_{h}")
                    if lat:
                        for h in range(2):
                            for u in range(4):
                                last = pe.matmul(ps[64 * h:64 * h + 64, 0, u * P:(u + 1) * P], WU[:, u, 0, h, :], LR[h][:, u, 1, :], start=True, stop=True)
                        PE.mark(last, products, "Q")
                    else:
                        PE.skip(pe, products, "Q")
                    wait(by_act, ACTS, "YC_1")
                    wait(by_act, ACTS, "TK")
                    for cc in range(2):
                        for u in range(4):
                            last = pe.matmul(ps[:, 3 + 4 * cc, u * P:(u + 1) * P], WU[row[cc], u, 0, :, :].rearrange("p h k -> p (h k)"), Bk[row[cc], u, :], start=True, stop=True)
                    PE.mark(last, products, "F")
                    for cc in range(2):
                        for u, (z, ti) in enumerate(units):
                            pe.matmul(ps[:, 4 + cc, u * P:(u + 1) * P], Bk[row[cc], u, :], WU[row[cc], u, 1, :, :].rearrange("p h k -> p (h k)"), start=True, stop=False)
                            last = pe.matmul(ps[:, 4 + cc, u * P:(u + 1) * P], Kk[row[cc], u, :], b["V"][row[cc], pair[ti], :], start=False, stop=True)
                    PE.mark(last, products, "G")
                run(ahead)
                pe.wait_ge(scan.late_go, 1)
                wait(by_act, ACTS, "WU_0")
                for z, j in scan.late():
                    scan.on_tensor(pe, z, j, z)

            @block.vector
            def _(dve):
                do = Chain(dve, chain_s)
                ahead = prepare.on_vector(dve) if prepare else nothing
                dve.memset(scan.S[:, :, :, :], 0.0).then_inc(scan.state_set, 1)
                for rnd, pair in enumerate(PAIRS):
                    lat = pair[0] < NT
                    wide = 2 * P if lat else P
                    for name, dst, bank in (("P1", LR, 0), ("P2", MR, 2)):
                        for h in range(2):
                            dve.wait_ge(products, PE.of(f"{name}_{h}", rnd))
                            for z in range(DIRS):
                                last = dve.tensor_tensor(dst[h][:, 2 * z:2 * z + 2, :, :].rearrange("p t a c -> p t (a c)")[:, :, 0:wide],
                                                         ps[:, 4 * h + bank + z, :].rearrange("p (t n) -> p t n", t=2)[:, :, 0:wide],
                                                         c_(f"lt{z}", 2)[:, 0:wide].unsqueeze(1).to_broadcast([P, 2, wide]), ALU.mult)
                            DVE.mark(last, by_dve, ("LR" if name == "P1" else "MR") + f"_{h}")
                    for n in lv:
                        if n < LEVELS - 1:
                            for h in range(2):
                                dve.wait_ge(products, PE.of(f"X{n}_{h}", rnd))
                                x = X[h][:, :, :].rearrange("p u c -> p (u c)")
                                DVE.mark(dve.tensor_tensor(x, ps[:, 4 * h, :], x, ALU.add), by_dve, f"X{n}_{h}")
                            next(ahead, None)
                        for h in range(2):
                            dve.wait_ge(products, PE.of(f"XT{n}_{h}", rnd))
                            x = XT[h][:, :, :].rearrange("p u c -> p (u c)")
                            DVE.mark(dve.tensor_tensor(x, ps[:, 4 * h + 3, :], x, ALU.add), by_dve, f"XT{n}_{h}")
                        if rnd and n < LEVELS - 1:
                            if n == 1:
                                dve.wait_ge(by_dve, DVE.of("G", rnd - 1))
                                dve.wait_ge(by_act, ACTS.of("YC_1", rnd - 1))
                            for z, j in scan.early(rnd, n):
                                scan.on_vector(dve, z, j)
                        next(ahead, None)
                    dve.wait_ge(products, PE.of("Q", rnd))
                    if pair[0] < NT:
                        for ti in range(2):
                            t0 = pair[ti] * P
                            last = dve.tensor_tensor(b["Q"][:, :, t0:t0 + P], ps[:, 0, :].rearrange("p (z t c) -> p z t c", z=2, t=2)[:, :, ti, :],
                                                     b["AR"][:, :, pair[ti], 1, :], ALU.add)
                        DVE.mark(last, by_dve, "Q")
                    else:
                        DVE.skip(dve, by_dve, "Q")
                    next(ahead, None)
                    dve.wait_ge(products, PE.of("F", rnd))
                    fold = lambda ap: ap.rearrange("p (z t c) -> p z t c", z=2, t=2)
                    ones4 = c_("head_ones").unsqueeze(1).to_broadcast([P, 4, P])
                    for cc in range(2):
                        do(dve.tensor_tensor(fm[:, :, :], ps[:, 3 + 4 * cc, :].rearrange("p (u c) -> p u c", u=4), ones4, ALU.mult))
                        for z in range(DIRS):
                            at = b["F"][:, z, 2 * pair[0] + cc:2 * pair[1] + cc + 1:2, :]
                            last = dve.tensor_tensor(at, fm[:, 2 * z:2 * z + 2, :], core.c("ident").unsqueeze(1).to_broadcast([P, 2, P]), ALU.add)
                        if cc == 0:
                            do(last)
                    DVE.mark(last, by_dve, "F")
                    dve.wait_ge(products, PE.of("G", rnd))
                    for cc in range(2):
                        for u, (z, ti) in enumerate(units):
                            ch = 2 * pair[ti] + cc
                            last = dve.scalar_tensor_tensor(b["G"][:, z, ch, :], ps[:, 4 + cc, u * P:(u + 1) * P], b["E"][:, z, ch:ch + 1], c_("head_ones"), ALU.mult, ALU.mult)
                    DVE.mark(last, by_dve, "G")
                    next(ahead, None)
                run(ahead)
                dve.wait_ge(by_dve, DVE.done)
                dve.wait_ge(by_act, ACTS.of("YC_1", 2))
                dve.sem_inc(scan.late_go, 1)
                for z, j in scan.late():
                    scan.on_vector(dve, z, j)

            @block.scalar
            def _(act):
                copy = lambda dst, src: act.activation(dst, src, ACT.Copy)
                ahead = prepare.on_scalar(act) if prepare else nothing
                for rnd, pair in enumerate(PAIRS):
                    need = lambda name: act.wait_ge(products, PE.of(name, rnd))
                    for h in range(2):
                        need(f"X0_{h}")
                        ACTS.mark(copy(X[h][:, :, :].rearrange("p u c -> p (u c)"), ps[:, 4 * h, :]), by_act, f"X0_{h}")
                    need("TA")
                    for h in range(2):
                        last = copy(AM[h][:, :, 0, :], ps[:, 2, :].rearrange("p (u h c) -> p u h c", u=4, h=2)[:, :, h, :])
                    ACTS.mark(last, by_act, "TA")
                    need("TB")
                    ACTS.mark(copy(Bk[:, :, :].rearrange("p u c -> p (u c)"), ps[:, 6, :]), by_act, "TB")
                    for h in range(2):
                        need(f"MV_{h}")
                        ACTS.mark(copy(AM[h][:, :, 1, :], ps[:, 4 * h + 2, 0:256].rearrange("p (u c) -> p u c", u=4)), by_act, f"MV_{h}")
                    for n in lv:
                        for h in range(2):
                            need(f"Z{n}_{h}")
                            ACTS.mark(copy(Z[h][:, :, :].rearrange("p u c -> p (u c)"), ps[:, 4 * h + 1, :]), by_act, f"Z{n}_{h}")
                        if (rnd == 0 and n <= 4) or (rnd == 2 and n <= 3):
                            next(ahead, None)
                    need("TK")
                    ACTS.mark(copy(Kk[:, :, :].rearrange("p u c -> p (u c)"), ps[:, 2, :]), by_act, "TK")
                    if rnd == 0:
                        next(ahead, None)
                    for h in range(2):
                        need(f"WU_{h}")
                        ACTS.mark(copy(WU[:, :, :, h, :], ps[:, 4 * h + 1, :].rearrange("p (u a c) -> p u a c", u=4, a=2)), by_act, f"WU_{h}")
                    for h in range(2):
                        need(f"YC_{h}")
                        if pair[0] < NT:
                            ACTS.mark(copy(b["Y"][:, pair[0]:pair[1] + 1, h * 64:(h + 1) * 64], ps[:, 4 * h + 3, 0:P].rearrange("p (t c) -> p t c", t=2)), by_act, f"YC_{h}")
                        else:
                            ACTS.skip(act, by_act, f"YC_{h}")
                    if rnd == 0:
                        for _ in range(3):
                            next(ahead, None)
                run(ahead)

            @block.gpsimd
            def _(pool):
                do = Chain(pool, pool_s)
                pm = lambda n: c_(f"q1_{n}", 2).rearrange("p (z c) -> p z c", z=2)
                four = lambda ap: ap.rearrange("p (z t) c -> p z t c", z=2)
                for rnd, pair in enumerate(PAIRS):
                    for h in range(2):
                        pool.wait_ge(by_dve, DVE.of(f"LR_{h}", rnd))
                        for ti in range(2):
                            last = pool.tensor_tensor(four(XT[h][:, :, :])[:, :, ti, :], four(LR[h][:, :, 0, :])[:, :, ti, :], pm(0), ALU.mult)
                        do(last)
                        POOL.mark(pool.tensor_tensor(XT[h][:, :, :], XT[h][:, :, :], core.c("ident").unsqueeze(1).to_broadcast([P, 4, P]), ALU.add),
                                  by_pool, f"XT0_{h}")
                    for n in lv:
                        for h in range(2):
                            if n > 2:
                                pool.wait_ge(products, PE.of(f"Z{n - 2}_{h}", rnd))
                            for ti in range(2):
                                last = pool.tensor_tensor(four(LQ[h][:, n % 2, :, :])[:, :, ti, :], four(LR[h][:, :, 0, :])[:, :, ti, :], pm(n), ALU.mult)
                            POOL.mark(last, by_pool, f"LQ{n}_{h}")


def rwkv_out(core, layer, tg, tg2, bonus, v_dram, y_dram, x_parked):
    nc, ins, ps = core.nc, core.ins, core.ps
    HEADS = 2 * KD
    with ExitStack() as held:
        sb = lambda name, shape, dt=F32: held.enter_context(nc.sbuf_tensor(name, shape, dt))
        wo = sb("wo", [P, KD, D])
        g2 = sb("gate_w2", [P, D])
        g2b = sb("gate_w2_rest", [GLORA - P, D])
        spread = sb("head_gain_bias", [P, 3, D])
        y, v = sb("y_here", [P, 2, D]), sb("v_here", [P, 2, D])
        sq = sb("y_squared", [P, D])
        m = sb("head_stats", [P, 4, HEADS])
        yT = sb("y_turned", [P, 2, KD, P])
        s = held.enter_context(signals(nc, "wo_in small_in y_in0 y_in1 gate_sum centred squares var_ready root_ready y_ready y_turned yt_low yt_high out_sum x_added dve_chain x_in_again"))
        wo_in, small_in, y_in0, y_in1, gate_sum, centred, squares, var_ready, root_ready, y_ready, y_turned, yt_low, yt_high, out_sum, x_added, chain_s, x_in_again = s
        y_in = [y_in0, y_in1]
        heads = lambda ap: ap.rearrange("p (h k) -> p h k", k=64)
        per = lambda ap: ap.unsqueeze(2).to_broadcast([P, HEADS, 64])
        with nc.Block() as block:
            @block.sync
            def _(sp):
                for n, (ap, at) in enumerate(((ins["rw_ln_g"], 0), (ins["rw_ln_b"], 0), mod_row(core, layer, 0, 2))):
                    sp.dma_start(spread[:, n, :], rows(ap, at, D)).then_inc(small_in, 16)
                sp.dma_start(g2[:, :], ins["rw_g2"][0, 0:P, :]).then_inc(small_in, 16)
                sp.dma_start(g2b[:, :], ins["rw_g2"][0, P:GLORA, :]).then_inc(small_in, 16)
                for t in range(NT):
                    if t >= 2:
                        sp.wait_ge(y_turned, 2 * (t - 1))
                        sp.wait_ge(x_added, 2 * (t - 1))
                    sp.dma_start(y[:, t % 2, :], y_dram[t * P:(t + 1) * P, :]).then_inc(y_in[t % 2], 16)
                    sp.dma_start(v[:, t % 2, :], v_dram[t * P:(t + 1) * P, :]).then_inc(y_in[t % 2], 16)
                    if t == 0:
                        sp.dma_start(wo[:, :, :], ins["rw_wo"][0].rearrange("(k p) n -> p k n", p=P)).then_inc(wo_in, 16)
                        sp.dma_start(core.x[:, 0:NT, :], x_parked.rearrange("(t p) d -> p t d", p=P)).then_inc(x_in_again, 16)

            @block.tensor
            def _(pe):
                def gate(t):
                    for half in range(2):
                        cols = slice(half * HALF, (half + 1) * HALF)
                        pe.matmul(ps[:, half, :], tg[:, t * P:(t + 1) * P], g2[:, cols], start=True, stop=False)
                        last = pe.matmul(ps[:, half, :], tg2[:, t * P:(t + 1) * P], g2b[:, cols], start=False, stop=True)
                    last.then_inc(gate_sum, 1)

                pe.wait_ge(small_in, 80)
                gate(0)
                for t in range(NT):
                    pe.wait_ge(y_ready, t + 1)
                    for half in range(2):
                        for k in range(4):
                            c0 = (half * 4 + k) * P
                            last = pe.transpose(ps[:, 2 + half, k * P:(k + 1) * P], y[:, t % 2, c0:c0 + P], core.c("ident"))
                        last.then_inc(y_turned, 1)
                    if t + 1 < NT:
                        gate(t + 1)
                    pe.wait_ge(yt_low, t + 1)
                    pe.wait_ge(yt_high, t + 1)
                    if t == 0:
                        pe.wait_ge(wo_in, 16)
                    if t >= 2:
                        pe.wait_ge(x_added, 2 * (t - 1))
                    for half in range(2):
                        for k in range(KD):
                            last = pe.matmul(ps[:, 4 + 2 * (t % 2) + half, :], yT[:, t % 2, k, :], wo[:, k, half * HALF:(half + 1) * HALF], start=k == 0, stop=k == KD - 1)
                        last.then_inc(out_sum, 1)

            @block.scalar
            def _(act):
                def variance(t):
                    act.wait_ge(centred, t + 1)
                    act.activation(sq[:, :], y[:, t % 2, :], ACT.Square).then_inc(squares, 1)
                    act.wait_ge(var_ready, t + 1)
                    act.activation(m[:, 2, :], m[:, 1, :], ACT.Sqrt).then_inc(root_ready, 1)

                variance(0)
                for t in range(NT):
                    act.wait_ge(y_turned, 2 * t + 2)
                    act.activation(yT[:, t % 2, 4:8, :].rearrange("p k c -> p (k c)"), ps[:, 3, :], ACT.Copy).then_inc(yt_high, 1)
                    if t + 1 < NT:
                        variance(t + 1)

            @block.vector
            def _(dve):
                do = Chain(dve, chain_s)

                def normed(t):
                    Y, V = y[:, t % 2, :], v[:, t % 2, :]
                    dve.wait_ge(y_in[t % 2], 32 * (t // 2 + 1))
                    do(dve.tensor_reduce(m[:, 0, :], heads(Y), AX, ALU.add))
                    do(dve.tensor_scalar(m[:, 0, :], m[:, 0, :], 1.0 / 64, None, ALU.mult))
                    do(dve.tensor_tensor(heads(Y), heads(Y), per(m[:, 0, :]), ALU.subtract))
                    dve.sem_inc(centred, 1)
                    do(dve.tensor_tensor(heads(V), heads(V), per(bonus[:, t, :]), ALU.mult))
                    dve.wait_ge(squares, t + 1)
                    do(dve.tensor_reduce(m[:, 1, :], heads(sq[:, :]), AX, ALU.add))
                    do(dve.tensor_scalar(m[:, 1, :], m[:, 1, :], 1.0 / 64, 64e-5, ALU.mult, ALU.add))
                    dve.sem_inc(var_ready, 1)
                    dve.wait_ge(root_ready, t + 1)
                    do(dve.reciprocal(m[:, 3, :], m[:, 2, :]))
                    do(dve.tensor_tensor(heads(Y), heads(Y), per(m[:, 3, :]), ALU.mult))
                    do(dve.tensor_tensor(Y, Y, spread[:, 0, :], ALU.mult))
                    do(dve.tensor_tensor(Y, Y, spread[:, 1, :], ALU.add))
                    do(dve.tensor_tensor(Y, Y, V, ALU.add))

                dve.wait_ge(small_in, 80)
                normed(0)
                for t in range(NT):
                    Y, V = y[:, t % 2, :], v[:, t % 2, :]
                    dve.wait_ge(gate_sum, t + 1)
                    dve.tensor_tensor(Y.rearrange("p (h n) -> p h n", h=2), Y.rearrange("p (h n) -> p h n", h=2), ps[:, 0:2, :], ALU.mult).then_inc(y_ready, 1)
                    dve.wait_ge(y_turned, 2 * t + 1)
                    dve.tensor_copy(yT[:, t % 2, 0:4, :].rearrange("p k c -> p (k c)"), ps[:, 2, :]).then_inc(yt_low, 1)
                    if t + 1 < NT:
                        normed(t + 1)
                    if t == 0:
                        dve.wait_ge(x_in_again, 16)
                    for half in range(2):
                        cols = slice(half * HALF, (half + 1) * HALF)
                        dve.wait_ge(out_sum, 2 * t + half + 1)
                        do(dve.tensor_tensor(V[:, cols], ps[:, 4 + 2 * (t % 2) + half, :], spread[:, 2, cols], ALU.mult))
                        dve.tensor_tensor(core.x[:, t, cols], core.x[:, t, cols], V[:, cols], ALU.add).then_inc(x_added, 1)


HD = 64
A_HEADS, B_HEADS, C_HEADS = 8, 8, 16
AB_IN = 3328
C_Q, C_KV, ROPE = 256, 128, 32
QK = HD + ROPE
C_FIRST = C_Q + C_KV + ROPE
BUCKETS, MAX_DISTANCE = 32, 2048
SPAN = T + P


def attention_constants():
    dist = (T - 1) - np.arange(SPAN)
    d = np.maximum(dist, 0)
    exact = BUCKETS // 2
    large = exact + (np.log(np.maximum(d, 1).astype(np.float32) / np.float32(exact)) / np.float32(np.log(MAX_DISTANCE / exact))
                     * np.float32(BUCKETS - exact)).astype(np.int32)
    bucket = np.where(d < exact, d, np.minimum(large, BUCKETS - 1))
    one_hot = (np.arange(BUCKETS)[:, None] == bucket[None, :])
    near = np.where((dist >= 0) & (dist <= 128), 0.0, NEG)
    count = (dist <= 128).astype(int) + (dist % 4 == 0) + (dist % 16 == 0)
    times = np.where((dist >= 0) & (count > 0), np.log(np.maximum(count, 1)), NEG)
    buckets = np.stack([np.concatenate([one_hot, near[None]]), np.concatenate([one_hot, times[None]])], 1)
    i = np.arange(P)[:, None]
    flip = (i + np.arange(P)[None, :] == P - 1)
    causal = np.where(np.arange(T)[None, :] - (T - P) <= i, 0.0, NEG)
    freq = np.tile((10000.0 ** (-np.arange(0, ROPE, 2, dtype=np.float32) / ROPE)).astype(np.float32), (P, 1))
    return (np.ascontiguousarray(buckets.reshape(BUCKETS + 1, -1), np.float32),
            np.ascontiguousarray(np.concatenate([flip, causal, freq], 1), np.float32))


BUCKET_CONST, ATT_CONST = attention_constants()


def norm_in_place(core, gain, dst=None):
    nc = core.nc
    with ExitStack() as held:
        tag = "last" if dst is not None else "mid"
        sb = lambda name, shape, dt=F32: held.enter_context(nc.sbuf_tensor(f"{name}_{tag}", shape, dt))
        g = sb("gain_spread", [P, D])
        junk = sb("squares", [P, D])
        ss = sb("sum_squares", [P, NT])
        s = held.enter_context(signals(nc, "gain_in squared rooted root_ready x_ready stored dve_chain act_chain"))
        gain_in, squared, rooted, root_ready, x_ready, stored, chain_s, act_s = s
        with nc.Block() as block:
            @block.sync
            def _(sp):
                sp.dma_start(g[:, :], rows(*gain, D)).then_inc(gain_in, 16)
                if dst is not None:
                    for t in range(NT):
                        sp.wait_ge(x_ready, t + 1)
                        sp.dma_start(dst[t * P:(t + 1) * P, :], core.x[:, t, :]).then_inc(stored, 16)
                    sp.wait_ge(stored, 16 * NT)

            @block.scalar
            def _(act):
                do = Chain(act, act_s)
                for t in range(NT):
                    do(act.activation(junk[:, :], core.x[:, t, :], ACT.Square, accum_out=ss[:, t:t + 1]))
                act.sem_inc(squared, 1)
                act.wait_ge(rooted, 1)
                act.activation(ss[:, :], ss[:, :], ACT.Sqrt).then_inc(root_ready, 1)

            @block.vector
            def _(dve):
                do = Chain(dve, chain_s)
                dve.wait_ge(squared, 1)
                dve.tensor_scalar(ss[:, :], ss[:, :], 1.0 / D, 1e-6, ALU.mult, ALU.add).then_inc(rooted, 1)
                dve.wait_ge(root_ready, 1)
                do(dve.reciprocal(ss[:, :], ss[:, :]))
                dve.wait_ge(gain_in, 16)
                for t in range(NT):
                    x = core.x[:, t, :]
                    dve.scalar_tensor_tensor(x, x, ss[:, t:t + 1], g[:, :], ALU.mult, ALU.mult).then_inc(x_ready, 1)


def attention(core, tag, units, w, w_out, w_in):
    nc, ps = core.nc, core.ps
    n = len(units)
    with ExitStack() as held:
        sb = lambda name, shape, dt=F32: held.enter_context(nc.sbuf_tensor(f"{name}_{tag}", shape, dt))
        s = sb("scores", [P, 3, HALF])
        pT = sb("probs_turned", [P, 2, HALF])
        stat = sb("row_stats", [P, n, 4])
        MAXI, DEN, SINK, INV = range(4)
        sems = held.enter_context(signals(nc, "scores_sum scored max_ready probs_ready probs_turned pt_ready pv_sum o_ready dve_chain"))
        scores_sum, scored, max_ready, probs_ready, probs_turned, pt_ready, pv_sum, o_ready, chain_s = sems
        width = lambda i: units[i][1].shape[1]
        with nc.Block() as block:
            @block.sync
            def _(sp):
                sp.dma_start(w[:, :, :], w_out.rearrange("(k p) n -> p k n", p=P)).then_inc(w_in, 16)

            @block.tensor
            def _(pe):
                for i in range(n + 3):
                    if i < n:
                        q, k = units[i][0], units[i][1]
                        if i >= 2:
                            pe.wait_ge(scored, i - 1)
                        pe.matmul(ps[:, i % 2, 0:width(i)], q, k, start=True, stop=True).then_inc(scores_sum, 1)
                    j = i - 2
                    if 0 <= j < n:
                        pe.wait_ge(probs_ready, j + 1)
                        if j >= 2:
                            pe.wait_ge(pt_ready, j - 1)
                        for b in range(width(j) // P):
                            last = pe.transpose(ps[:, 2 + j % 2, b * P:(b + 1) * P], s[:, j % 3, b * P:(b + 1) * P], core.c("ident"))
                        last.then_inc(probs_turned, 1)
                    j = i - 3
                    if 0 <= j < n:
                        values = units[j][4]
                        pe.wait_ge(pt_ready, j + 1)
                        if j >= 2:
                            pe.wait_ge(o_ready, j - 1)
                        for b, v in enumerate(values):
                            last = pe.matmul(ps[:, 4 + j % 2, 0:HD], pT[:, j % 2, b * P:(b + 1) * P], v, start=b == 0, stop=b == len(values) - 1)
                        last.then_inc(pv_sum, 1)

            @block.vector
            def _(dve):
                do = Chain(dve, chain_s)
                for i in range(n + 4):
                    if i < n:
                        _, _, bias, scale, _, sink, _ = units[i]
                        x = s[:, i % 3, 0:width(i)]
                        m = stat[:, i, MAXI:MAXI + 1]
                        dve.wait_ge(scores_sum, i + 1)
                        if i >= 3:
                            dve.wait_ge(probs_turned, i - 2)
                        dve.scalar_tensor_tensor(x, ps[:, i % 2, 0:width(i)], scale, bias, ALU.mult, ALU.add).then_inc(scored, 1)
                        dve.wait_ge(scored, i + 1)
                        do(dve.tensor_reduce(m, x, AX, ALU.max))
                        if sink is None:
                            dve.tensor_scalar(m, m, -1.0, None, ALU.mult).then_inc(max_ready, 1)
                        else:
                            dve.tensor_scalar(m, m, sink, -1.0, ALU.max, ALU.mult).then_inc(max_ready, 1)
                    j = i - 4
                    if 0 <= j < n:
                        den, inv = stat[:, j, DEN:DEN + 1], stat[:, j, INV:INV + 1]
                        dve.wait_ge(pv_sum, j + 1)
                        if units[j][5] is not None:
                            do(dve.tensor_tensor(den, den, stat[:, j, SINK:SINK + 1], ALU.add))
                        do(dve.reciprocal(inv, den))
                        dve.tensor_scalar(units[j][6], ps[:, 4 + j % 2, 0:HD], inv, None, ALU.mult).then_inc(o_ready, 1)

            @block.scalar
            def _(act):
                for i in range(n + 2):
                    j = i - 2
                    if 0 <= j < n:
                        act.wait_ge(probs_turned, j + 1)
                        if j >= 2:
                            act.wait_ge(pv_sum, j - 1)
                        act.activation(pT[:, j % 2, 0:width(j)], ps[:, 2 + j % 2, 0:width(j)], ACT.Copy).then_inc(pt_ready, 1)
                    if i < n:
                        x, sink = s[:, i % 3, 0:width(i)], units[i][5]
                        act.wait_ge(max_ready, i + 1)
                        if sink is not None:
                            act.activation(stat[:, i, SINK:SINK + 1], sink, ACT.Exp, bias=stat[:, i, MAXI:MAXI + 1])
                        act.activation(x, x, ACT.Exp, bias=stat[:, i, MAXI:MAXI + 1], accum_out=stat[:, i, DEN:DEN + 1]).then_inc(probs_ready, 1)


def gated_out(core, tag, o, z, w, w_in):
    nc, ps = core.nc, core.ps
    with ExitStack() as held:
        sb = lambda name, shape, dt=F32: held.enter_context(nc.sbuf_tensor(f"{name}_{tag}", shape, dt))
        oT = sb("o_turned", [P, 2, KD, P])
        s = held.enter_context(signals(nc, "gated turned low high out_sum added"))
        gated, turned, low, high, out_sum, added = s
        with nc.Block() as block:
            @block.tensor
            def _(pe):
                def turn(t):
                    pe.wait_ge(gated, t + 1)
                    for half in range(2):
                        for k in range(4):
                            c0 = (half * 4 + k) * P
                            last = pe.transpose(ps[:, half, k * P:(k + 1) * P], o[:, t, c0:c0 + P], core.c("ident"))
                        last.then_inc(turned, 1)

                turn(0)
                for t in range(NT):
                    pe.wait_ge(low, t + 1)
                    pe.wait_ge(high, t + 1)
                    if t + 1 < NT:
                        turn(t + 1)
                    if t == 0:
                        pe.wait_ge(w_in, 16)
                    if t >= 2:
                        pe.wait_ge(added, 2 * (t - 1))
                    for half in range(2):
                        for k in range(KD):
                            last = pe.matmul(ps[:, 4 + 2 * (t % 2) + half, :], oT[:, t % 2, k, :], w[:, k, half * HALF:(half + 1) * HALF], start=k == 0, stop=k == KD - 1)
                        last.then_inc(out_sum, 1)

            @block.scalar
            def _(act):
                for t in range(NT):
                    if t >= 2:
                        act.wait_ge(out_sum, 2 * (t - 1))
                    act.wait_ge(turned, 2 * t + 2)
                    act.activation(oT[:, t % 2, 4:8, :].rearrange("p k c -> p (k c)"), ps[:, 1, :], ACT.Copy).then_inc(high, 1)

            @block.vector
            def _(dve):
                def move(t):
                    dve.wait_ge(turned, 2 * t + 1)
                    dve.tensor_copy(oT[:, t % 2, 0:4, :].rearrange("p k c -> p (k c)"), ps[:, 0, :]).then_inc(low, 1)

                def gate(t):
                    dve.tensor_tensor(o[:, t, :], o[:, t, :], z[:, t, :], ALU.mult).then_inc(gated, 1)

                gate(0)
                gate(1)
                move(0)
                for t in range(NT):
                    if t + 2 < NT:
                        gate(t + 2)
                    if t + 1 < NT:
                        if t:
                            dve.wait_ge(out_sum, 2 * t)
                        move(t + 1)
                    for half in range(2):
                        x = core.x[:, t, half * HALF:(half + 1) * HALF]
                        dve.wait_ge(out_sum, 2 * t + half + 1)
                        dve.tensor_tensor(x, x, ps[:, 4 + 2 * (t % 2) + half, :], ALU.add).then_inc(added, 1)


def window_layer(core):
    nc, ins, ps = core.nc, core.ins, core.ps
    with ExitStack() as held:
        sb = lambda name, shape, dt=F32: held.enter_context(nc.sbuf_tensor(name, shape, dt))
        e_dram = nc.dram_tensor("bias_by_distance", [2, A_HEADS, SPAN], F32, kind="Internal").ap()
        NQ, NK = 8, 6
        qT, kT = sb("q_channels_ab", [P, NQ, T]), sb("k_channels_ab", [P, NK, T])
        v, z = sb("v_tokens_ab", [P, NT, P + B_HEADS * HD]), sb("z_tokens_ab", [P, NT, D])
        bias = sb("bias_tables", [P, 2, A_HEADS, T])
        sinks = sb("sinks", [P, A_HEADS])
        with nc.sbuf_tensor("h_turned_ab", [P, KD, T], F32) as hT:
            norm_turn(core, list(range(NT)), [(ins["norm_w_2"], 0)] * NT, [None] * NT, 1e-6, hT)
            window_inputs(core, hT, qT, kT, v, z, bias, sinks, e_dram)
        o = sb("o_tokens_ab", [P, NT, D])
        units = []
        for h in range(A_HEADS + B_HEADS):
            for t in range(NT):
                row = slice(64 * (h % 2), 64 * (h % 2) + 64)
                a = h < A_HEADS
                first = max(t - 1, 0) if a else 0
                kb = h // 4 if a else 2 + (h - A_HEADS) // 2
                hh = h if a else h - A_HEADS
                vc = (h // 4) * HD if a else P + hh * HD
                u0 = (NT - 1 - t + first) * P
                units.append((qT[row, h // 2, t * P:(t + 1) * P], kT[row, kb, first * P:(t + 1) * P],
                              bias[:, 0 if a else 1, hh, u0:T], float(HD) ** -0.5, [v[:, j, vc:vc + HD] for j in range(first, t + 1)],
                              sinks[:, h:h + 1] if a else None, o[:, t, h * HD:(h + 1) * HD]))
        w_out = sb("w_out_ab", [P, KD, D])
        (w_in,) = held.enter_context(signals(nc, "w_in"))
        attention(core, "ab", units, w_out, ins["ab_w_out_2"][0], w_in)
        gated_out(core, "ab", o, z, w_out, w_in)


def window_inputs(core, hT, qT, kT, v, z, bias, sinks, e_dram):
    nc, ins, ps = core.nc, core.ins, core.ps
    with ExitStack() as held:
        sb = lambda name, shape, dt=F32: held.enter_context(nc.sbuf_tensor(name, shape, dt))
        RING = 2
        ring = sb("ab_weights", [P, RING, KD, HALF])
        rel = sb("rel_bias_rows", [BUCKETS + 1, 2 * A_HEADS])
        hot = sb("bucket_rows", [BUCKETS + 1, 2, SPAN])
        con = sb("flip_const", [P, P])
        by_dist = sb("by_distance", [A_HEADS, 2, SPAN])
        slid = sb("slid_rows", [P, 2, T])
        s = held.enter_context(signals(nc, "rel_in hot_in one_set w_in0 w_in1 product moved e_sum e_moved e_out slid_in0 slid_in1 table_sum table_ready"))
        rel_in, hot_in, one_set, w_in0, w_in1, product, moved, e_sum, e_moved, e_out, slid_in0, slid_in1, table_sum, table_ready = s
        w_in, slid_in = [w_in0, w_in1], [slid_in0, slid_in1]
        w = ins["ab_w_in_2"][0].rearrange("(k p) n -> p k n", p=P)
        LOADS = [[(0, 512, 0)], [(512, 64, 0), (512, 64, 64), (576, 64, 128), (576, 64, 192), (640, 128, 256)],
                 [(768, 512, 0)], [(1280, 512, 0)], [(1792, 512, 0)], [(2304, 512, 0)], [(2816, 512, 0)]]
        SUMS = [(0, "ch", m * P, P, qT[:, m, :]) for m in range(4)]
        SUMS += [(1, "ch", m * P, P, kT[:, m, :]) for m in range(2)]
        SUMS += [(1, t, 256, P, v[:, t, 0:P]) for t in range(NT)]
        SUMS += [(2, "ch", m * P, P, qT[:, 4 + m, :]) for m in range(4)]
        SUMS += [(3, "ch", m * P, P, kT[:, 2 + m, :]) for m in range(4)]
        SUMS += [(4, t, 0, HALF, v[:, t, P:P + HALF]) for t in range(NT)]
        SUMS += [(5 + n, t, 0, HALF, z[:, t, n * HALF:(n + 1) * HALF]) for n in range(2) for t in range(NT)]
        last_of = lambda n: max(i for i, x in enumerate(SUMS) if x[0] == n) + 1
        arrived = lambda n: 16 * sum(len(LOADS[q]) for q in range(n % RING, n + 1, RING))
        with nc.Block() as block:
            @block.gpsimd
            def _(pool):
                pool.memset(rel[BUCKETS:BUCKETS + 1, :], 1.0).then_inc(one_set, 1)

            @block.sync
            def _(sp):
                sp.dma_start(rel[0:BUCKETS, :], ins["rel_bias_2"]).then_inc(rel_in, 16)
                sp.dma_start(hot[:, :, :].rearrange("b a n -> b (a n)"), ins["bucket_const"]).then_inc(rel_in, 16)
                sp.dma_start(con[:, :], ins["att_const"][:, 0:P]).then_inc(rel_in, 16)
                sp.dma_start(sinks[:, :], rows(ins["ab_sinks_2"], 0, A_HEADS)).then_inc(rel_in, 16)
                for n, parts in enumerate(LOADS):
                    if n >= RING:
                        sp.wait_ge(product, last_of(n - RING))
                    for c0, cols, at in parts:
                        sp.dma_start(ring[:, n % RING, :, at:at + cols], w[:, :, c0:c0 + cols]).then_inc(w_in[n % RING], 16)
                    if n == 1:
                        sp.wait_ge(e_moved, 4)
                        sp.dma_start(e_dram.rearrange("a h n -> h a n"), by_dist[:, :, :]).then_inc(e_out, 16)
                        sp.wait_ge(e_out, 16)
                for g in range(2 * A_HEADS):
                    if g >= 2:
                        sp.wait_ge(table_sum, g - 1)
                    sp.dma_start(slid[:, g % 2, :], bass.AP(tensor=e_dram.tensor, offset=g * SPAN, ap=[[1, P], [1, T]])).then_inc(slid_in[g % 2], 16)

            @block.tensor
            def _(pe):
                pe.wait_ge(rel_in, 64)
                pe.wait_ge(one_set, 1)
                for a in range(2):
                    for half in range(2):
                        n = SPAN // 2
                        pe.matmul(ps[0:A_HEADS, 2 * a + half, 0:n], rel[:, a * A_HEADS:(a + 1) * A_HEADS], hot[:, a, half * n:(half + 1) * n],
                                  start=True, stop=True).then_inc(e_sum, 1)
                pe.wait_ge(e_moved, 4)
                for i, (n, kind, at, cols, dst) in enumerate(SUMS):
                    pe.wait_ge(w_in[n % RING], arrived(n))
                    if i >= 8:
                        pe.wait_ge(moved, i - 7)
                    for k in range(KD):
                        if kind == "ch":
                            last = pe.matmul(ps[:, i % 8, :], ring[:, n % RING, k, at:at + cols], hT[:, k, :], start=k == 0, stop=k == KD - 1)
                        else:
                            last = pe.matmul(ps[:, i % 8, 0:cols], hT[:, k, kind * P:(kind + 1) * P], ring[:, n % RING, k, at:at + cols], start=k == 0, stop=k == KD - 1)
                    last.then_inc(product, 1)
                pe.wait_ge(moved, len(SUMS))
                for g in range(2 * A_HEADS):
                    pe.wait_ge(slid_in[g % 2], 16 * (g // 2 + 1))
                    if g >= 8:
                        pe.wait_ge(table_ready, g - 7)
                    pe.matmul(ps[:, g % 8, :], con[:, :], slid[:, g % 2, :], start=True, stop=True).then_inc(table_sum, 1)

            @block.scalar
            def _(act):
                for i, (n, kind, at, cols, dst) in enumerate(SUMS):
                    act.wait_ge(product, i + 1)
                    src = ps[:, i % 8, :] if kind == "ch" else ps[:, i % 8, 0:cols]
                    act.activation(dst, src, ACT.Silu if n >= 5 else ACT.Copy).then_inc(moved, 1)

            @block.vector
            def _(dve):
                for j in range(4):
                    n = SPAN // 2
                    dve.wait_ge(e_sum, j + 1)
                    dve.tensor_copy(by_dist[:, j // 2, (j % 2) * n:(j % 2 + 1) * n], ps[0:A_HEADS, j, 0:n]).then_inc(e_moved, 1)
                for g in range(2 * A_HEADS):
                    dve.wait_ge(table_sum, g + 1)
                    dve.tensor_copy(bias[:, g // A_HEADS, g % A_HEADS, :], ps[:, g % 8, :]).then_inc(table_ready, 1)


def latent_layer(core):
    nc, ins, ps = core.nc, core.ins, core.ps
    with ExitStack() as held:
        sb = lambda name, shape, dt=F32: held.enter_context(nc.sbuf_tensor(name, shape, dt))
        qT, kT = sb("q_channels_c", [QK, C_HEADS, T]), sb("k_channels_c", [QK, C_HEADS, T])
        v, z = sb("v_tokens_c", [P, NT, D]), sb("z_tokens_c", [P, NT, D])
        con = sb("att_masks", [P, ATT_CONST.shape[1]])
        with nc.sbuf_tensor("h_turned_c", [P, KD, T], F32) as hT:
            norm_turn(core, list(range(NT)), [(ins["norm_w_2"], D)] * NT, [None] * NT, 1e-6, hT)
            latent_inputs(core, hT, qT, kT, v, z, con)
        o = sb("o_tokens_c", [P, NT, D])
        units = []
        for h in range(C_HEADS):
            for t in range(NT):
                u0 = (NT - 1 - t) * P
                units.append((qT[:, h, t * P:(t + 1) * P], kT[:, h, 0:(t + 1) * P], con[:, P + u0:P + T], float(QK) ** -0.5,
                              [v[:, j, h * HD:(h + 1) * HD] for j in range(t + 1)], None, o[:, t, h * HD:(h + 1) * HD]))
        w_out = sb("w_out_c", [P, KD, D])
        (w_in,) = held.enter_context(signals(nc, "w_in"))
        attention(core, "c", units, w_out, ins["c_w_out_2"][0], w_in)
        gated_out(core, "c", o, z, w_out, w_in)


def latent_inputs(core, hT, qT, kT, v, z, con):
    nc, ins, ps = core.nc, core.ins, core.ps
    HF = ROPE // 2
    with ExitStack() as held:
        sb = lambda name, shape, dt=F32: held.enter_context(nc.sbuf_tensor(name, shape, dt))
        wc = sb("c_w_first", [P, KD, C_FIRST])
        wz = wc
        wq = sb("c_w_q", [P, 2, C_HEADS * QK])
        wkv = sb("c_w_kv", [P, C_HEADS * 2 * HD])
        gains = sb("c_gains", [P, C_Q + C_KV])
        pos_i, pos = sb("pos_int", [P, NT], I32), sb("pos_float", [P, NT])
        ang, turns_i, turns = sb("angle", [P, NT, 2, HF]), sb("turns_int", [P, NT, 2, HF], I32), sb("turns", [P, NT, 2, HF])
        cs = sb("sin_cos", [P, NT, 2, HF])
        first = sb("c_first", [P, NT, C_FIRST])
        junk = sb("c_squares", [P, C_Q])
        ss = sb("c_sum_squares", [P, NT, 2])
        cT = sb("c_turned", [P, 3, T])
        kpe = sb("k_pe", [P, NT, ROPE])
        tq, tk = sb("q_tokens", [P, C_HEADS, QK]), sb("k_tokens_c", [P, C_HEADS, QK])
        rot = sb("rotated", [P, 4, C_HEADS, HF])
        s = held.enter_context(signals(nc, "small_in pos_in wc_in wq_in first_sum first_done ang_ready trig_done squared rooted root_ready c_ready c_turned c_moved z_in z_sum z_done q_sum kv_sum kv_moved v_moved q_ready k_ready q_turned k_turned qT_done kT_done dve_chain act_chain", core.soft))
        (small_in, pos_in, wc_in, wq_in, first_sum, first_done, ang_ready, trig_done, squared, rooted, root_ready, c_ready, c_turned, c_moved,
         z_in, z_sum, z_done, q_sum, kv_sum, kv_moved, v_moved, q_ready, k_ready, q_turned, k_turned, qT_done, kT_done, chain_s, act_s) = s
        w = ins["c_w_in_2"][0].rearrange("(k p) n -> p k n", p=P)
        Z0 = C_FIRST
        ZP = [(0, 384), (384, 384), (768, 256)]
        with nc.Block() as block:
            @block.gpsimd
            def _(pool):
                with nc.allow_non_contiguous_dma(reason="512 positions, by token on partitions"):
                    pool.dma_start(pos_i[:, :], ins["positions_2"].rearrange("a (t p) -> p (a t)", p=P)).then_inc(pos_in, 16)

            @block.sync
            def _(sp):
                sp.dma_start(wc[:, :, :], w[:, :, 0:C_FIRST]).then_inc(wc_in, 16)
                sp.dma_start(con[:, :], ins["att_const"]).then_inc(small_in, 16)
                sp.dma_start(gains[:, 0:C_Q], rows(ins["c_q_norm_2"], 0, C_Q)).then_inc(small_in, 16)
                sp.dma_start(gains[:, C_Q:], rows(ins["c_kv_norm_2"], 0, C_KV)).then_inc(small_in, 16)
                sp.dma_start(wq[:, :, :], ins["c_w_qb_2"][0].rearrange("(k p) n -> p k n", p=P)).then_inc(wq_in, 16)
                sp.dma_start(wkv[:, :], ins["c_w_kvb_2"][0]).then_inc(wq_in, 16)
                for n, (c0, cols) in enumerate(ZP):
                    if n == 0:
                        sp.wait_ge(first_sum, NT)
                    else:
                        sp.wait_ge(z_sum, NT * n)
                    sp.dma_start(wz[:, :, 0:cols], w[:, :, Z0 + c0:Z0 + c0 + cols]).then_inc(z_in, 16)

            @block.tensor
            def _(pe):
                pe.wait_ge(wc_in, 16)
                for t in range(NT):
                    for k in range(KD):
                        last = pe.matmul(ps[:, t, 0:C_FIRST], hT[:, k, t * P:(t + 1) * P], wc[:, k, :], start=k == 0, stop=k == KD - 1)
                    last.then_inc(first_sum, 1)
                step = 0
                for n, (c0, cols) in enumerate(ZP):
                    pe.wait_ge(z_in, 16 * (n + 1))
                    for t in range(NT):
                        if step >= 4:
                            pe.wait_ge(z_done, step - 3)
                        for k in range(KD):
                            last = pe.matmul(ps[:, 4 + step % 4, 0:cols], hT[:, k, t * P:(t + 1) * P], wz[:, k, 0:cols], start=k == 0, stop=k == KD - 1)
                        last.then_inc(z_sum, 1)
                        step += 1
                pe.wait_ge(c_ready, 1)
                pe.wait_ge(first_done, NT)
                for j in range(3):
                    for t in range(NT):
                        last = pe.transpose(ps[:, j, t * P:(t + 1) * P], first[:, t, j * P:(j + 1) * P], core.c("ident"))
                last.then_inc(c_turned, 1)
                pe.wait_ge(c_moved, 1)
                pe.wait_ge(wq_in, 32)
                pe.wait_ge(z_done, step)
                for t in range(NT):
                    tok = slice(t * P, (t + 1) * P)
                    if t:
                        pe.wait_ge(q_ready, t)
                        pe.wait_ge(kT_done, 4 * t)
                        pe.wait_ge(qT_done, 4 * t)
                    for n in range(3):
                        for k in range(2):
                            last = pe.matmul(ps[:, n, :], cT[:, k, tok], wq[:, k, n * HALF:(n + 1) * HALF], start=k == 0, stop=k == 1)
                    last.then_inc(q_sum, 1)
                    for n in range(4):
                        last = pe.matmul(ps[:, 3 + n, :], cT[:, 2, tok], wkv[:, n * HALF:(n + 1) * HALF], start=True, stop=True)
                    last.then_inc(kv_sum, 1)
                    for src, ready, turned, done in ((tq, q_ready, q_turned, qT_done), (tk, k_ready, k_turned, kT_done)):
                        pe.wait_ge(ready, t + 1)
                        if src is tk:
                            pe.wait_ge(v_moved, t + 1)
                            pe.wait_ge(qT_done, 4 * t + 4)
                        for g in range(4):
                            bank = g if src is tq else 4 + g
                            if src is tq and g == 3:
                                pe.wait_ge(kv_moved, t + 1)
                                pe.wait_ge(v_moved, t + 1)
                            for h in range(4):
                                last = pe.transpose(ps[0:QK, bank, h * P:(h + 1) * P], src[:, 4 * g + h, :], core.c("ident"))
                            last.then_inc(turned, 1)

            @block.scalar
            def _(act):
                do = Chain(act, act_s)
                for t in range(NT):
                    act.wait_ge(first_sum, t + 1)
                    act.activation(first[:, t, :], ps[:, t, 0:C_FIRST], ACT.Copy).then_inc(first_done, 1)
                act.wait_ge(first_done, NT)
                for t in range(NT):
                    for j, (a, b) in enumerate(((0, C_Q), (C_Q, C_Q + C_KV))):
                        do(act.activation(junk[:, 0:b - a], first[:, t, a:b], ACT.Square, accum_out=ss[:, t, j:j + 1]))
                act.sem_inc(squared, 1)
                act.wait_ge(rooted, 1)
                act.activation(ss[:, :, :], ss[:, :, :], ACT.Sqrt).then_inc(root_ready, 1)
                act.wait_ge(ang_ready, 1)
                act.activation(cs[:, :, :, :], ang[:, :, :, :], ACT.Sin).then_inc(trig_done, 1)
                step = 0
                for n, (c0, cols) in enumerate(ZP):
                    for t in range(NT):
                        step += 1
                        act.wait_ge(z_sum, step)
                        act.activation(z[:, t, c0:c0 + cols], ps[:, 4 + (step - 1) % 4, 0:cols], ACT.Silu).then_inc(z_done, 1)
                for t in range(NT):
                    tok = slice(t * P, (t + 1) * P)
                    act.wait_ge(kv_sum, t + 1)
                    for n in range(4):
                        last = act.activation(v[:, t, n * 256:(n + 1) * 256].rearrange("p (h c) -> p h c", h=4),
                                              ps[:, 3 + n, :].rearrange("p (h a c) -> p h a c", h=4, a=2)[:, :, 1, :], ACT.Copy)
                    last.then_inc(v_moved, 1)
                    for g in range(4):
                        act.wait_ge(q_turned, 4 * t + g + 1)
                        act.activation(qT[:, 4 * g:4 * g + 4, tok], ps[0:QK, g, :].rearrange("p (h c) -> p h c", h=4), ACT.Copy).then_inc(qT_done, 1)

            @block.vector
            def _(dve):
                do = Chain(dve, chain_s)
                dve.wait_ge(pos_in, 16)
                dve.wait_ge(small_in, 48)
                do(dve.tensor_copy(pos[:, :], pos_i[:, :]))
                freq = con[:, P + T:P + T + HF]
                A0 = ang[:, :, 0, :]
                do(dve.tensor_tensor(A0, freq.unsqueeze(1).to_broadcast([P, NT, HF]), pos[:, :].unsqueeze(2).to_broadcast([P, NT, HF]), ALU.mult))
                C1, C2 = 6.28125, 1.9353071795e-3
                HALF_PI = float(np.pi / 2)
                do(dve.tensor_scalar(turns[:, :, 0, :], A0, float(1 / (2 * np.pi)), None, ALU.mult))
                do(dve.tensor_scalar(turns[:, :, 1, :], A0, float(1 / (2 * np.pi)), 0.25, ALU.mult, ALU.add))
                do(dve.tensor_scalar(turns[:, :, :, :], turns[:, :, :, :], 12582912.0, None, ALU.add))
                do(dve.tensor_scalar(turns[:, :, :, :], turns[:, :, :, :], -12582912.0, None, ALU.add))
                do(dve.tensor_copy(ang[:, :, 1, :], A0))
                do(dve.scalar_tensor_tensor(ang[:, :, :, :].rearrange("p t a f -> p (t a f)"), turns[:, :, :, :].rearrange("p t a f -> p (t a f)"), -C1,
                                            ang[:, :, :, :].rearrange("p t a f -> p (t a f)"), ALU.mult, ALU.add))
                do(dve.scalar_tensor_tensor(ang[:, :, :, :].rearrange("p t a f -> p (t a f)"), turns[:, :, :, :].rearrange("p t a f -> p (t a f)"), -C2,
                                            ang[:, :, :, :].rearrange("p t a f -> p (t a f)"), ALU.mult, ALU.add))
                do(dve.tensor_scalar(ang[:, :, 1, :], ang[:, :, 1, :], HALF_PI, None, ALU.add))
                do(dve.tensor_scalar(ang[:, :, :, :], ang[:, :, :, :], 3.1415925, -3.1415925, ALU.min, ALU.max))
                dve.sem_inc(ang_ready, 1)
                dve.wait_ge(squared, 1)
                do(dve.tensor_scalar(ss[:, :, 0], ss[:, :, 0], 1.0 / C_Q, 1e-6, ALU.mult, ALU.add))
                do(dve.tensor_scalar(ss[:, :, 1], ss[:, :, 1], 1.0 / C_KV, 1e-6, ALU.mult, ALU.add))
                dve.sem_inc(rooted, 1)
                dve.wait_ge(root_ready, 1)
                do(dve.reciprocal(ss[:, :, :], ss[:, :, :]))
                for t in range(NT):
                    for j, (a, b) in enumerate(((0, C_Q), (C_Q, C_Q + C_KV))):
                        f = first[:, t, a:b]
                        last = dve.scalar_tensor_tensor(f, f, ss[:, t, j:j + 1], gains[:, a:b], ALU.mult, ALU.mult)
                do(last)
                dve.sem_inc(c_ready, 1)
                dve.wait_ge(trig_done, 1)
                sin, cos = cs[:, :, 0, :], cs[:, :, 1, :]
                k1, k2 = first[:, :, C_Q + C_KV:C_Q + C_KV + HF], first[:, :, C_Q + C_KV + HF:C_FIRST]
                tmp = turns[:, :, 0, :]
                do(dve.tensor_tensor(kpe[:, :, 0:HF], k1, cos, ALU.mult))
                do(dve.tensor_tensor(tmp, k2, sin, ALU.mult))
                do(dve.tensor_tensor(kpe[:, :, 0:HF], kpe[:, :, 0:HF], tmp, ALU.subtract))
                do(dve.tensor_tensor(kpe[:, :, HF:], k1, sin, ALU.mult))
                do(dve.tensor_tensor(tmp, k2, cos, ALU.mult))
                do(dve.tensor_tensor(kpe[:, :, HF:], kpe[:, :, HF:], tmp, ALU.add))
                dve.wait_ge(c_turned, 1)
                do(dve.tensor_copy(cT[:, :, :], ps[:, 0:3, :]))
                dve.sem_inc(c_moved, 1)
                for t in range(NT):
                    tok = slice(t * P, (t + 1) * P)
                    per = lambda ap: ap.unsqueeze(1).to_broadcast([P, C_HEADS, HF])
                    dve.wait_ge(q_sum, t + 1)
                    if t:
                        dve.wait_ge(q_turned, 4 * t)
                        dve.wait_ge(k_turned, 4 * t)
                    do(dve.tensor_copy(tq[:, :, :].rearrange("p h c -> p (h c)").rearrange("p (n c) -> p n c", n=3), ps[:, 0:3, :]))
                    q1, q2 = tq[:, :, HD:HD + HF], tq[:, :, HD + HF:QK]
                    do(dve.tensor_tensor(rot[:, 0, :, :], q1, per(cos[:, t, :]), ALU.mult))
                    do(dve.tensor_tensor(rot[:, 1, :, :], q2, per(sin[:, t, :]), ALU.mult))
                    do(dve.tensor_tensor(rot[:, 2, :, :], q1, per(sin[:, t, :]), ALU.mult))
                    do(dve.tensor_tensor(rot[:, 3, :, :], q2, per(cos[:, t, :]), ALU.mult))
                    do(dve.tensor_tensor(q1, rot[:, 0, :, :], rot[:, 1, :, :], ALU.subtract))
                    do(dve.tensor_tensor(q2, rot[:, 2, :, :], rot[:, 3, :, :], ALU.add))
                    dve.sem_inc(q_ready, 1)
                    dve.wait_ge(v_moved, t + 1)
                    for n in range(4):
                        last = dve.tensor_copy(tk[:, 4 * n:4 * n + 4, 0:HD], ps[:, 3 + n, :].rearrange("p (h a c) -> p h a c", h=4, a=2)[:, :, 0, :])
                    do(last)
                    dve.sem_inc(kv_moved, 1)
                    do(dve.tensor_copy(tk[:, :, HD:QK], kpe[:, t, :].unsqueeze(1).to_broadcast([P, C_HEADS, ROPE])))
                    dve.sem_inc(k_ready, 1)
                    for g in range(4):
                        dve.wait_ge(k_turned, 4 * t + g + 1)
                        dve.tensor_copy(kT[:, 4 * g:4 * g + 4, tok], ps[0:QK, 4 + g, :].rearrange("p (h c) -> p h c", h=4)).then_inc(kT_done, 1)


def build(nc, ins, out):
    with ExitStack() as held:
        core = Core(nc, held, ins)
        load_start(core)
        modulation(core)
        with nc.sbuf_tensor("h_turned_gmlp", [P, KD, TA], F32) as hT:
            norm_turn(core, list(range(NTA)), [mod_row(core, 0, t >= NT, 1) for t in range(NTA)],
                      [mod_row(core, 0, t >= NT, 0) for t in range(NTA)], 1e-6, hT)
            gmlp(core, hT)
        moe(core, 0, NTA)
        rwkv(core, 1)
        moe(core, 1, NT)
        norm_in_place(core, (ins["final_g"], 0))
        window_layer(core)
        latent_layer(core)
        norm_in_place(core, (ins["final_norm_2"], 0), dst=out)


INPUTS = ("x c ctx c_ctx ada_w ada_b norm1_g norm2_g final_g ga_w_in ga_b_in ga_ln_g ga_ln_b ga_w_s ga_b_s ga_w_out ga_b_out "
          "rw_mu rw_wr rw_wk rw_wv rw_wo rw_w0 rw_w1 rw_w2 rw_a0 rw_a1 rw_a2 rw_g1 rw_g2 rw_k_k rw_k_a rw_r_k rw_ln_g rw_ln_b "
          "moe_w_grp moe_b_grp moe_w_exp moe_b_exp moe_w_gate moe_w_up moe_w_down positions_2 norm_w_2 rel_bias_2 ab_w_in_2 "
          "ab_sinks_2 ab_w_out_2 c_w_in_2 c_q_norm_2 c_w_qb_2 c_kv_norm_2 c_w_kvb_2 c_w_out_2 final_norm_2").split()


def kernel(**inputs):
    import numpy as _np
    import concourse.bacc as _bacc
    from concourse import mybir as _mybir
    from concourse.bass_utils import run_bass_kernel_spmd as _run

    nc = _bacc.Bacc("TRN2", target_bir_lowering=False, num_devices=1)
    given = {name: _np.ascontiguousarray(inputs[name]) for name in INPUTS}
    given["const"], given["scan_const"] = CONST, SCAN_CONST
    given["bucket_const"], given["att_const"] = BUCKET_CONST, ATT_CONST
    for layer, tiles in ((0, NTA), (1, NT)):
        given[f"cells{layer}"], given[f"entries{layer}"] = tables(tiles)
    arrays, ins = {}, {}
    for name, a in given.items():
        arrays[f"in_{name}_dram"] = a
        ins[name] = nc.dram_tensor(f"in_{name}_dram", a.shape, _mybir.dt.from_np(a.dtype), kind="ExternalInput").ap()
    out = nc.dram_tensor("out_0_dram", (T, D), _mybir.dt.float32, kind="ExternalOutput").ap()
    build(nc, ins, out)
    r = _run(nc, [arrays], core_ids=[0])
    return r.results[0]["out_0_dram"].reshape(1, T, D)
```
